# Optimizing a Trainium2 kernel written in Bass

```python
import math
import jax, jax.numpy as jnp
from jax import lax
import numpy as np

D_MODEL = 1024
BATCH = 1
SEQ = 256
DEPTH = 2

HEAD_DIM = 64
ROPE_THETA = 10000.0
NORM_EPS = 1e-6
N_MIXERS = 2
N_MOD = 6
A_Q_HEADS = D_MODEL // HEAD_DIM
A_KV_HEADS = A_Q_HEADS // 4
A_RADIUS = 128
B_GROUPS = ((128, 1), (512, 4), (2048, 16))
B_HEADS = D_MODEL // (2 * HEAD_DIM)
N_EXPERTS = 16
N_EXPERT_GROUPS = 4
TOP_K = 2
D_EXPERT = D_MODEL // 2
N_A_LAYERS = (DEPTH + 1) // 2
N_B_LAYERS = DEPTH // 2

kernel_name = 'hybrid_window_dilated_moe_encoder'

def rms_norm(x, g):
    xf = x.astype(jnp.float32)
    y = xf * lax.rsqrt(jnp.mean(xf * xf, axis=-1, keepdims=True) + NORM_EPS)
    return (y * g.astype(jnp.float32)).astype(x.dtype)

def rope_tables(positions):
    inv_freq = ROPE_THETA ** (-jnp.arange(0, HEAD_DIM, 2, dtype=jnp.float32) / HEAD_DIM)
    ang = positions.astype(jnp.float32)[..., None] * inv_freq
    return jnp.cos(ang)[:, :, None, :], jnp.sin(ang)[:, :, None, :]

def apply_rope(x, cos, sin):
    x1, x2 = jnp.split(x.astype(jnp.float32), 2, axis=-1)
    return jnp.concatenate([x1 * cos - x2 * sin, x2 * cos + x1 * sin], axis=-1).astype(x.dtype)

def banded_attention(q, k, v, radius, sink=None):
    bt, L, hq, dh = q.shape
    hkv = k.shape[2]
    g = hq // hkv
    nb = -(-L // radius)
    lp = nb * radius
    pad = lp - L
    qb = jnp.pad(q, ((0, 0), (0, pad), (0, 0), (0, 0))).reshape(bt, nb, radius, hkv, g, dh)
    kp = jnp.pad(k, ((0, 0), (radius, radius + pad), (0, 0), (0, 0))).reshape(bt, nb + 2, radius, hkv, dh)
    vp = jnp.pad(v, ((0, 0), (radius, radius + pad), (0, 0), (0, 0))).reshape(bt, nb + 2, radius, hkv, dh)
    kb = jnp.concatenate([kp[:, :nb], kp[:, 1:nb + 1], kp[:, 2:nb + 2]], axis=2)
    vb = jnp.concatenate([vp[:, :nb], vp[:, 1:nb + 1], vp[:, 2:nb + 2]], axis=2)
    s = jnp.einsum('bnqhgd,bnkhd->bnhgqk', qb, kb, preferred_element_type=jnp.float32) * (dh ** -0.5)
    qpos = jnp.arange(lp).reshape(nb, radius, 1)
    kpos = (jnp.arange(nb)[:, None, None] - 1) * radius + jnp.arange(3 * radius)[None, None, :]
    valid = (jnp.abs(kpos - qpos) <= radius) & (kpos >= 0) & (kpos < L)
    s = jnp.where(valid[None, :, None, None], s, -jnp.inf)
    m = jnp.max(s, axis=-1, keepdims=True)
    if sink is not None:
        sink_b = sink.astype(jnp.float32).reshape(1, 1, hkv, g, 1, 1)
        m = jnp.maximum(m, sink_b)
    p = jnp.exp(s - m)
    denom = jnp.sum(p, axis=-1, keepdims=True)
    if sink is not None:
        denom = denom + jnp.exp(sink_b - m)
    o = jnp.einsum('bnhgqk,bnkhd->bnqhgd', p.astype(v.dtype), vb, preferred_element_type=jnp.float32)
    o = o / jnp.transpose(denom[..., 0], (0, 1, 4, 2, 3))[..., None]
    lse = jnp.transpose((m + jnp.log(denom))[..., 0], (0, 1, 4, 2, 3)).reshape(bt, lp, hq)[:, :L]
    return o.reshape(bt, lp, hq, dh)[:, :L].astype(q.dtype), lse

def mixer_a(h, cos, sin, w_qkv, w_o, sink):
    b, s, _ = h.shape
    qkv = h @ w_qkv
    q, k, v = jnp.split(qkv, [A_Q_HEADS * HEAD_DIM, (A_Q_HEADS + A_KV_HEADS) * HEAD_DIM], axis=-1)
    q = apply_rope(q.reshape(b, s, A_Q_HEADS, HEAD_DIM), cos, sin)
    k = apply_rope(k.reshape(b, s, A_KV_HEADS, HEAD_DIM), cos, sin)
    v = v.reshape(b, s, A_KV_HEADS, HEAD_DIM)
    o, _ = banded_attention(q, k, v, A_RADIUS, sink)
    return o.reshape(b, s, A_Q_HEADS * HEAD_DIM) @ w_o

def dilated_group_attention(q, k, v, dilation, radius):
    b, s, hh, dh = q.shape
    L = s // dilation

    def to_strided(t):
        return t.reshape(b, L, dilation, hh, dh).transpose(0, 2, 1, 3, 4).reshape(b * dilation, L, hh, dh)

    o, lse = banded_attention(to_strided(q), to_strided(k), to_strided(v), radius)
    o = o.reshape(b, dilation, L, hh, dh).transpose(0, 2, 1, 3, 4).reshape(b, s, hh, dh)
    lse = lse.reshape(b, dilation, L, hh).transpose(0, 2, 1, 3).reshape(b, s, hh)
    return o, lse

def mixer_b(h, cos, sin, w_qkv, w_o):
    b, s, _ = h.shape
    qkv = (h @ w_qkv).reshape(b, s, len(B_GROUPS), 3, B_HEADS, HEAD_DIM)
    outs, lses = [], []
    for gi, (window, dilation) in enumerate(B_GROUPS):
        q = apply_rope(qkv[:, :, gi, 0], cos, sin)
        k = apply_rope(qkv[:, :, gi, 1], cos, sin)
        o, lse = dilated_group_attention(q, k, qkv[:, :, gi, 2], dilation, window // (2 * dilation))
        outs.append(o)
        lses.append(lse)
    w = jax.nn.softmax(jnp.stack(lses, axis=0), axis=0)
    o = jnp.einsum('gbsh,gbshd->bshd', w, jnp.stack(outs, axis=0).astype(jnp.float32)).astype(h.dtype)
    return o.reshape(b, s, B_HEADS * HEAD_DIM) @ w_o

def route(h_flat, router_w, router_bias):
    scores = jax.nn.sigmoid(h_flat.astype(jnp.float32) @ router_w.astype(jnp.float32))
    biased = scores + router_bias.astype(jnp.float32)
    per_group = N_EXPERTS // N_EXPERT_GROUPS
    group_score = jnp.sum(lax.top_k(biased.reshape(-1, N_EXPERT_GROUPS, per_group), 2)[0], axis=-1)
    gsel = jnp.argmax(group_score, axis=-1)
    in_group = (jnp.arange(N_EXPERTS) // per_group)[None, :] == gsel[:, None]
    _, idx = lax.top_k(jnp.where(in_group, biased, -jnp.inf), TOP_K)
    w = jnp.take_along_axis(scores, idx, axis=-1)
    w = w / jnp.sum(w, axis=-1, keepdims=True)
    return jnp.sum(jax.nn.one_hot(idx, N_EXPERTS, dtype=jnp.float32) * w[..., None], axis=1)

def moe_ffn(h, combine, w_gate, w_up, w_down):
    b, s, d = h.shape
    t = h.reshape(b * s, d)
    y = jnp.zeros_like(t)
    for e in range(N_EXPERTS):
        a = jax.nn.silu(t @ w_gate[e]) * (t @ w_up[e])
        y = y + combine[:, e:e + 1].astype(t.dtype) * (a @ w_down[e])
    return y.reshape(b, s, d)

def setup_inputs(seed: int = 0) -> dict:
    key = jax.random.key(seed)
    ks = jax.random.split(key, 18)

    def nrm(k, shape, scale):
        return jax.random.normal(k, shape, jnp.float32) * scale

    x = nrm(ks[0], (BATCH, SEQ, D_MODEL), 1.0)
    c = nrm(ks[1], (BATCH, D_MODEL), 1.0)
    positions = jnp.arange(SEQ, dtype=jnp.int32)[None, :] + jax.random.randint(ks[2], (BATCH, 1), 0, 4096, dtype=jnp.int32)
    ada_w = nrm(ks[3], (DEPTH, D_MODEL, N_MOD * D_MODEL), 0.5 * D_MODEL ** -0.5)
    ada_b = nrm(ks[4], (DEPTH, N_MOD * D_MODEL), 0.02)
    norm_mix_g = 1.0 + nrm(ks[5], (DEPTH, D_MODEL), 0.05)
    norm_ffn_g = 1.0 + nrm(ks[6], (DEPTH, D_MODEL), 0.05)
    a_w_qkv = nrm(ks[7], (N_A_LAYERS, D_MODEL, (A_Q_HEADS + 2 * A_KV_HEADS) * HEAD_DIM), D_MODEL ** -0.5)
    a_w_o = nrm(ks[8], (N_A_LAYERS, A_Q_HEADS * HEAD_DIM, D_MODEL), (A_Q_HEADS * HEAD_DIM) ** -0.5)
    a_sink = nrm(ks[9], (N_A_LAYERS, A_Q_HEADS), 1.0)
    b_w_qkv = nrm(ks[10], (N_B_LAYERS, D_MODEL, len(B_GROUPS) * 3 * B_HEADS * HEAD_DIM), D_MODEL ** -0.5)
    b_w_o = nrm(ks[11], (N_B_LAYERS, B_HEADS * HEAD_DIM, D_MODEL), (B_HEADS * HEAD_DIM) ** -0.5)
    router_w = nrm(ks[12], (D_MODEL, N_EXPERTS), D_MODEL ** -0.5)
    router_bias = nrm(ks[13], (N_EXPERTS,), 0.01)
    exp_w_gate = nrm(ks[14], (DEPTH, N_EXPERTS, D_MODEL, D_EXPERT), D_MODEL ** -0.5)
    exp_w_up = nrm(ks[15], (DEPTH, N_EXPERTS, D_MODEL, D_EXPERT), D_MODEL ** -0.5)
    exp_w_down = nrm(ks[16], (DEPTH, N_EXPERTS, D_EXPERT, D_MODEL), D_EXPERT ** -0.5)
    final_norm_g = 1.0 + nrm(ks[17], (D_MODEL,), 0.05)
    return {'x': x, 'c': c, 'positions': positions, 'ada_w': ada_w, 'ada_b': ada_b,
            'norm_mix_g': norm_mix_g, 'norm_ffn_g': norm_ffn_g,
            'a_w_qkv': a_w_qkv, 'a_w_o': a_w_o, 'a_sink': a_sink,
            'b_w_qkv': b_w_qkv, 'b_w_o': b_w_o,
            'router_w': router_w, 'router_bias': router_bias,
            'exp_w_gate': exp_w_gate, 'exp_w_up': exp_w_up, 'exp_w_down': exp_w_down,
            'final_norm_g': final_norm_g}

def reference(x, c, positions, ada_w, ada_b, norm_mix_g, norm_ffn_g, a_w_qkv, a_w_o, a_sink,
              b_w_qkv, b_w_o, router_w, router_bias, exp_w_gate, exp_w_up, exp_w_down, final_norm_g):
    cos, sin = rope_tables(positions)
    mod_in = jax.nn.silu(c)
    for i in range(DEPTH):
        mod = mod_in @ ada_w[i] + ada_b[i]
        sh_m, sc_m, g_m, sh_f, sc_f, g_f = [t[:, None, :] for t in jnp.split(mod, N_MOD, axis=-1)]
        h = rms_norm(x, norm_mix_g[i]) * (1.0 + sc_m) + sh_m
        j = i // N_MIXERS
        if i % N_MIXERS == 0:
            mix = mixer_a(h, cos, sin, a_w_qkv[j], a_w_o[j], a_sink[j])
        else:
            mix = mixer_b(h, cos, sin, b_w_qkv[j], b_w_o[j])
        x = x + g_m * mix
        h = rms_norm(x, norm_ffn_g[i]) * (1.0 + sc_f) + sh_f
        combine = route(h.reshape(-1, D_MODEL), router_w, router_bias)
        x = x + g_f * moe_ffn(h, combine, exp_w_gate[i], exp_w_up[i], exp_w_down[i])
    return rms_norm(x, final_norm_g)


_drawn_inputs = setup_inputs


def setup_inputs(seed=0):
    import zlib

    import numpy as np

    out = dict(_drawn_inputs(seed))
    spreads = {}
    factors = {'a_sink': 8.0}
    for name, (base, spread) in spreads.items():
        noise = np.random.default_rng([zlib.crc32(name.encode()), seed]).standard_normal(out[name].shape)
        drawn = base * np.exp(spread * noise) if base else spread * noise
        out[name] = __import__('jax').numpy.asarray(drawn.astype(out[name].dtype))
    for name, factor in factors.items():
        out[name] = (out[name] * factor).astype(out[name].dtype)
    return out
```

```python
from contextlib import ExitStack

import numpy as np

import concourse.bass as bass
from concourse import mybir

ALU = mybir.AluOpType
ACT = mybir.ActivationFunctionType
F32 = mybir.dt.float32
I32 = mybir.dt.int32
AX_X = mybir.AxisListType.X

P = 128
S, D = 256, 1024
NT = S // P
KD = D // P
HD = 64
HALF = HD // 2
A_HEADS, A_KV = 16, 4
B_HEADS, B_GRPS = 8, 3
E, GRP = 16, 4
F = 512
KF = F // P
C = 64
PAIRS = E // 2
RING = 6
SLOT = 4096
EPS = 1e-6
SCALE = float(HD) ** -0.5
TWO_PI_HI = 6.28125
TWO_PI_MID = float(np.float32(2 * np.pi - TWO_PI_HI).view(np.uint32) & 0xFFFFF000)
TWO_PI_MID = float(np.uint32(int(TWO_PI_MID)).view(np.float32))
TWO_PI_LO = float(2 * np.pi - TWO_PI_HI - TWO_PI_MID)
ROUND = 1.5 * 2.0 ** 23
PI_SAFE = 3.1415925

IDENT, ONES, TRI, IOTA, INVF = 0, P, 2 * P, 3 * P, 3 * P + S
N_CONST = INVF + HALF


def token_of_row():
    t = np.arange(S).reshape(S // 16, 4, 4)
    return t.transpose(2, 1, 0).reshape(S)


def constants():
    c = np.zeros((P, N_CONST), np.float32)
    c[:, IDENT:IDENT + P] = np.eye(P)
    c[:, ONES:ONES + P] = 1.0
    c[:, TRI:TRI + P] = np.triu(np.ones((P, P)), 1)
    c[:, IOTA:IOTA + S] = np.arange(S)
    c[:, INVF:] = (10000.0 ** (-np.arange(0, HD, 2) / HD)).astype(np.float32)
    return c


def masks():
    t = token_of_row()
    gap = np.abs(t[:, None] - t[None, :])
    own = np.stack([gap[:P, :P], gap[P:, P:]], 1)
    full = np.stack([gap[:P], gap[P:]], 1)
    parts = [full <= 128, full <= 64, (own % 4 == 0) & (own <= 64 * 4), (own % 16 == 0) & (own <= 64 * 16)]
    m = np.concatenate([p.reshape(P, -1) for p in parts], 1)
    return np.where(m, 0.0, -1e30).astype(np.float32)


M_A, M_B0, M_B1, M_B2, N_MASK = 0, 512, 1024, 1280, 1536


def plan_loads():
    order = [("ada", 0, 0, j) for j in range(4)]
    order += [("qkv", 0, j) for j in range(3)]
    order += [("ada", 0, 1, j) for j in range(4)] + [("ada", 0, 2, j) for j in range(4)]
    order += [("wo", 0, j) for j in range(2)]
    order += [("moe", 0, j) for j in range(3 * E)]
    order += [("ada", 1, 0, j) for j in range(4)]
    order += [("qkv", 1, j) for j in range(3)] + [("ada", 1, 1, j) for j in range(4)]
    order += [("qkv", 1, j) for j in range(3, 6)] + [("ada", 1, 2, j) for j in range(4)]
    order += [("qkv", 1, j) for j in range(6, 9)] + [("wo", 1, 0)]
    order += [("moe", 1, j) for j in range(3 * E)]
    return order


ORDER = plan_loads()
LOAD = {name: n for n, name in enumerate(ORDER)}


def plan_units():
    units = [(0, c, t, "kv" if c == 2 else "q") for c in range(3) for t in range(NT)]
    units += [(1, c, t, "qkv"[c % 3]) for c in range(9) for t in range(NT)]
    return units


UNITS = plan_units()


def plan_heads():
    return [(0, 0, h, False) for h in range(A_HEADS)] + \
           [(1, g, h, g > 0) for g in range(B_GRPS) for h in range(B_HEADS)]


HEADS = plan_heads()
RUNS = {(0, 0): (range(0, 6), range(0, 16)),
        (1, 0): (range(6, 12), range(16, 24)),
        (1, 1): (range(12, 18), range(24, 32)),
        (1, 2): (range(18, 24), range(32, 40))}
RUNS_BEFORE = {6: 16, 12: 24, 18: 32}
PIECES = {(layer, part): 7 * layer + (0, 1, 4)[part] for layer in range(2) for part in range(3)}
GATHERS = PAIRS * 2 + 1


def ropes_before(u):
    return sum(k != "v" for _, _, _, k in UNITS[:u])


def v_copies_before(u):
    return sum("v" in k for _, _, _, k in UNITS[:u])


class Own:

    def __init__(self, eng, sem):
        self.eng, self.sem, self.n, self.turn = eng, sem, 0, 0

    def __call__(self, ins):
        self.n += 1
        ins.then_inc(self.sem, 1)
        self.eng.wait_ge(self.sem, self.turn + self.n)


def build(nc, x, c, positions, ada_w, ada_b, norm_mix_g, norm_ffn_g, a_w_qkv, a_w_o, a_sink, b_w_qkv,
          b_w_o, router_w, router_bias, exp_w_gate, exp_w_up, exp_w_down, final_norm_g, const, mask, out):
    ctx = ExitStack()
    with ctx:
        def sb(name, shape, dt=F32):
            return ctx.enter_context(nc.sbuf_tensor(name, shape, dt))

        def sem(name):
            return ctx.enter_context(nc.semaphore(name))

        ring = [sb(f"ring{s}", [P, SLOT]) for s in range(RING)]
        shared = sb("shared", [P, 3 * SLOT])
        xs = sb("xs", [P, NT, D])
        xn = sb("xn", [P, NT, KD, P])
        hT = sb("hT", [P, KD, S])
        acc = sb("acc", [P, 2048])
        gate_b = sb("gate_b", [P, D])
        cst = sb("cst", [P, N_CONST])
        cos2 = sb("cos2", [P, NT, HD])
        sin2 = sb("sin2", [P, NT, HD])
        ye = sb("ye", [P, D])
        xg = [sb(f"xg{b}", [P, KD, C]) for b in range(2)]
        eg = [sb(f"eg{b}", [P, KF * C]) for b in range(2)]
        sg = [sb(f"sg{b}", [P, KF * C]) for b in range(2)]
        aT = [sb(f"aT{b}", [P, KF, C]) for b in range(2)]
        pick = [sb(f"pick{b}", [P, NT, C]) for b in range(2)]
        pw = sb("pw", [P, NT, P])
        pwT = sb("pwT", [P, S])
        colm = sb("colm", [P, 2, 4, KD])
        colb = sb("colb", [P, 2, 6, KD])
        colg = sb("colg", [P, 2, 2, KD])
        colt = sb("colt", [P, KD])
        cc = sb("cc", [P, KD])
        sc = sb("sc", [P, KD])
        ct = sb("ct", [P, 2, KD])
        rw = sb("rw", [P, KD, E])
        rbias = sb("rbias", [P, E])
        sink = sb("sink", [P, A_HEADS])
        posi = sb("posi", [P, NT], I32)
        posf = sb("posf", [P, NT])
        ss = sb("ss", [P, NT])
        std = sb("std", [P, NT])
        rstd = sb("rstd", [P, NT])
        rt = sb("rt", [P, 10, NT * E])
        rr = sb("rr", [P, 4, NT * E])
        sel = sb("sel", [P, NT, E])
        wgt = sb("wgt", [P, NT, E + 2])
        slot = sb("slot", [P, NT, E + 2])
        slot_raw = sb("slot_raw", [P, NT, E])
        cnt = sb("cnt", [P, E + 1], I32)
        cntf = sb("cntf", [P, 1])
        nm = sb("nm", [P, B_GRPS * B_HEADS, NT])
        den = sb("den", [P, B_GRPS * B_HEADS, NT])
        esk = sb("esk", [P, A_HEADS, NT])
        mx = sb("mx", [P, NT])
        aw = sb("aw", [P, 3, B_GRPS * B_HEADS, NT])
        ps = ctx.enter_context(nc.psum_tensor("ps", [P, 8, 512], F32))

        ident = cst[:, IDENT:IDENT + P]
        ones = cst[:, ONES:ONES + P]
        tri = cst[:, TRI:TRI + P]

        def area(at, n):
            return shared[:, at:at + n]
        qT = area(0, 2048).rearrange("p (c t) -> p c t", t=S)
        kT = area(2048, 1024).rearrange("p (c t) -> p c t", t=S)
        vv = area(3072, 1024).rearrange("p (t n) -> p t n", t=NT)
        sm = [area(4096 + 512 * b, 512) for b in range(2)]
        pr = [area(5120 + 512 * b, 512) for b in range(2)]
        pT = [area(6144 + 512 * b, 512) for b in range(2)]
        o_all = area(7168, 3072)
        msk = area(10240, N_MASK)
        oA = o_all[:, 0:2048].rearrange("p (t n) -> p t n", t=NT)
        oB = o_all.rearrange("p (g t n) -> p g t n", g=B_GRPS, t=NT)
        xnf = xn[:, :, :, :].rearrange("p t k n -> p (t k n)")
        rope1, rope2 = xnf[:, 0:512], xnf[:, 512:1024]
        roped_sb = [xnf[:, 1024 + 512 * b:1536 + 512 * b] for b in range(2)]
        oT = hT
        yacc = hT[:, :, :].rearrange("p k s -> p (k s)").rearrange("p (t n) -> p t n", t=NT)
        junk = yacc
        x_gate, x_up, x_down = (area(SLOT * j, SLOT) for j in range(3))
        ang, turns = xnf[:, 0:64], xnf[:, 64:128]

        landed = [sem(f"landed{s}") for s in range(RING)]
        s_const, s_x, s_c, s_misc, s_bias, s_out = (sem(n) for n in (
            "const_landed", "x_landed", "c_landed", "misc_landed", "gate_bias_landed", "out_stored"))
        s_mask = sem("mask_landed")
        dve_step, act_step = sem("dve_step"), sem("act_step")
        c_exp, c_silu, angles, tables = sem("c_exp"), sem("c_silu"), sem("angles"), sem("rope_tables")
        ada_summed, ada_read = sem("ada_summed"), sem("ada_read")
        mod_out, mod_read = sem("mod_out"), sem("mod_read")
        squared, var_ready, std_ready = sem("squared"), sem("var_ready"), sem("std_ready")
        xn_ready, xn_turned = sem("xn_ready"), sem("xn_turned")
        hT_dve, hT_act = sem("hT_dve"), sem("hT_act")
        projected, rope_read, roped = sem("projected"), sem("rope_read"), sem("roped")
        v_copied, qk_turned, qk_copied = sem("v_copied"), sem("qk_turned"), sem("qk_copied")
        scored, masked, negmax, exped = sem("scored"), sem("masked"), sem("negmax"), sem("exped")
        sink_exped, p_turned, pT_copied = sem("sink_exped"), sem("p_turned"), sem("pT_copied")
        pv_done, o_copied = sem("pv_done"), sem("o_copied")
        merge_in, merge_exped, o_ready = sem("merge_in"), sem("merge_exped"), sem("o_ready")
        o_turned, oT_dve, oT_act = sem("o_turned"), sem("oT_dve"), sem("oT_act")
        mixed, x_updated = sem("mixed"), sem("x_updated")
        logits, logits_exped, routed = sem("logits"), sem("logits_exped"), sem("routed")
        ranked, counted = sem("ranked"), sem("counted")
        picked, pw_ready, pw_turned, pwT_ready = sem("picked"), sem("pw_ready"), sem("pw_turned"), sem("pwT_ready")
        gathered, xg_ready = sem("gathered"), sem("xg_ready")
        gate_done, up_done, gate_exped, a_ready = sem("gate_done"), sem("up_done"), sem("gate_exped"), sem("a_ready")
        down_done, y_copied = sem("down_done"), sem("y_copied")
        scattered, scatter_free = sem("scattered"), sem("scatter_free")
        e_landed, e_picked, e_gathered, e_xg = sem("e_landed"), sem("e_picked"), sem("e_gathered"), sem("e_xg")
        e_up, e_exped, e_a, e_down, e_y = sem("e_up"), sem("e_exped"), sem("e_a"), sem("e_down"), sem("e_y")
        e_scattered, e_added, e_dve = sem("e_scattered"), sem("e_added"), sem("e_dve")

        def slot_of(name):
            return ring[LOAD[name] % RING]

        def arrived(eng, name):
            n = LOAD[name]
            eng.wait_ge(landed[n % RING], 16 * (n // RING + 1))

        def last_use(name):
            kind, layer = name[0], name[1]
            if kind == "ada":
                return ada_read, 12 * layer + 4 * name[2] + name[3] + 1
            if kind == "qkv":
                return projected, 6 * layer + 2 * name[2] + 2
            if kind == "wo":
                return mixed, 4 * layer + 4
            expert = E * layer + name[2] // 3
            return (gate_done, up_done, down_done)[name[2] % 3], expert + 1

        def source(name):
            kind, layer = name[0], name[1]
            if kind == "ada":
                part, j = name[2], name[3]
                return ada_w[layer].rearrange("(p k) n -> p k n", k=KD)[:, 2 * j:2 * j + 2,
                                                                     2048 * part:2048 * part + 2048]
            if kind == "qkv":
                w = (a_w_qkv, b_w_qkv)[layer][0].rearrange("(p k) n -> p k n", k=KD)
                at = 512 * name[2]
                if layer == 1:
                    at = 1536 * (name[2] // 3) + 512 * (name[2] % 3)
                return w[:, :, at:at + 512]
            w = (a_w_o, b_w_o)[layer][0].rearrange("(c p) n -> p c n", p=P)
            return w[:, 4 * name[2]:4 * name[2] + 4, :]

        def expert_source(layer, e, part):
            w = (exp_w_gate, exp_w_up, exp_w_down)[part][layer][bass.ds(e, 1)]
            if part == 2:
                return w.rearrange("e (c p) n -> p (e c) n", p=P)
            return w.rearrange("e (p k) f -> p (e k) f", k=KD)

        def as_chunks(t, n):
            return t[:, :].rearrange("p (k n) -> p k n", n=n)

        def rows_of(dram, q):
            return dram.rearrange("(a b c) d -> c b a d", a=S // 16, b=4, c=4)[q]

        def extra_blocks(eng, layer, block_of):
            eng.wait_ge(counted, layer + 1)
            most = eng.value_load(cnt[0:1, E:E + 1], min_val=0, max_val=S)
            with eng.If(most > C):
                with eng.Fori(0, E) as e:
                    tokens = eng.value_load(cnt[0:1, bass.ds(e, 1)], min_val=0, max_val=S)
                    with eng.Fori(1, S // C) as j:
                        with eng.If(tokens > j * C):
                            block_of(layer, e, j)

        block = ctx.enter_context(nc.Block())

        @block.sync
        def _(sp):
            def load(name):
                n = LOAD[name]
                if n >= RING:
                    sp.wait_ge(*last_use(ORDER[n - RING]))
                t = slot_of(name)
                width = {"ada": 2048, "qkv": 512, "wo": D}[name[0]]
                sp.dma_start(as_chunks(t, width), source(name)).then_inc(landed[n % RING], 16)

            def load_experts(layer):
                base = LOAD[("moe", layer, 0)]

                def one_pair(i, first):
                    for j in range(6):
                        n = base + j
                        if first:
                            sp.wait_ge(*last_use(ORDER[n - RING]))
                        else:
                            done, value = last_use(ORDER[n])
                            sp.wait_ge(done, i * 2 + (value - 2))
                        sp.dma_start(as_chunks(ring[n % RING], D if j % 3 == 2 else F),
                                     expert_source(layer, i * 2 + j // 3, j % 3))\
                          .then_inc(landed[n % RING], 16)
                one_pair(0, True)
                with sp.Fori(1, PAIRS) as i:
                    one_pair(i, False)

            for n in range(LOAD[("moe", 0, 0)]):
                load(ORDER[n])
            load_experts(0)
            for n in range(LOAD[("ada", 1, 0, 0)], LOAD[("moe", 1, 0)]):
                load(ORDER[n])
            load_experts(1)
            sp.wait_ge(x_updated, 5)
            for q in range(4):
                sp.dma_start(rows_of(out[0], q), yacc[64 * (q % 2):64 * (q % 2) + 64, q // 2, :])\
                  .then_inc(s_out, 16)
            sp.wait_ge(s_out, 64)

        @block.scalar
        def _(act):
            own = Own(act, act_step)
            act.dma_start(cc[:, :], c[0].rearrange("(p k) -> p k", k=KD)).then_inc(s_c, 16)
            for q in range(4):
                rows = slice(64 * (q % 2), 64 * (q % 2) + 64)
                act.dma_start(xs[rows, q // 2, :], rows_of(x[0], q)).then_inc(s_x, 16)
            act.dma_start(cst[:, :], const).then_inc(s_const, 16)
            pos_rows = positions.rearrange("o (a b c) -> c b a o", a=S // 16, b=4, c=4)
            for q in range(4):
                act.dma_start(posi[64 * (q % 2):64 * (q % 2) + 64, q // 2:q // 2 + 1], pos_rows[q],
                              allow_slow_non_contiguous=True).then_inc(s_const, 16)
            act.dma_start(msk, mask).then_inc(s_mask, 16)
            for layer in range(2):
                act.dma_start(colb[:, layer], ada_b[layer].rearrange("(v p k) -> p v k", v=6, k=KD))\
                   .then_inc(s_misc, 16)
                act.dma_start(colg[:, layer, 0], norm_mix_g[layer].rearrange("(p k) -> p k", k=KD)).then_inc(s_misc, 16)
                act.dma_start(colg[:, layer, 1], norm_ffn_g[layer].rearrange("(p k) -> p k", k=KD)).then_inc(s_misc, 16)
            act.dma_start(rw[:, :, :], router_w.rearrange("(p k) e -> p k e", k=KD)).then_inc(s_misc, 16)
            act.dma_start(rbias[:, :], router_bias.partition_broadcast(P)).then_inc(s_misc, 16)
            act.dma_start(sink[:, :], a_sink[0].partition_broadcast(P)).then_inc(s_misc, 16)

            def gate_bias(layer, vector):
                act.dma_start(gate_b[:, :], ada_b[layer, D * vector:D * vector + D].partition_broadcast(P))\
                   .then_inc(s_bias, 16)
            gate_bias(0, 2)

            act.wait_ge(s_c, 16)
            act.activation(ct[:, 0], cc[:, :], ACT.Exp, scale=-1.0).then_inc(c_exp, 1)
            act.wait_ge(angles, 2)
            for t in range(NT):
                act.activation(cos2[:, t, 0:HALF], ang[:, t * HALF:(t + 1) * HALF], ACT.Sin).then_inc(tables, 1)
                act.activation(cos2[:, t, HALF:HD], ang[:, t * HALF:(t + 1) * HALF], ACT.Sin).then_inc(tables, 1)
                act.activation(sin2[:, t, HALF:HD], turns[:, t * HALF:(t + 1) * HALF], ACT.Sin).then_inc(tables, 1)
                act.activation(sin2[:, t, 0:HALF], turns[:, t * HALF:(t + 1) * HALF], ACT.Sin, scale=-1.0).then_inc(tables, 1)

            def norm(n):
                if n == 0:
                    act.wait_ge(s_x, 64)
                else:
                    act.wait_ge(x_updated, n)
                for t in range(NT):
                    act.activation(junk[:, t], xs[:, t], ACT.Square, accum_out=ss[:, t:t + 1]).then_inc(squared, 1)
                act.wait_ge(var_ready, n + 1)
                act.activation(std[:, :], ss[:, :], ACT.Sqrt).then_inc(std_ready, 1)

            def modulate(n):
                layer, which = n // 2, n % 2
                act.wait_ge(mod_read, PIECES[layer, 0] + 1 if which == 0 else PIECES[layer, 2] + 1)
                for b in (1, 3):
                    act.wait_ge(xn_turned, 4 * n + b + 1)
                    for k in (2 * b, 2 * b + 1):
                        act.activation(hT[:, k, :], ps[:, b, (k % 2) * S:(k % 2 + 1) * S], ACT.Identity,
                                       bias=colm[:, layer, 2 * which + 1, k:k + 1],
                                       scale=colm[:, layer, 2 * which, k:k + 1]).then_inc(hT_act, 1)

            def project(units):
                if units[0] > 0:
                    act.wait_ge(pv_done, RUNS_BEFORE[units[0]])
                for u in units:
                    layer, chunk, t, kind = UNITS[u]
                    if "v" in kind:
                        act.wait_ge(projected, u + 1)
                        if kind == "kv":
                            act.wait_ge(rope_read, ropes_before(u) + 1)
                            src, dst = ps[:, 6 + u % 2, 256:512], vv[:, t, 0:256]
                        else:
                            src, dst = ps[:, 6 + u % 2, :], vv[:, t, :]
                        act.activation(dst, src, ACT.Copy).then_inc(v_copied, 1)
                    if kind != "v":
                        r = ropes_before(u)
                        act.wait_ge(qk_turned, r + 1)
                        if kind == "q":
                            first = 4 * (chunk % 3) if layer == 0 else 0
                            dst = qT[:, first:first + 4, t * P:(t + 1) * P]
                        else:
                            dst = kT[:, :, t * P:(t + 1) * P]
                        act.activation(dst, ps[:, r % 2, :].rearrange("p (c t) -> p c t", t=P), ACT.Copy)\
                           .then_inc(qk_copied, 1)

            def copy_pT(s):
                narrow = HEADS[s][3]
                act.wait_ge(p_turned, s + 1)
                if s >= 2:
                    act.wait_ge(pv_done, s - 1)
                n = S if narrow else 2 * S
                act.activation(pT[s % 2][:, 0:n], ps[:, 2 + s % 2, 0:n], ACT.Copy).then_inc(pT_copied, 1)

            def heads(steps):
                for s in steps:
                    layer, group, h, narrow = HEADS[s]
                    width = P if narrow else S
                    col = group * B_HEADS + h
                    act.wait_ge(negmax, s + 1)
                    if s >= 2:
                        act.wait_ge(p_turned, s - 1)
                    for t in range(NT):
                        act.activation(pr[s % 2][:, t * width:(t + 1) * width], sm[s % 2][:, t * width:(t + 1) * width],
                                       ACT.Exp, bias=nm[:, col, t:t + 1], accum_out=den[:, col, t:t + 1])\
                           .then_inc(exped, 1)
                    if layer == 0:
                        act.activation(esk[:, h, :], nm[:, col, :], ACT.Exp, bias=sink[:, h:h + 1])\
                           .then_inc(sink_exped, 1)
                    if s > steps[0]:
                        copy_pT(s - 1)
                copy_pT(steps[-1])

            def copy_oT(layer):
                for b in (range(4) if layer == 0 else range(2)):
                    if b % 2:
                        act.wait_ge(o_turned, (0, 4)[layer] + b + 1)
                        act.activation(oT[:, 2 * b:2 * b + 2, :], ps[:, b, :].rearrange("p (c t) -> p c t", t=S),
                                       ACT.Copy).then_inc(oT_act, 1)

            def experts(layer):
                act.wait_ge(logits, layer + 1)
                act.activation(rt[:, 0], ps[:, 4, 0:NT * E], ACT.Exp, scale=-1.0).then_inc(logits_exped, 1)
                q0 = PAIRS * layer
                with act.Fori(0, PAIRS) as i:
                    for b in range(2):
                        act.wait_ge(up_done, i * 2 + (2 * q0 + b + 1))
                        act.activation(eg[b][:, :], ps[:, 1 + b, 0:KF * C], ACT.Exp, scale=-1.0).then_inc(gate_exped, 1)
                    for b in range(2):
                        rows = slice(C * b, C * b + C)
                        act.wait_ge(down_done, i * 2 + (2 * q0 + b + 1))
                        act.wait_ge(scatter_free, i * 4 + (4 * q0 + 2 * layer + 2))
                        for h in range(2):
                            act.activation(ye[rows, 512 * h:512 * h + 512], ps[rows, 3 + h, :], ACT.Copy)\
                               .then_inc(y_copied, 1)

            blocks = act.alloc_register("act_blocks")
            act.reg_mov(blocks, 1)

            def extra_block(layer, e, j):
                act.wait_ge(e_added, blocks)
                for part, dst in enumerate((x_gate, x_up, x_down)):
                    act.dma_start(as_chunks(dst, D if part == 2 else F), expert_source(layer, e, part))\
                       .then_inc(e_landed, 16)
                act.wait_ge(e_up, blocks)
                act.activation(eg[0][:, :], ps[:, 1, 0:KF * C], ACT.Exp, scale=-1.0).then_inc(e_exped, 1)
                act.wait_ge(e_down, blocks)
                act.activation(ye[0:C, 0:512], ps[0:C, 3, :], ACT.Copy)
                act.activation(ye[0:C, 512:D], ps[0:C, 4, :], ACT.Copy).then_inc(e_y, 1)
                act.reg_add(blocks, blocks, 1)

            norm(0)
            modulate(0)
            project(RUNS[0, 0][0])
            heads(RUNS[0, 0][1])
            copy_oT(0)
            act.wait_ge(x_updated, 1)
            gate_bias(0, 5)
            norm(1)
            modulate(1)
            experts(0)
            extra_blocks(act, 0, extra_block)
            act.wait_ge(x_updated, 2)
            gate_bias(1, 2)
            act.dma_start(msk, mask).then_inc(s_mask, 16)
            norm(2)
            modulate(2)
            for g in range(B_GRPS):
                project(RUNS[1, g][0])
                heads(RUNS[1, g][1])
            act.wait_ge(merge_in, 1)
            act.activation(aw[:, 0], aw[:, 0], ACT.Exp, scale=-1.0).then_inc(merge_exped, 1)
            copy_oT(1)
            act.wait_ge(x_updated, 3)
            gate_bias(1, 5)
            norm(3)
            modulate(3)
            experts(1)
            extra_blocks(act, 1, extra_block)
            act.wait_ge(x_updated, 4)
            act.dma_start(gate_b[:, :], final_norm_g.partition_broadcast(P)).then_inc(s_bias, 16)
            norm(4)

        @block.vector
        def _(dve):
            own = Own(dve, dve_step)
            own(dve.memset(wgt[:, :, :], 0.0))
            dve.memset(slot[:, :, :], -1.0).then_inc(e_added, 1)

            def sign(ins, s, value):
                ins.then_inc(s, 1)
                dve.wait_ge(s, value)

            dve.wait_ge(c_exp, 1)
            own(dve.tensor_scalar(ct[:, 1], ct[:, 0], 1.0, None, ALU.add))
            own(dve.reciprocal(ct[:, 0], ct[:, 1]))
            sign(dve.tensor_tensor(sc[:, :], cc[:, :], ct[:, 0], ALU.mult), c_silu, 1)

            dve.wait_ge(s_const, 80)
            own(dve.tensor_copy(posf[:, :], posi[:, :]))
            raw, k1, k2 = xnf[:, 128:192], xnf[:, 192:256], xnf[:, 256:320]
            for t in range(NT):
                own(dve.tensor_scalar(raw[:, t * HALF:(t + 1) * HALF], cst[:, INVF:INVF + HALF], posf[:, t:t + 1], None,
                                      ALU.mult))
            for dst, lead in ((ang, 0.25), (turns, 0.0)):
                own(dve.tensor_scalar(k1, raw, 1.0 / (2 * np.pi), lead, ALU.mult, ALU.add))
                own(dve.tensor_scalar(k2, k1, ROUND, None, ALU.add))
                own(dve.tensor_scalar(k1, k2, ROUND, None, ALU.subtract))
                own(dve.scalar_tensor_tensor(dst, k1, -TWO_PI_HI, raw, ALU.mult, ALU.add))
                own(dve.scalar_tensor_tensor(k2, k1, -TWO_PI_MID, dst, ALU.mult, ALU.add))
                own(dve.scalar_tensor_tensor(dst, k1, -TWO_PI_LO, k2, ALU.mult, ALU.add))
                own(dve.tensor_scalar(k2, dst, lead * 2 * np.pi, PI_SAFE, ALU.add, ALU.min))
                dve.tensor_scalar(dst, k2, -PI_SAFE, None, ALU.max).then_inc(angles, 1)

            def ada(layer, part, k):
                name = ("ada", layer, part, k // 2)
                w = as_chunks(slot_of(name), 2048)[:, k % 2, :]
                if k % 2 == 0:
                    arrived(dve, name)
                if k == 0:
                    before = PIECES[layer, part]
                    if before:
                        dve.wait_ge(mod_out, before)
                    ins = dve.tensor_scalar(acc[:, :], w, sc[:, 0:1], None, ALU.mult)
                else:
                    ins = dve.scalar_tensor_tensor(acc[:, :], w, sc[:, k:k + 1], acc[:, :], ALU.mult, ALU.add)
                if k % 2:
                    sign(ins, ada_read, 12 * layer + 4 * part + k // 2 + 1)
                else:
                    own(ins)

            def mod(layer, part):
                n = PIECES[layer, part]
                dve.wait_ge(mod_out, n + 1)
                if n == 0:
                    dve.wait_ge(s_misc, 144)
                b = ps[:, 6 + n % 2, :]
                if part == 0:
                    own(dve.tensor_tensor(colm[:, layer, 1], b[:, 0:KD], colb[:, layer, 0], ALU.add))
                    own(dve.tensor_tensor(colt[:, :], b[:, KD:2 * KD], colb[:, layer, 1], ALU.add))
                    sign(dve.scalar_tensor_tensor(colm[:, layer, 0], colt[:, :], 1.0, colg[:, layer, 0], ALU.add,
                                                  ALU.mult), mod_read, n + 1)
                    return
                if part == 1:
                    sign(dve.tensor_tensor(colm[:, layer, 3], b[:, 0:KD], colb[:, layer, 3], ALU.add), mod_read, n + 1)
                else:
                    own(dve.tensor_tensor(colt[:, :], b[:, 0:KD], colb[:, layer, 4], ALU.add))
                    sign(dve.scalar_tensor_tensor(colm[:, layer, 2], colt[:, :], 1.0, colg[:, layer, 1], ALU.add,
                                                  ALU.mult), mod_read, n + 1)
                dve.wait_ge(s_bias, 16 * (2 * layer + part))
                for h in range(2):
                    dve.wait_ge(mod_out, n + 2 + h)
                    part_b = gate_b[:, 512 * h:512 * h + 512]
                    sign(dve.tensor_tensor(part_b, ps[:, 6 + (n + 1 + h) % 2, :], part_b, ALU.add), mod_read, n + 2 + h)

            def norm(n):
                dve.wait_ge(squared, 2 * n + 2)
                sign(dve.tensor_scalar(ss[:, :], ss[:, :], 1.0 / D, EPS, ALU.mult, ALU.add), var_ready, n + 1)
                dve.wait_ge(std_ready, n + 1)
                own(dve.reciprocal(rstd[:, :], std[:, :]))

            def norm_and_modulate(n):
                norm(n)
                if n == 0:
                    dve.wait_ge(tables, 8)
                for t in range(NT):
                    dve.tensor_scalar(xn[:, t].rearrange("p k n -> p n k"),
                                      xs[:, t].rearrange("p (n k) -> p n k", k=KD), rstd[:, t:t + 1], None, ALU.mult)\
                       .then_inc(xn_ready, 1)
                layer, which = n // 2, n % 2
                if which == 0:
                    mod(layer, 0)
                else:
                    mod(layer, 2)
                for b in (0, 2):
                    dve.wait_ge(xn_turned, 4 * n + b + 1)
                    for k in (2 * b, 2 * b + 1):
                        dve.tensor_scalar(hT[:, k, :], ps[:, b, (k % 2) * S:(k % 2 + 1) * S],
                                          colm[:, layer, 2 * which, k:k + 1], colm[:, layer, 2 * which + 1, k:k + 1],
                                          ALU.mult, ALU.add).then_inc(hT_dve, 1)

            def project(units):
                if units[0] in (0, 6):
                    dve.wait_ge(xn_turned, 4 if units[0] == 0 else 12)
                for u in units:
                    layer, chunk, t, kind = UNITS[u]
                    if kind == "v":
                        continue
                    r = ropes_before(u)
                    n = 256 if kind == "kv" else 512
                    hn = n // HD
                    b = ps[:, 6 + u % 2, 0:n]
                    b3 = b.rearrange("p (h d) -> p h d", d=HD)
                    r2 = rope2[:, 0:n].rearrange("p (h d) -> p h d", d=HD)
                    dve.wait_ge(projected, u + 1)
                    own(dve.tensor_tensor(rope1[:, 0:n].rearrange("p (h d) -> p h d", d=HD), b3,
                                          cos2[:, t].unsqueeze(1).to_broadcast([P, hn, HD]), ALU.mult))
                    own(dve.tensor_tensor(r2[:, :, 0:HALF], b3[:, :, HALF:HD],
                                          sin2[:, t, 0:HALF].unsqueeze(1).to_broadcast([P, hn, HALF]), ALU.mult))
                    sign(dve.tensor_tensor(r2[:, :, HALF:HD], b3[:, :, 0:HALF],
                                           sin2[:, t, HALF:HD].unsqueeze(1).to_broadcast([P, hn, HALF]), ALU.mult),
                         rope_read, r + 1)
                    if r >= 2:
                        dve.wait_ge(qk_turned, r - 1)
                    if kind == "kv":
                        dup = roped_sb[r % 2].rearrange("p (j two d) -> p j two d", two=2, d=HD)
                        a, bb = (z[:, 0:n].rearrange("p (j d) -> p j d", d=HD) for z in (rope1, rope2))
                        own(dve.tensor_tensor(dup[:, :, 0], a, bb, ALU.add))
                        sign(dve.tensor_tensor(dup[:, :, 1], a, bb, ALU.add), roped, r + 1)
                    else:
                        sign(dve.tensor_tensor(roped_sb[r % 2], rope1, rope2, ALU.add), roped, r + 1)

            def take_o(s):
                layer, group, h, narrow = HEADS[s]
                dve.wait_ge(exped, 2 * s + 2)
                dve.wait_ge(pv_done, s + 1)
                src = ps[:, 4 + s % 2, 0:NT * HD].rearrange("p (t d) -> p t d", d=HD)
                if layer == 0:
                    dve.wait_ge(sink_exped, h + 1)
                    own(dve.tensor_tensor(den[:, h], den[:, h], esk[:, h], ALU.add))
                    own(dve.reciprocal(esk[:, h], den[:, h]))
                    dve.tensor_tensor(oA[:, :, HD * h:HD * h + HD], src,
                                      esk[:, h].unsqueeze(2).to_broadcast([P, NT, HD]), ALU.mult).then_inc(o_copied, 1)
                else:
                    dve.tensor_copy(oB[:, group, :, HD * h:HD * h + HD], src).then_inc(o_copied, 1)

            def heads(steps, side):
                for s in steps:
                    layer, group, h, narrow = HEADS[s]
                    width = P if narrow else S
                    col = group * B_HEADS + h
                    m = (M_A if layer == 0 else (M_B0, M_B1, M_B2)[group])
                    dve.wait_ge(s_mask, 16 * (layer + 1))
                    dve.wait_ge(scored, s + 1)
                    if s >= 2:
                        dve.wait_ge(exped, 2 * (s - 1))
                    sign(dve.scalar_tensor_tensor(sm[s % 2][:, 0:2 * width], ps[:, s % 2, 0:2 * width], SCALE,
                                                  msk[:, m:m + 2 * width], ALU.mult, ALU.add), masked, s + 1)
                    own(dve.reduce_max(mx[:, :], sm[s % 2][:, 0:2 * width].rearrange("p (t n) -> p t n", t=NT), AX_X))
                    if layer == 0:
                        dve.tensor_scalar(nm[:, col], mx[:, :], sink[:, h:h + 1], -1.0, ALU.max, ALU.mult).then_inc(negmax, 1)
                    else:
                        dve.tensor_scalar(nm[:, col], mx[:, :], -1.0, None, ALU.mult).then_inc(negmax, 1)
                    if s - steps[0] >= 3:
                        take_o(s - 3)
                    for job in side.get(s - steps[0], ()):
                        job()
                for s in steps[-3:]:
                    take_o(s)

            def mix_out(layer):
                for b in (range(4) if layer == 0 else range(2)):
                    if b % 2 == 0:
                        dve.wait_ge(o_turned, (0, 4)[layer] + b + 1)
                        dve.tensor_copy(oT[:, 2 * b:2 * b + 2, :], ps[:, b, :].rearrange("p (c t) -> p c t", t=S))\
                           .then_inc(oT_dve, 1)
                for n in range(4):
                    t, h = n // 2, n % 2
                    cols = slice(512 * h, 512 * h + 512)
                    tmp = xnf[:, 512 * n:512 * n + 512]
                    dve.wait_ge(mixed, 4 * layer + n + 1)
                    own(dve.tensor_tensor(tmp, ps[:, 4 + n, :], gate_b[:, cols], ALU.mult))
                    ins = dve.tensor_tensor(xs[:, t, cols], xs[:, t, cols], tmp, ALU.add)
                    if n == 3:
                        sign(ins, x_updated, 2 * layer + 1)
                    else:
                        own(ins)

            def ranks(values, n):
                for j in range(4):
                    cmp = rr[:, j, 0:4 * n].rearrange("p (g i) -> p g i", i=4)
                    dve_first = values[:, :, j:j + 1]
                    own(dve.tensor_tensor(cmp[:, :, 0:j + 1], dve_first.to_broadcast([P, n, j + 1]),
                                          values[:, :, 0:j + 1], ALU.is_gt))
                    if j < 3:
                        own(dve.tensor_tensor(cmp[:, :, j + 1:4], dve_first.to_broadcast([P, n, 3 - j]),
                                              values[:, :, j + 1:4], ALU.is_ge))
                own(dve.tensor_tensor(rr[:, 0:2, 0:4 * n], rr[:, 0:2, 0:4 * n], rr[:, 2:4, 0:4 * n], ALU.add))
                own(dve.tensor_tensor(rr[:, 0, 0:4 * n], rr[:, 0, 0:4 * n], rr[:, 1, 0:4 * n], ALU.add))

            def route(layer):
                scores, biased, hi, lo, m1, m2, g_score, g_sel, wsel = (rt[:, j] for j in range(1, 10))
                dve.wait_ge(logits_exped, layer + 1)
                own(dve.tensor_scalar(biased, rt[:, 0], 1.0, None, ALU.add))
                own(dve.reciprocal(scores, biased))
                own(dve.tensor_tensor(biased.rearrange("p (t e) -> p t e", t=NT),
                                      scores.rearrange("p (t e) -> p t e", t=NT),
                                      rbias[:, :].unsqueeze(1).to_broadcast([P, NT, E]), ALU.add))
                b4 = biased.rearrange("p (g i) -> p g i", i=4)
                pair = biased.rearrange("p (m two) -> p m two", two=2)
                own(dve.tensor_tensor(hi[:, 0:16], pair[:, :, 0], pair[:, :, 1], ALU.max))
                own(dve.tensor_tensor(lo[:, 0:16], pair[:, :, 0], pair[:, :, 1], ALU.min))
                h2, l2 = (z[:, 0:16].rearrange("p (g two) -> p g two", two=2) for z in (hi, lo))
                own(dve.tensor_tensor(m1[:, 0:8], h2[:, :, 0], h2[:, :, 1], ALU.max))
                own(dve.tensor_tensor(m2[:, 0:8], h2[:, :, 0], h2[:, :, 1], ALU.min))
                own(dve.tensor_tensor(m2[:, 8:16], l2[:, :, 0], l2[:, :, 1], ALU.max))
                own(dve.tensor_tensor(m2[:, 16:24], m2[:, 0:8], m2[:, 8:16], ALU.max))
                own(dve.tensor_tensor(g_score[:, 0:8], m1[:, 0:8], m2[:, 16:24], ALU.add))
                ranks(g_score[:, 0:8].rearrange("p (t g) -> p t g", g=4), NT)
                own(dve.tensor_scalar(g_sel[:, 0:8], rr[:, 0, 0:8], 0.5, None, ALU.is_lt))
                ranks(b4, 8)
                s3 = sel[:, :, :].rearrange("p t (g i) -> p (t g) i", i=4)
                sign(dve.scalar_tensor_tensor(s3, rr[:, 0, :].rearrange("p (g i) -> p g i", i=4), 1.5,
                                             g_sel[:, 0:8].unsqueeze(2).to_broadcast([P, 8, 4]), ALU.is_lt, ALU.mult),
                     routed, layer + 1)
                w3 = wsel.rearrange("p (t e) -> p t e", t=NT)
                own(dve.tensor_tensor(w3, scores.rearrange("p (t e) -> p t e", t=NT), sel[:, :, :], ALU.mult))
                own(dve.reduce_sum(m1[:, 0:NT], w3, AX_X))
                own(dve.reciprocal(m2[:, 0:NT], m1[:, 0:NT]))
                own(dve.tensor_tensor(wgt[:, :, 0:E], w3, m2[:, 0:NT].unsqueeze(2).to_broadcast([P, NT, E]), ALU.mult))
                dve.wait_ge(ranked, layer + 1)
                own(dve.scalar_tensor_tensor(slot_raw[:, :, :], ps[:, 5, 0:NT * E].rearrange("p (t e) -> p t e", t=NT), 1.0,
                                             sel[:, :, :], ALU.add, ALU.mult))
                own(dve.tensor_scalar(slot[:, :, 0:E], slot_raw[:, :, :], -1.0, None, ALU.add))
                own(dve.reduce_max(cntf[:, :], ps[:, 5, NT * E:NT * E + E], AX_X))
                own(dve.tensor_copy(cnt[:, E:E + 1], cntf[:, :]))
                sign(dve.tensor_copy(cnt[:, 0:E], ps[:, 5, NT * E:NT * E + E]), counted, layer + 1)

            def make_pick(buf, e):
                for t in range(NT):
                    dve.tensor_scalar(pick[buf][:, t, :], cst[:, IOTA:IOTA + C], slot[:, t, bass.ds(e, 1)], None,
                                      ALU.is_equal).then_inc(picked, 1)

            def modulate_gather(buf, layer, n):
                dve.wait_ge(gathered, n)
                g3 = ps[:, 0, :].rearrange("p (k s) -> p k s", s=C)
                own(dve.tensor_tensor(xg[buf][:, :, :], g3, colm[:, layer, 2].unsqueeze(2).to_broadcast([P, KD, C]),
                                      ALU.mult))
                dve.tensor_tensor(xg[buf][:, :, :], xg[buf][:, :, :],
                                  colm[:, layer, 3].unsqueeze(2).to_broadcast([P, KD, C]), ALU.add).then_inc(xg_ready, 1)

            def experts(layer):
                q0, g0 = PAIRS * layer, GATHERS * layer
                for t in range(NT):
                    dve.memset(yacc[:, t], 0.0).then_inc(scatter_free, 1)
                make_pick(0, 0)
                modulate_gather(0, layer, g0 + 1)
                static = own.n
                per = 2 * 1 + 2 * 3
                with dve.Fori(0, PAIRS) as i:
                    own.turn = i * per

                    def silu_mul(b):
                        gate, up = ps[:, 1 + b, 0:KF * C], ps[:, 1 + b, KF * C:2 * KF * C]
                        dve.wait_ge(gate_exped, i * 2 + (2 * q0 + b + 1))
                        own(dve.tensor_scalar(sg[b][:, :], eg[b][:, :], 1.0, None, ALU.add))
                        own(dve.reciprocal(eg[b][:, :], sg[b][:, :]))
                        own(dve.tensor_tensor(sg[b][:, :], gate, eg[b][:, :], ALU.mult))
                        dve.tensor_tensor(aT[b][:, :, :].rearrange("p k s -> p (k s)"), up, sg[b][:, :], ALU.mult)\
                           .then_inc(a_ready, 1)

                    make_pick(1, i * 2 + 1)
                    for b in range(2):
                        for t in range(NT):
                            ins = dve.tensor_scalar(pw[:, t, C * b:C * b + C], cst[:, IOTA:IOTA + C],
                                                    slot[:, t, bass.ds(i * 2 + b, 1)], wgt[:, t, bass.ds(i * 2 + b, 1)],
                                                    ALU.is_equal, ALU.mult)
                    ins.then_inc(pw_ready, 1)
                    modulate_gather(1, layer, i * 2 + (g0 + 2))
                    dve.wait_ge(pw_turned, i + (q0 + 1))
                    dve.tensor_copy(pwT[:, :], ps[:, 7, 0:S]).then_inc(pwT_ready, 1)
                    silu_mul(0)
                    make_pick(0, i * 2 + 2)
                    silu_mul(1)
                    modulate_gather(0, layer, i * 2 + (g0 + 3))
                    for n in range(4):
                        t, h = n // 2, n % 2
                        y = yacc[:, t, 512 * h:512 * h + 512]
                        dve.wait_ge(scattered, i * 4 + (4 * q0 + n + 1))
                        dve.tensor_tensor(y, y, ps[:, 5 + n % 2, :], ALU.add).then_inc(scatter_free, 1)
                assert own.n - static == per, own.n - static
                own.turn = 0
                own.n = static + per * PAIRS

            blocks = dve.alloc_register("dve_blocks")
            steps = dve.alloc_register("dve_steps")
            dve.reg_mov(blocks, 1)
            dve.reg_mov(steps, 0)

            def extra_block(layer, e, j):
                def link(ins):
                    ins.then_inc(e_dve, 1)
                    dve.reg_add(steps, steps, 1)
                    dve.wait_ge(e_dve, steps)
                late = cst[:, bass.ds(j * C + IOTA, C)]
                for t in range(NT):
                    link(dve.tensor_scalar(pick[0][:, t, :], late, slot[:, t, bass.ds(e, 1)], None, ALU.is_equal))
                for t in range(NT):
                    ins = dve.tensor_scalar(pw[:, t, 0:C], late, slot[:, t, bass.ds(e, 1)], wgt[:, t, bass.ds(e, 1)],
                                            ALU.is_equal, ALU.mult)
                    if t == 0:
                        link(ins)
                ins.then_inc(e_picked, 1)
                dve.wait_ge(e_gathered, blocks)
                g3 = ps[:, 0, :].rearrange("p (k s) -> p k s", s=C)
                link(dve.tensor_tensor(xg[0][:, :, :], g3, colm[:, layer, 2].unsqueeze(2).to_broadcast([P, KD, C]),
                                       ALU.mult))
                link(dve.tensor_tensor(xg[0][:, :, :], xg[0][:, :, :],
                                       colm[:, layer, 3].unsqueeze(2).to_broadcast([P, KD, C]), ALU.add))
                dve.tensor_copy(pwT[0:C, :], ps[0:C, 7, 0:S]).then_inc(e_xg, 1)
                dve.wait_ge(e_exped, blocks)
                link(dve.tensor_scalar(sg[0][:, :], eg[0][:, :], 1.0, None, ALU.add))
                link(dve.reciprocal(eg[0][:, :], sg[0][:, :]))
                link(dve.tensor_tensor(sg[0][:, :], ps[:, 1, 0:KF * C], eg[0][:, :], ALU.mult))
                dve.tensor_tensor(aT[0][:, :, :].rearrange("p k s -> p (k s)"), ps[:, 1, KF * C:2 * KF * C], sg[0][:, :],
                                  ALU.mult).then_inc(e_a, 1)
                dve.wait_ge(e_scattered, blocks)
                for n in range(4):
                    t, h = n // 2, n % 2
                    y = yacc[:, t, 512 * h:512 * h + 512]
                    ins = dve.tensor_tensor(y, y, ps[:, (5, 6, 1, 2)[n], :], ALU.add)
                    if n < 3:
                        link(ins)
                ins.then_inc(e_added, 1)
                dve.reg_add(blocks, blocks, 1)

            def ffn_out(layer):
                dve.wait_ge(scatter_free, 2 * (layer + 1) + 4 * PAIRS * (layer + 1))
                dve.wait_ge(e_added, blocks)
                for t in range(NT):
                    own(dve.tensor_tensor(yacc[:, t], yacc[:, t], gate_b[:, :], ALU.mult))
                    ins = dve.tensor_tensor(xs[:, t], xs[:, t], yacc[:, t], ALU.add)
                    if t == NT - 1:
                        sign(ins, x_updated, 2 * layer + 2)
                    else:
                        own(ins)

            def ffn(layer):
                norm_and_modulate(2 * layer + 1)
                route(layer)
                experts(layer)
                extra_blocks(dve, layer, extra_block)
                ffn_out(layer)

            for k in range(KD):
                ada(0, 0, k)
            norm_and_modulate(0)
            project(RUNS[0, 0][0])
            side = {s: [lambda k=s: ada(0, 1, k)] for s in range(8)}
            side[10] = [lambda: mod(0, 1)]
            side.update({s: [lambda k=s - 11: ada(0, 2, k)] for s in range(11, 16)})
            heads(RUNS[0, 0][1], side)
            for k in range(5, 8):
                ada(0, 2, k)
            mix_out(0)
            ffn(0)
            for k in range(KD):
                ada(1, 0, k)
            norm_and_modulate(2)
            for g in range(B_GRPS):
                project(RUNS[1, g][0])
                heads(RUNS[1, g][1], {s: [lambda k=s, g=g: ada(1, g + 1, k)] for s in range(8)} if g < 2 else {})
                if g == 0:
                    mod(1, 1)

            def grp(v, g):
                return v[:, g * B_HEADS:(g + 1) * B_HEADS, :]
            least, z = aw[:, 1, 0:B_HEADS], aw[:, 1, B_HEADS:2 * B_HEADS]
            own(dve.tensor_tensor(z, grp(nm, 0), grp(nm, 1), ALU.min))
            own(dve.tensor_tensor(least, z, grp(nm, 2), ALU.min))
            for g in range(B_GRPS):
                ins = dve.tensor_tensor(grp(aw[:, 0], g), grp(nm, g), least, ALU.subtract)
                if g < 2:
                    own(ins)
            sign(ins, merge_in, 1)
            dve.wait_ge(merge_exped, 1)
            own(dve.tensor_tensor(aw[:, 2], aw[:, 0], den[:, :, :], ALU.mult))
            own(dve.tensor_tensor(z, grp(aw[:, 2], 0), grp(aw[:, 2], 1), ALU.add))
            own(dve.tensor_tensor(least, z, grp(aw[:, 2], 2), ALU.add))
            own(dve.reciprocal(z, least))
            for g in range(B_GRPS):
                own(dve.tensor_tensor(grp(aw[:, 2], g), grp(aw[:, 0], g), z, ALU.mult))
            dve.wait_ge(o_copied, len(HEADS))
            for g in range(B_GRPS):
                for t in range(NT):
                    o = oB[:, g, t].rearrange("p (h d) -> p h d", d=HD)
                    own(dve.tensor_tensor(o, o, grp(aw[:, 2], g)[:, :, t:t + 1].to_broadcast([P, B_HEADS, HD]), ALU.mult))
            own(dve.tensor_tensor(oB[:, 0], oB[:, 0], oB[:, 1], ALU.add))
            dve.tensor_tensor(oB[:, 0], oB[:, 0], oB[:, 2], ALU.add).then_inc(o_ready, 1)

            mix_out(1)
            ffn(1)
            norm(4)
            dve.wait_ge(s_bias, 80)
            for t in range(NT):
                ins = dve.scalar_tensor_tensor(yacc[:, t], xs[:, t], rstd[:, t:t + 1], gate_b[:, :], ALU.mult, ALU.mult)
                if t == 0:
                    own(ins)
            ins.then_inc(x_updated, 1)

        @block.tensor
        def _(pe):
            def mod(layer, part):
                n = PIECES[layer, part]
                pe.wait_ge(ada_read, 12 * layer + 4 * part + 4)
                for piece in range(1 if part == 0 else 3):
                    if n + piece >= 2:
                        pe.wait_ge(mod_read, n + piece - 1)
                    b = ps[:, 6 + (n + piece) % 2, :]
                    if piece == 0:
                        at = {0: 0, 1: D, 2: 0}[part]
                        for j in range(2 if part == 0 else 1):
                            v = acc[:, at + D * j:at + D * j + D].rearrange("p (n k) -> p n k", k=KD)
                            for k in range(KD):
                                ins = pe.matmul(b[:, KD * j + k:KD * j + k + 1], v[:, :, k], ones[:, 0:1],
                                                start=True, stop=True)
                    else:
                        at = {1: 0, 2: D}[part] + 512 * (piece - 1)
                        ins = pe.matmul(b, ones, acc[:, at:at + 512], start=True, stop=True)
                    ins.then_inc(mod_out, 1)

            def turn_xn(n):
                for b in range(4):
                    if b == 0:
                        pe.wait_ge(xn_ready, 2 * n + 2)
                    for k in (2 * b, 2 * b + 1):
                        for t in range(NT):
                            ins = pe.transpose(ps[:, b, (k % 2) * S + t * P:(k % 2) * S + (t + 1) * P], xn[:, t, k, :], ident)
                    ins.then_inc(xn_turned, 1)

            def project(units):
                def turn(u):
                    if UNITS[u][3] == "v":
                        return
                    r = ropes_before(u)
                    pe.wait_ge(roped, r + 1)
                    if r >= 2:
                        pe.wait_ge(qk_copied, r - 1)
                    for m in range(4):
                        ins = pe.transpose(ps[:, r % 2, m * P:(m + 1) * P], roped_sb[r % 2][:, m * P:(m + 1) * P], ident)
                    ins.then_inc(qk_turned, 1)

                for u in units:
                    layer, chunk, t, kind = UNITS[u]
                    name = ("qkv", layer, chunk)
                    if t == 0:
                        arrived(pe, name)
                    if u >= 2:
                        pe.wait_ge(rope_read, ropes_before(u - 1))
                        if v_copies_before(u - 1):
                            pe.wait_ge(v_copied, v_copies_before(u - 1))
                    w = as_chunks(slot_of(name), 512)
                    for k in range(KD):
                        ins = pe.matmul(ps[:, 6 + u % 2, :], hT[:, k, t * P:(t + 1) * P], w[:, k, :], start=k == 0,
                                        stop=k == KD - 1)
                    ins.then_inc(projected, 1)
                    if u > units[0]:
                        turn(u - 1)
                turn(units[-1])
                pe.wait_ge(qk_copied, ropes_before(units[-1] + 1))
                pe.wait_ge(v_copied, v_copies_before(units[-1] + 1))

            def score(s):
                layer, group, h, narrow = HEADS[s]
                rows = slice(HD * (h % 2), HD * (h % 2) + HD)
                kc = h // 4 if layer == 0 else h // 2
                if s >= 2:
                    pe.wait_ge(masked, s - 1)
                for t in range(NT):
                    q = qT[rows, h // 2, t * P:(t + 1) * P]
                    if narrow:
                        ins = pe.matmul(ps[:, s % 2, t * P:(t + 1) * P], q, kT[rows, kc, t * P:(t + 1) * P], start=True, stop=True)
                    else:
                        ins = pe.matmul(ps[:, s % 2, t * S:(t + 1) * S], q, kT[rows, kc, :], start=True, stop=True)
                ins.then_inc(scored, 1)

            def turn_p(s):
                narrow = HEADS[s][3]
                pe.wait_ge(exped, 2 * s + 2)
                if s >= 2:
                    pe.wait_ge(pT_copied, s - 1)
                for t in range(NT):
                    for kt in range(1 if narrow else NT):
                        src = pr[s % 2][:, t * P:(t + 1) * P] if narrow else pr[s % 2][:, t * S + kt * P:t * S + (kt + 1) * P]
                        ins = pe.transpose(ps[:, 2 + s % 2, kt * S + t * P:kt * S + (t + 1) * P], src, ident)
                ins.then_inc(p_turned, 1)

            def p_times_v(s):
                layer, group, h, narrow = HEADS[s]
                vc = HD * (h // 4 if layer == 0 else h)
                pe.wait_ge(pT_copied, s + 1)
                if s >= 2:
                    pe.wait_ge(o_copied, s - 1)
                for t in range(NT):
                    o = ps[:, 4 + s % 2, t * HD:(t + 1) * HD]
                    if narrow:
                        ins = pe.matmul(o, pT[s % 2][:, t * P:(t + 1) * P], vv[:, t, vc:vc + HD], start=True, stop=True)
                    else:
                        for kt in range(NT):
                            ins = pe.matmul(o, pT[s % 2][:, kt * S + t * P:kt * S + (t + 1) * P], vv[:, kt, vc:vc + HD],
                                            start=kt == 0, stop=kt == NT - 1)
                ins.then_inc(pv_done, 1)

            def heads(steps, side):
                for s in steps:
                    score(s)
                    if s >= steps[0] + 1:
                        turn_p(s - 1)
                    if s >= steps[0] + 2:
                        p_times_v(s - 2)
                    if s - steps[0] in side:
                        side[s - steps[0]]()
                turn_p(steps[-1])
                p_times_v(steps[-2])
                p_times_v(steps[-1])

            def mix_out(layer):
                n_ch = (8, 4)[layer]
                o = oA if layer == 0 else oB[:, 0]
                if layer == 0:
                    pe.wait_ge(o_copied, A_HEADS)
                else:
                    pe.wait_ge(o_ready, 1)
                for b in range(n_ch // 2):
                    for ch in (2 * b, 2 * b + 1):
                        for t in range(NT):
                            ins = pe.transpose(ps[:, b, (ch % 2) * S + t * P:(ch % 2) * S + (t + 1) * P],
                                               o[:, t, P * ch:P * ch + P], ident)
                    ins.then_inc(o_turned, 1)
                pe.wait_ge(oT_dve, (2, 3)[layer])
                pe.wait_ge(oT_act, (2, 3)[layer])
                for n in range(4):
                    t, h = n // 2, n % 2
                    for ch in range(n_ch):
                        name = ("wo", layer, ch // 4)
                        if n == 0 and ch % 4 == 0:
                            arrived(pe, name)
                        ins = pe.matmul(ps[:, 4 + n, :], oT[:, ch, t * P:(t + 1) * P],
                                        as_chunks(slot_of(name), D)[:, ch % 4, 512 * h:512 * h + 512],
                                        start=ch == 0, stop=ch == n_ch - 1)
                    ins.then_inc(mixed, 1)

            def route(layer):
                pe.wait_ge(hT_dve, 8 * layer + 8)
                pe.wait_ge(hT_act, 8 * layer + 8)
                for t in range(NT):
                    for k in range(KD):
                        ins = pe.matmul(ps[:, 4, t * E:(t + 1) * E], hT[:, k, t * P:(t + 1) * P], rw[:, k, :], start=k == 0,
                                        stop=k == KD - 1)
                ins.then_inc(logits, 1)
                pe.wait_ge(routed, layer + 1)
                r = ps[:, 5, :]
                pe.matmul(r[:, 0:E], tri, sel[:, 0, :], start=True, stop=True)
                pe.matmul(r[:, E:2 * E], ones, sel[:, 0, :], start=True, stop=False)
                pe.matmul(r[:, E:2 * E], tri, sel[:, 1, :], start=False, stop=True)
                pe.matmul(r[:, 2 * E:3 * E], ones, sel[:, 0, :], start=True, stop=False)
                pe.matmul(r[:, 2 * E:3 * E], ones, sel[:, 1, :], start=False, stop=True).then_inc(ranked, 1)

            def gather(buf):
                for k in range(KD):
                    for t in range(NT):
                        ins = pe.matmul(ps[:, 0, k * C:(k + 1) * C], xn[:, t, k, :], pick[buf][:, t, :], start=t == 0,
                                        stop=t == NT - 1)
                return ins

            def widen(w, src, bank, col):
                for f in range(KF):
                    for k in range(KD):
                        ins = pe.matmul(bank[:, col + f * C:col + (f + 1) * C], w[:, k, f * P:(f + 1) * P], src[:, k, :],
                                        start=k == 0, stop=k == KD - 1)
                return ins

            def narrow_down(w, src, rows):
                for h in range(2):
                    for f in range(KF):
                        ins = pe.matmul(ps[rows, 3 + h, :], src[:, f, :], w[:, f, 512 * h:512 * h + 512], start=f == 0,
                                        stop=f == KF - 1)
                return ins

            def experts(layer):
                base = LOAD[("moe", layer, 0)]
                q0, g0 = PAIRS * layer, GATHERS * layer
                pe.wait_ge(picked, 2 * g0 + 2)
                gather(0).then_inc(gathered, 1)
                with pe.Fori(0, PAIRS) as i:
                    def weights(j):
                        n = base + j
                        pe.wait_ge(landed[n % RING], i * 16 + 16 * (n // RING + 1))
                        return as_chunks(ring[n % RING], D if j % 3 == 2 else F)

                    gate_w = weights(0)
                    pe.wait_ge(xg_ready, i * 2 + (g0 + 1))
                    widen(gate_w, xg[0], ps[:, 1, :], 0).then_inc(gate_done, 1)
                    pe.wait_ge(picked, i * 4 + (2 * g0 + 4))
                    gather(1).then_inc(gathered, 1)
                    up_w = weights(1)
                    widen(up_w, xg[0], ps[:, 1, :], KF * C).then_inc(up_done, 1)
                    pe.wait_ge(pw_ready, i + (q0 + 1))
                    for t in range(NT):
                        ins = pe.transpose(ps[:, 7, t * P:(t + 1) * P], pw[:, t, :], ident)
                    ins.then_inc(pw_turned, 1)
                    gate_w = weights(3)
                    pe.wait_ge(xg_ready, i * 2 + (g0 + 2))
                    widen(gate_w, xg[1], ps[:, 2, :], 0).then_inc(gate_done, 1)
                    up_w = weights(4)
                    widen(up_w, xg[1], ps[:, 2, :], KF * C).then_inc(up_done, 1)
                    for b in range(2):
                        down_w = weights(2 + 3 * b)
                        pe.wait_ge(a_ready, i * 2 + (2 * q0 + b + 1))
                        narrow_down(down_w, aT[b], slice(C * b, C * b + C)).then_inc(down_done, 1)
                    pe.wait_ge(picked, i * 4 + (2 * g0 + 6))
                    gather(0).then_inc(gathered, 1)
                    pe.wait_ge(pwT_ready, i + (q0 + 1))
                    pe.wait_ge(y_copied, i * 4 + (4 * q0 + 4))
                    for n in range(4):
                        t, h = n // 2, n % 2
                        pe.wait_ge(scatter_free, i * 4 + (4 * q0 + n + 2 * layer + 1))
                        pe.matmul(ps[:, 5 + n % 2, :], pwT[:, t * P:(t + 1) * P], ye[:, 512 * h:512 * h + 512],
                                  start=True, stop=True).then_inc(scattered, 1)

            blocks = pe.alloc_register("pe_blocks")
            landings = pe.alloc_register("pe_landings")
            pe.reg_mov(blocks, 1)
            pe.reg_mov(landings, 48)

            def extra_block(layer, e, j):
                pe.wait_ge(e_picked, blocks)
                gather(0)
                for t in range(NT):
                    ins = pe.transpose(ps[0:C, 7, t * P:(t + 1) * P], pw[:, t, 0:C], ident)
                ins.then_inc(e_gathered, 1)
                pe.wait_ge(e_landed, landings)
                pe.wait_ge(e_xg, blocks)
                widen(as_chunks(x_gate, F), xg[0], ps[:, 1, :], 0)
                widen(as_chunks(x_up, F), xg[0], ps[:, 1, :], KF * C).then_inc(e_up, 1)
                pe.wait_ge(e_a, blocks)
                narrow_down(as_chunks(x_down, D), aT[0], slice(0, C)).then_inc(e_down, 1)
                pe.wait_ge(e_y, blocks)
                for n in range(4):
                    t, h = n // 2, n % 2
                    ins = pe.matmul(ps[:, (5, 6, 1, 2)[n], :], pwT[0:C, t * P:(t + 1) * P], ye[0:C, 512 * h:512 * h + 512],
                                    start=True, stop=True)
                ins.then_inc(e_scattered, 1)
                pe.reg_add(blocks, blocks, 1)
                pe.reg_add(landings, landings, 48)

            pe.wait_ge(s_const, 80)
            mod(0, 0)
            turn_xn(0)
            pe.wait_ge(hT_dve, 4)
            pe.wait_ge(hT_act, 4)
            pe.wait_ge(mod_read, PIECES[0, 0] + 1)
            project(RUNS[0, 0][0])
            heads(RUNS[0, 0][1], {10: lambda: mod(0, 1)})
            mix_out(0)
            pe.wait_ge(x_updated, 1)
            mod(0, 2)
            turn_xn(1)
            route(0)
            experts(0)
            extra_blocks(pe, 0, extra_block)
            mod(1, 0)
            turn_xn(2)
            pe.wait_ge(hT_dve, 12)
            pe.wait_ge(hT_act, 12)
            for g in range(B_GRPS):
                if g == 1:
                    mod(1, 1)
                    pe.wait_ge(mod_read, PIECES[1, 1] + 3)
                project(RUNS[1, g][0])
                heads(RUNS[1, g][1], {})
            mix_out(1)
            pe.wait_ge(x_updated, 3)
            mod(1, 2)
            turn_xn(3)
            route(1)
            experts(1)
            extra_blocks(pe, 1, extra_block)


INPUTS = ["x", "c", "positions", "ada_w", "ada_b", "norm_mix_g", "norm_ffn_g", "a_w_qkv", "a_w_o", "a_sink",
          "b_w_qkv", "b_w_o", "router_w", "router_bias", "exp_w_gate", "exp_w_up", "exp_w_down", "final_norm_g"]


def kernel(**inputs):
    import concourse.bacc as bacc
    from concourse.bass_utils import run_bass_kernel_spmd

    nc = bacc.Bacc("TRN2", target_bir_lowering=False, num_devices=1)
    arrays = {name: np.ascontiguousarray(inputs[name]) for name in INPUTS}
    arrays["const"] = constants()
    arrays["mask"] = masks()
    args = [nc.dram_tensor(name, a.shape, mybir.dt.from_np(a.dtype), kind="ExternalInput").ap()
            for name, a in arrays.items()]
    args.append(nc.dram_tensor("out", (1, S, D), F32, kind="ExternalOutput").ap())
    build(nc, *args)
    result = run_bass_kernel_spmd(nc, [arrays], core_ids=[0])
    return result.results[0]["out"]
```

```python
from contextlib import ExitStack

import numpy as np

import concourse.bass as bass
from concourse import mybir

ALU = mybir.AluOpType
ACT = mybir.ActivationFunctionType
F32 = mybir.dt.float32
I32 = mybir.dt.int32
AX_X = mybir.AxisListType.X

P = 128
S, D = 256, 1024
NT = S // P
KD = D // P
HD = 64
HALF = HD // 2
A_HEADS, A_KV = 16, 4
B_HEADS, B_GRPS = 8, 3
E, GRP = 16, 4
F = 512
KF = F // P
C = 64
PAIRS = E // 2
TOP_K = 2
X_BLOCKS = S * TOP_K // C - 1
RING = 6
SLOT = 4096
EPS = 1e-6
SCALE = float(HD) ** -0.5
TWO_PI_HI = 6.28125
TWO_PI_MID = float(np.float32(2 * np.pi - TWO_PI_HI).view(np.uint32) & 0xFFFFF000)
TWO_PI_MID = float(np.uint32(int(TWO_PI_MID)).view(np.float32))
TWO_PI_LO = float(2 * np.pi - TWO_PI_HI - TWO_PI_MID)
ROUND = 1.5 * 2.0 ** 23
PI_SAFE = 3.1415925

IDENT, ONES, TRI, IOTA, INVF = 0, P, 2 * P, 3 * P, 3 * P + S
N_CONST = INVF + HALF


def token_of_row():
    t = np.arange(S).reshape(S // 16, 4, 4)
    return t.transpose(2, 1, 0).reshape(S)


def constants():
    c = np.zeros((P, N_CONST), np.float32)
    c[:, IDENT:IDENT + P] = np.eye(P)
    c[:, ONES:ONES + P] = 1.0
    c[:, TRI:TRI + P] = np.triu(np.ones((P, P)), 1)
    c[:, IOTA:IOTA + S] = np.arange(S)
    c[:, INVF:] = (10000.0 ** (-np.arange(0, HD, 2) / HD)).astype(np.float32)
    return c


def masks():
    t = token_of_row()
    gap = np.abs(t[:, None] - t[None, :])
    own = np.stack([gap[:P, :P], gap[P:, P:]], 1)
    full = np.stack([gap[:P], gap[P:]], 1)
    parts = [full <= 128, full <= 64, (own % 4 == 0) & (own <= 64 * 4), (own % 16 == 0) & (own <= 64 * 16)]
    m = np.concatenate([p.reshape(P, -1) for p in parts], 1)
    return np.where(m, 0.0, -1e30).astype(np.float32)


M_A, M_B0, M_B1, M_B2, N_MASK = 0, 512, 1024, 1280, 1536


def plan_loads():
    order = [("ada", 0, 0, j) for j in range(4)]
    order += [("qkv", 0, j) for j in range(3)]
    order += [("ada", 0, 1, j) for j in range(4)] + [("ada", 0, 2, j) for j in range(4)]
    order += [("wo", 0, j) for j in range(2)] + [("ada", 1, 0, j) for j in range(4)]
    order += [("moe", 0, j) for j in range(3 * E)]
    order += [("qkv", 1, j) for j in range(3)] + [("ada", 1, 1, j) for j in range(4)]
    order += [("qkv", 1, j) for j in range(3, 6)] + [("ada", 1, 2, j) for j in range(4)]
    order += [("qkv", 1, j) for j in range(6, 9)] + [("wo", 1, 0)]
    order += [("moe", 1, j) for j in range(3 * E)]
    return order


ORDER = plan_loads()
LOAD = {name: n for n, name in enumerate(ORDER)}


def plan_units():
    units = [(0, c, t, "kv" if c == 2 else "q") for c in range(3) for t in range(NT)]
    units += [(1, c, t, "qkv"[c % 3]) for c in range(9) for t in range(NT)]
    return units


UNITS = plan_units()


def plan_heads():
    return [(0, 0, h, False) for h in range(A_HEADS)] + \
           [(1, g, h, g > 0) for g in range(B_GRPS) for h in range(B_HEADS)]


HEADS = plan_heads()
RUNS = {(0, 0): (range(0, 6), range(0, 16)),
        (1, 0): (range(6, 12), range(16, 24)),
        (1, 1): (range(12, 18), range(24, 32)),
        (1, 2): (range(18, 24), range(32, 40))}
RUNS_BEFORE = {6: 16, 12: 24, 18: 32}
PIECES = {(layer, part): 7 * layer + (0, 1, 4)[part] for layer in range(2) for part in range(3)}
GATHERS = PAIRS + 1


def ropes_before(u):
    return sum(k != "v" for _, _, _, k in UNITS[:u])


def v_copies_before(u):
    return sum("v" in k for _, _, _, k in UNITS[:u])


class Own:

    def __init__(self, eng, sem):
        self.eng, self.sem, self.n, self.turn = eng, sem, 0, 0

    def __call__(self, ins):
        self.n += 1
        ins.then_inc(self.sem, 1)
        self.eng.wait_ge(self.sem, self.turn + self.n)


def build(nc, x, c, positions, ada_w, ada_b, norm_mix_g, norm_ffn_g, a_w_qkv, a_w_o, a_sink, b_w_qkv,
          b_w_o, router_w, router_bias, exp_w_gate, exp_w_up, exp_w_down, final_norm_g, const, mask, out):
    ctx = ExitStack()
    with ctx:
        def sb(name, shape, dt=F32):
            return ctx.enter_context(nc.sbuf_tensor(name, shape, dt))

        def sem(name):
            return ctx.enter_context(nc.semaphore(name))

        ring = [sb(f"ring{s}", [P, SLOT]) for s in range(RING)]
        shared = sb("shared", [P, 3 * SLOT])
        xs = sb("xs", [P, NT, D])
        xn = sb("xn", [P, NT, KD, P])
        hT = sb("hT", [P, KD, S])
        acc = sb("acc", [P, 2048])
        gate_b = sb("gate_b", [P, D])
        cst = sb("cst", [P, N_CONST])
        cos2 = sb("cos2", [P, NT, HD])
        sin2 = sb("sin2", [P, NT, HD])
        yxg = sb("yxg", [P, 2 * D])
        ye = yxg[:, 0:D]
        xg = yxg[:, D:2 * D].rearrange("p (k s) -> p k s", s=P)
        acc_b = yxg[:, :]
        eg = sb("eg", [P, F])
        sg = sb("sg", [P, F])
        aT = sb("aT", [P, KF, P])
        pick = sb("pick", [P, NT, P])
        pw = sb("pw", [P, NT, P])
        pwT = sb("pwT", [P, S])
        x_xg = sb("x_xg", [P, KD, C])
        x_pwT = sb("x_pwT", [P, S])
        x_ye = sb("x_ye", [P, 512])
        colm = sb("colm", [P, 2, 4, KD])
        colb = sb("colb", [P, 2, 6, KD])
        colg = sb("colg", [P, 2, 2, KD])
        colt = sb("colt", [P, KD])
        cc = sb("cc", [P, KD])
        sc = sb("sc", [P, KD])
        rw = sb("rw", [P, KD, E])
        rbias = sb("rbias", [P, E])
        sink = sb("sink", [P, A_HEADS])
        posi = sb("posi", [P, NT], I32)
        posf = sb("posf", [P, NT])
        ss = sb("ss", [P, NT])
        std = sb("std", [P, NT])
        rstd = sb("rstd", [P, NT])
        sel = sb("sel", [P, NT, E])
        wgt = sb("wgt", [P, NT, E + 2])
        slot = sb("slot", [P, NT, E + 2])
        blk = sb("blk", [P, 2, 2 * X_BLOCKS + 1], I32)
        ps = ctx.enter_context(nc.psum_tensor("ps", [P, 8, 512], F32))

        ident = cst[:, IDENT:IDENT + P]
        ones = cst[:, ONES:ONES + P]
        tri = cst[:, TRI:TRI + P]

        def area(at, n):
            return shared[:, at:at + n]
        qT = area(0, 2048).rearrange("p (c t) -> p c t", t=S)
        kT = area(2048, 1024).rearrange("p (c t) -> p c t", t=S)
        vv = area(3072, 1024).rearrange("p (t n) -> p t n", t=NT)
        pT = [area(6144 + 512 * b, 512) for b in range(2)]
        o_all = area(7168, 3072)
        msk = area(10240, N_MASK)
        STEPS = B_GRPS * B_HEADS
        nm = area(11776, STEPS * NT).rearrange("p (s t) -> p s t", t=NT)
        den = area(11824, STEPS * NT).rearrange("p (s t) -> p s t", t=NT)
        esk = area(11872, A_HEADS * NT).rearrange("p (s t) -> p s t", t=NT)
        mx = area(11904, NT)
        aw = area(11906, 3 * STEPS * NT).rearrange("p (j s t) -> p j s t", j=3, t=NT)
        rt = area(0, 320).rearrange("p (j n) -> p j n", j=10)
        rr = area(320, 128).rearrange("p (j n) -> p j n", j=4)
        xb = area(448, 144).rearrange("p (j n) -> p j n", j=6)
        xcmp = area(592, 2 * X_BLOCKS * E).rearrange("p (j n) -> p j n", j=2)
        xsum = area(816, 4 * X_BLOCKS).rearrange("p (j n) -> p j n", j=4)
        slot_raw = area(848, NT * E).rearrange("p (t e) -> p t e", e=E)
        oA = o_all[:, 0:2048].rearrange("p (t n) -> p t n", t=NT)
        oB = o_all.rearrange("p (g t n) -> p g t n", g=B_GRPS, t=NT)
        xnf = xn[:, :, :, :].rearrange("p t k n -> p (t k n)")
        rope1, rope2 = xnf[:, 0:512], xnf[:, 512:1024]
        sm = [area(4096, 512), area(4608, 512), rope1]
        pr = [area(5120, 512), area(5632, 512), rope2]
        roped_sb = [xnf[:, 1024 + 512 * b:1536 + 512 * b] for b in range(2)]
        oT = hT
        yacc = hT[:, :, :].rearrange("p k s -> p (k s)").rearrange("p (t n) -> p t n", t=NT)
        junk = yacc
        x_gate, x_up, x_down = (area(SLOT * j, SLOT) for j in range(3))
        ang, turns = xnf[:, 0:64], xnf[:, 64:128]
        ct = xnf[:, 320:336].rearrange("p (j k) -> p j k", j=2)

        landed = [sem(f"landed{s}") for s in range(RING)]
        s_const, s_x, s_c, s_misc, s_bias, s_out = (sem(n) for n in (
            "const_landed", "x_landed", "c_landed", "misc_landed", "gate_bias_landed", "out_stored"))
        s_mask = sem("mask_landed")
        dve_step, act_step = sem("dve_step"), sem("act_step")
        c_exp, c_silu, angles, tables = sem("c_exp"), sem("c_silu"), sem("angles"), sem("rope_tables")
        ada_summed, ada_read = sem("ada_summed"), sem("ada_read")
        mod_out, mod_read = sem("mod_out"), sem("mod_read")
        squared, var_ready, std_ready = sem("squared"), sem("var_ready"), sem("std_ready")
        xn_ready, xn_turned = sem("xn_ready"), sem("xn_turned")
        hT_dve, hT_act = sem("hT_dve"), sem("hT_act")
        projected, rope_read, roped = sem("projected"), sem("rope_read"), sem("roped")
        v_copied, qk_turned, qk_copied = sem("v_copied"), sem("qk_turned"), sem("qk_copied")
        scored, masked, negmax, exped = sem("scored"), sem("masked"), sem("negmax"), sem("exped")
        sink_exped, p_turned, pT_copied = sem("sink_exped"), sem("p_turned"), sem("pT_copied")
        pv_done, o_copied = sem("pv_done"), sem("o_copied")
        merge_in, merge_exped, o_ready = sem("merge_in"), sem("merge_exped"), sem("o_ready")
        o_turned, oT_dve, oT_act = sem("o_turned"), sem("oT_dve"), sem("oT_act")
        mixed, x_updated = sem("mixed"), sem("x_updated")
        logits, logits_exped, routed = sem("logits"), sem("logits_exped"), sem("routed")
        ranked, counted = sem("ranked"), sem("counted")
        picked, pw_ready, pw_turned, pwT_ready = sem("picked"), sem("pw_ready"), sem("pw_turned"), sem("pwT_ready")
        gathered, xg_ready = sem("gathered"), sem("xg_ready")
        gate_done, up_done, gate_exped, a_ready = sem("gate_done"), sem("up_done"), sem("gate_exped"), sem("a_ready")
        down_done, y_copied = sem("down_done"), sem("y_copied")
        a_turned, aT_ready, e_turned, e_aT = sem("a_turned"), sem("aT_ready"), sem("e_turned"), sem("e_aT")
        scattered, scatter_free = sem("scattered"), sem("scatter_free")
        e_landed, e_picked, e_gathered, e_xg = sem("e_landed"), sem("e_picked"), sem("e_gathered"), sem("e_xg")
        e_up, e_exped, e_a, e_down, e_y = sem("e_up"), sem("e_exped"), sem("e_a"), sem("e_down"), sem("e_y")
        e_scattered, e_added, e_dve = sem("e_scattered"), sem("e_added"), sem("e_dve")

        def slot_of(name):
            return ring[LOAD[name] % RING]

        def arrived(eng, name):
            n = LOAD[name]
            eng.wait_ge(landed[n % RING], 16 * (n // RING + 1))

        def last_use(name):
            kind, layer = name[0], name[1]
            if kind == "ada":
                return ada_read, 12 * layer + 4 * name[2] + name[3] + 1
            if kind == "qkv":
                return projected, 6 * layer + 2 * name[2] + 2
            if kind == "wo":
                return mixed, 4 * layer + 4
            return (gate_done, up_done, down_done)[name[2] % 6 // 2], PAIRS * layer + name[2] // 6 + 1

        def source(name):
            kind, layer = name[0], name[1]
            if kind == "ada":
                part, j = name[2], name[3]
                return ada_w[layer].rearrange("(p k) n -> p k n", k=KD)[:, 2 * j:2 * j + 2,
                                                                     2048 * part:2048 * part + 2048]
            if kind == "qkv":
                w = (a_w_qkv, b_w_qkv)[layer][0].rearrange("(p k) n -> p k n", k=KD)
                at = 512 * name[2]
                if layer == 1:
                    at = 1536 * (name[2] // 3) + 512 * (name[2] % 3)
                return w[:, :, at:at + 512]
            w = (a_w_o, b_w_o)[layer][0].rearrange("(c p) n -> p c n", p=P)
            return w[:, 4 * name[2]:4 * name[2] + 4, :]

        def expert_source(layer, e, part):
            w = (exp_w_gate, exp_w_up, exp_w_down)[part][layer][bass.ds(e, 1)]
            if part == 2:
                return w.rearrange("e (c p) n -> p (e c) n", p=P)
            return w.rearrange("e (p k) f -> p (e k) f", k=KD)

        def as_chunks(t, n):
            return t[:, :].rearrange("p (k n) -> p k n", n=n)

        def rows_of(dram, q):
            return dram.rearrange("(a b c) d -> c b a d", a=S // 16, b=4, c=4)[q]

        def extra_block_count(eng, layer):
            eng.wait_ge(counted, layer + 1)
            return eng.value_load(blk[0:1, layer, 2 * X_BLOCKS:2 * X_BLOCKS + 1], min_val=0, max_val=X_BLOCKS)

        block = ctx.enter_context(nc.Block())

        @block.sync
        def _(sp):
            def load(name):
                n = LOAD[name]
                if n >= RING:
                    sp.wait_ge(*last_use(ORDER[n - RING]))
                t = slot_of(name)
                width = {"ada": 2048, "qkv": 512, "wo": D}[name[0]]
                sp.dma_start(as_chunks(t, width), source(name)).then_inc(landed[n % RING], 16)

            def load_experts(layer):
                base = LOAD[("moe", layer, 0)]

                def one_pair(i, first):
                    for j in range(6):
                        n = base + j
                        if first:
                            sp.wait_ge(*last_use(ORDER[n - RING]))
                        else:
                            done, value = last_use(ORDER[n])
                            sp.wait_ge(done, i + (value - 1))
                        sp.dma_start(as_chunks(ring[n % RING], D if j // 2 == 2 else F),
                                     expert_source(layer, i * 2 + j % 2, j // 2))\
                          .then_inc(landed[n % RING], 16)
                one_pair(0, True)
                with sp.Fori(1, PAIRS) as i:
                    one_pair(i, False)

            sp.dma_start(cc[:, :], c[0].rearrange("(p k) -> p k", k=KD)).then_inc(s_c, 16)
            for q in range(4):
                sp.dma_start(xs[64 * (q % 2):64 * (q % 2) + 64, q // 2, :], rows_of(x[0], q)).then_inc(s_x, 16)
            sp.dma_start(cst[:, :], const).then_inc(s_const, 16)
            for n in range(LOAD[("moe", 0, 0)]):
                load(ORDER[n])
            load_experts(0)
            for n in range(LOAD[("qkv", 1, 0)], LOAD[("moe", 1, 0)]):
                load(ORDER[n])
            load_experts(1)
            sp.wait_ge(x_updated, 5)
            for q in range(4):
                sp.dma_start(rows_of(out[0], q), yacc[64 * (q % 2):64 * (q % 2) + 64, q // 2, :])\
                  .then_inc(s_out, 16)
            sp.wait_ge(s_out, 64)

        @block.scalar
        def _(act):
            own = Own(act, act_step)
            pos_rows = positions.rearrange("o (a b c) -> c b a o", a=S // 16, b=4, c=4)
            for q in range(4):
                act.dma_start(posi[64 * (q % 2):64 * (q % 2) + 64, q // 2:q // 2 + 1], pos_rows[q],
                              allow_slow_non_contiguous=True).then_inc(s_const, 16)
            act.dma_start(msk, mask).then_inc(s_mask, 16)
            for layer in range(2):
                act.dma_start(colb[:, layer], ada_b[layer].rearrange("(v p k) -> p v k", v=6, k=KD))\
                   .then_inc(s_misc, 16)
                act.dma_start(colg[:, layer, 0], norm_mix_g[layer].rearrange("(p k) -> p k", k=KD)).then_inc(s_misc, 16)
                act.dma_start(colg[:, layer, 1], norm_ffn_g[layer].rearrange("(p k) -> p k", k=KD)).then_inc(s_misc, 16)
            act.dma_start(rw[:, :, :], router_w.rearrange("(p k) e -> p k e", k=KD)).then_inc(s_misc, 16)
            act.dma_start(rbias[:, :], router_bias.partition_broadcast(P)).then_inc(s_misc, 16)
            act.dma_start(sink[:, :], a_sink[0].partition_broadcast(P)).then_inc(s_misc, 16)

            def gate_bias(layer, vector):
                act.dma_start(gate_b[:, :], ada_b[layer, D * vector:D * vector + D].partition_broadcast(P))\
                   .then_inc(s_bias, 16)
            gate_bias(0, 2)

            act.wait_ge(s_c, 16)
            act.activation(ct[:, 0], cc[:, :], ACT.Exp, scale=-1.0).then_inc(c_exp, 1)
            act.wait_ge(angles, 2)
            for t in range(NT):
                act.activation(cos2[:, t, 0:HALF], ang[:, t * HALF:(t + 1) * HALF], ACT.Sin).then_inc(tables, 1)
                act.activation(cos2[:, t, HALF:HD], ang[:, t * HALF:(t + 1) * HALF], ACT.Sin).then_inc(tables, 1)
                act.activation(sin2[:, t, HALF:HD], turns[:, t * HALF:(t + 1) * HALF], ACT.Sin).then_inc(tables, 1)
                act.activation(sin2[:, t, 0:HALF], turns[:, t * HALF:(t + 1) * HALF], ACT.Sin, scale=-1.0).then_inc(tables, 1)

            def norm(n):
                if n == 0:
                    act.wait_ge(s_x, 64)
                else:
                    act.wait_ge(x_updated, n)
                for t in range(NT):
                    act.activation(junk[:, t], xs[:, t], ACT.Square, accum_out=ss[:, t:t + 1]).then_inc(squared, 1)
                act.wait_ge(var_ready, n + 1)
                act.activation(std[:, :], ss[:, :], ACT.Sqrt).then_inc(std_ready, 1)

            def modulate(n):
                layer, which = n // 2, n % 2
                act.wait_ge(mod_read, PIECES[layer, 0] + 1 if which == 0 else PIECES[layer, 2] + 1)
                for b in (1, 3):
                    act.wait_ge(xn_turned, 4 * n + b + 1)
                    for k in (2 * b, 2 * b + 1):
                        act.activation(hT[:, k, :], ps[:, b, (k % 2) * S:(k % 2 + 1) * S], ACT.Identity,
                                       bias=colm[:, layer, 2 * which + 1, k:k + 1],
                                       scale=colm[:, layer, 2 * which, k:k + 1]).then_inc(hT_act, 1)

            def project(units):
                if units[0] > 0:
                    act.wait_ge(pv_done, RUNS_BEFORE[units[0]])
                for u in units:
                    layer, chunk, t, kind = UNITS[u]
                    if "v" in kind:
                        act.wait_ge(projected, u + 1)
                        if kind == "kv":
                            act.wait_ge(rope_read, ropes_before(u) + 1)
                            src, dst = ps[:, 6 + u % 2, 256:512], vv[:, t, 0:256]
                        else:
                            src, dst = ps[:, 6 + u % 2, :], vv[:, t, :]
                        act.activation(dst, src, ACT.Copy).then_inc(v_copied, 1)
                    if kind != "v":
                        r = ropes_before(u)
                        act.wait_ge(qk_turned, r + 1)
                        if kind == "q":
                            first = 4 * (chunk % 3) if layer == 0 else 0
                            dst = qT[:, first:first + 4, t * P:(t + 1) * P]
                        else:
                            dst = kT[:, :, t * P:(t + 1) * P]
                        act.activation(dst, ps[:, r % 2, :].rearrange("p (c t) -> p c t", t=P), ACT.Copy)\
                           .then_inc(qk_copied, 1)

            def copy_pT(s):
                narrow = HEADS[s][3]
                act.wait_ge(p_turned, s + 1)
                if s >= 2:
                    act.wait_ge(pv_done, s - 1)
                n = S if narrow else 2 * S
                act.activation(pT[s % 2][:, 0:n], ps[:, 3 + s % 2, 0:n], ACT.Copy).then_inc(pT_copied, 1)

            def heads(steps):
                for s in steps:
                    layer, group, h, narrow = HEADS[s]
                    width = P if narrow else S
                    col = group * B_HEADS + h
                    if s >= steps[0] + 2:
                        copy_pT(s - 2)
                    act.wait_ge(negmax, s + 1)
                    if s >= 3:
                        act.wait_ge(p_turned, s - 2)
                    for t in range(NT):
                        act.activation(pr[s % 3][:, t * width:(t + 1) * width], sm[s % 3][:, t * width:(t + 1) * width],
                                       ACT.Exp, bias=nm[:, col, t:t + 1], accum_out=den[:, col, t:t + 1])\
                           .then_inc(exped, 1)
                    if layer == 0:
                        act.activation(esk[:, h, :], nm[:, col, :], ACT.Exp, bias=sink[:, h:h + 1])\
                           .then_inc(sink_exped, 1)
                copy_pT(steps[-2])
                copy_pT(steps[-1])

            def copy_oT(layer):
                for b in (range(4) if layer == 0 else range(2)):
                    if b % 2:
                        act.wait_ge(o_turned, (0, 4)[layer] + b + 1)
                        act.activation(oT[:, 2 * b:2 * b + 2, :], ps[:, b, :].rearrange("p (c t) -> p c t", t=S),
                                       ACT.Copy).then_inc(oT_act, 1)

            def experts(layer):
                act.wait_ge(logits, layer + 1)
                act.activation(rt[:, 0], ps[:, 4, 0:NT * E], ACT.Exp, scale=-1.0).then_inc(logits_exped, 1)
                q0 = PAIRS * layer
                blocks_here = extra_block_count(act, layer)

                def pair(i, first):
                    act.wait_ge(gate_done, i + (q0 + 1))
                    act.activation(eg[:, :], ps[:, 2, :], ACT.Exp, scale=-1.0).then_inc(gate_exped, 1)
                    act.wait_ge(a_turned, i + (q0 + 1))
                    act.activation(aT[:, :, :].rearrange("p f s -> p (f s)"), ps[:, 2, :], ACT.Copy).then_inc(aT_ready, 1)
                    act.wait_ge(down_done, i + (q0 + 1))
                    if not first:
                        act.wait_ge(scattered, i * 4 + 4 * q0)
                    for h in range(2):
                        act.activation(ye[:, 512 * h:512 * h + 512], ps[:, 4 + h, :], ACT.Copy).then_inc(y_copied, 1)
                pair(0, True)
                with act.Fori(1, PAIRS) as i:
                    pair(i, False)
                    with act.If(blocks_here > i - 1):
                        extra_block()

            blocks = act.alloc_register("act_blocks")
            act.reg_mov(blocks, 1)

            def extra_block():
                act.wait_ge(e_up, blocks)
                act.activation(eg[0:C, :], ps[0:C, 2, :], ACT.Exp, scale=-1.0).then_inc(e_exped, 1)
                act.wait_ge(e_turned, blocks)
                act.activation(aT[:, :, 0:C], ps[:, 2, 0:KF * C].rearrange("p (f s) -> p f s", s=C), ACT.Copy)\
                   .then_inc(e_aT, 1)
                act.wait_ge(e_down, blocks)
                act.activation(x_ye[0:C, :], ps[0:C, 4, :], ACT.Copy)
                act.activation(x_ye[C:P, :], ps[C:P, 5, :], ACT.Copy).then_inc(e_y, 1)
                act.reg_add(blocks, blocks, 1)

            norm(0)
            modulate(0)
            project(RUNS[0, 0][0])
            heads(RUNS[0, 0][1])
            copy_oT(0)
            act.wait_ge(x_updated, 1)
            gate_bias(0, 5)
            norm(1)
            modulate(1)
            experts(0)
            act.wait_ge(x_updated, 2)
            gate_bias(1, 2)
            act.dma_start(msk, mask).then_inc(s_mask, 16)
            norm(2)
            modulate(2)
            for g in range(B_GRPS):
                project(RUNS[1, g][0])
                heads(RUNS[1, g][1])
            act.wait_ge(merge_in, 1)
            act.activation(aw[:, 0], aw[:, 0], ACT.Exp, scale=-1.0).then_inc(merge_exped, 1)
            copy_oT(1)
            act.wait_ge(x_updated, 3)
            gate_bias(1, 5)
            norm(3)
            modulate(3)
            experts(1)
            act.wait_ge(x_updated, 4)
            act.dma_start(gate_b[:, :], final_norm_g.partition_broadcast(P)).then_inc(s_bias, 16)
            norm(4)

        @block.gpsimd
        def _(pool):
            blocks = pool.alloc_register("pool_blocks")
            pool.reg_mov(blocks, 1)
            for layer in range(2):
                blocks_here = extra_block_count(pool, layer)
                with pool.Fori(0, X_BLOCKS) as b:
                    with pool.If(blocks_here > b):
                        pool.wait_ge(e_added, blocks)
                        pool.reg_add(blocks, blocks, 1)
                        e = pool.value_load(blk[0:1, layer, bass.ds(b, 1)], min_val=0, max_val=E - 1)
                        for part, dst in enumerate((x_gate, x_up, x_down)):
                            pool.dma_start(as_chunks(dst, D if part == 2 else F), expert_source(layer, e, part))\
                                .then_inc(e_landed, 16)

        @block.vector
        def _(dve):
            own = Own(dve, dve_step)
            own(dve.memset(wgt[:, :, :], 0.0))
            dve.memset(slot[:, :, :], -1.0).then_inc(e_added, 1)

            def sign(ins, s, value):
                ins.then_inc(s, 1)
                dve.wait_ge(s, value)

            dve.wait_ge(c_exp, 1)
            own(dve.tensor_scalar(ct[:, 1], ct[:, 0], 1.0, None, ALU.add))
            own(dve.reciprocal(ct[:, 0], ct[:, 1]))
            sign(dve.tensor_tensor(sc[:, :], cc[:, :], ct[:, 0], ALU.mult), c_silu, 1)

            def rotary_angles():
                dve.wait_ge(s_const, 80)
                own(dve.tensor_copy(posf[:, :], posi[:, :]))
                raw, k1, k2 = xnf[:, 128:192], xnf[:, 192:256], xnf[:, 256:320]
                for t in range(NT):
                    own(dve.tensor_scalar(raw[:, t * HALF:(t + 1) * HALF], cst[:, INVF:INVF + HALF], posf[:, t:t + 1], None,
                                          ALU.mult))
                for dst, lead in ((ang, 0.25), (turns, 0.0)):
                    own(dve.tensor_scalar(k1, raw, 1.0 / (2 * np.pi), lead, ALU.mult, ALU.add))
                    own(dve.tensor_scalar(k2, k1, ROUND, None, ALU.add))
                    own(dve.tensor_scalar(k1, k2, ROUND, None, ALU.subtract))
                    own(dve.scalar_tensor_tensor(dst, k1, -TWO_PI_HI, raw, ALU.mult, ALU.add))
                    own(dve.scalar_tensor_tensor(k2, k1, -TWO_PI_MID, dst, ALU.mult, ALU.add))
                    own(dve.scalar_tensor_tensor(dst, k1, -TWO_PI_LO, k2, ALU.mult, ALU.add))
                    own(dve.tensor_scalar(k2, dst, lead * 2 * np.pi, PI_SAFE, ALU.add, ALU.min))
                    dve.tensor_scalar(dst, k2, -PI_SAFE, None, ALU.max).then_inc(angles, 1)

            def ada(layer, part, k):
                name = ("ada", layer, part, k // 2)
                w = as_chunks(slot_of(name), 2048)[:, k % 2, :]
                if k % 2 == 0:
                    arrived(dve, name)
                acc_k = acc_b if (layer, part) == (1, 0) else acc[:, :]
                if k == 0:
                    if part:
                        dve.wait_ge(mod_out, PIECES[layer, part])
                    ins = dve.tensor_scalar(acc_k, w, sc[:, 0:1], None, ALU.mult)
                else:
                    ins = dve.scalar_tensor_tensor(acc_k, w, sc[:, k:k + 1], acc_k, ALU.mult, ALU.add)
                if k % 2:
                    sign(ins, ada_read, 12 * layer + 4 * part + k // 2 + 1)
                else:
                    own(ins)

            def mod(layer, part):
                n = PIECES[layer, part]
                dve.wait_ge(mod_out, n + 1)
                if n == 0:
                    dve.wait_ge(s_misc, 144)
                b = ps[:, 7, :]
                if part == 0:
                    own(dve.tensor_tensor(colm[:, layer, 1], b[:, 0:KD], colb[:, layer, 0], ALU.add))
                    own(dve.tensor_tensor(colt[:, :], b[:, KD:2 * KD], colb[:, layer, 1], ALU.add))
                    sign(dve.scalar_tensor_tensor(colm[:, layer, 0], colt[:, :], 1.0, colg[:, layer, 0], ALU.add,
                                                  ALU.mult), mod_read, n + 1)
                    return
                if part == 1:
                    sign(dve.tensor_tensor(colm[:, layer, 3], b[:, 0:KD], colb[:, layer, 3], ALU.add), mod_read, n + 1)
                else:
                    own(dve.tensor_tensor(colt[:, :], b[:, 0:KD], colb[:, layer, 4], ALU.add))
                    sign(dve.scalar_tensor_tensor(colm[:, layer, 2], colt[:, :], 1.0, colg[:, layer, 1], ALU.add,
                                                  ALU.mult), mod_read, n + 1)
                dve.wait_ge(s_bias, 16 * (2 * layer + part))
                for h in range(2):
                    dve.wait_ge(mod_out, n + 2 + h)
                    part_b = gate_b[:, 512 * h:512 * h + 512]
                    sign(dve.tensor_tensor(part_b, ps[:, 7, :], part_b, ALU.add), mod_read, n + 2 + h)

            def norm(n):
                dve.wait_ge(squared, 2 * n + 2)
                sign(dve.tensor_scalar(ss[:, :], ss[:, :], 1.0 / D, EPS, ALU.mult, ALU.add), var_ready, n + 1)
                dve.wait_ge(std_ready, n + 1)
                own(dve.reciprocal(rstd[:, :], std[:, :]))

            def norm_and_modulate(n):
                norm(n)
                if n == 0:
                    dve.wait_ge(tables, 8)
                for t in range(NT):
                    dve.tensor_scalar(xn[:, t].rearrange("p k n -> p n k"),
                                      xs[:, t].rearrange("p (n k) -> p n k", k=KD), rstd[:, t:t + 1], None, ALU.mult)\
                       .then_inc(xn_ready, 1)
                layer, which = n // 2, n % 2
                if n == 0:
                    mod(0, 0)
                elif which == 1:
                    mod(layer, 2)
                    if layer == 0:
                        mod(1, 0)
                for b in (0, 2):
                    dve.wait_ge(xn_turned, 4 * n + b + 1)
                    for k in (2 * b, 2 * b + 1):
                        dve.tensor_scalar(hT[:, k, :], ps[:, b, (k % 2) * S:(k % 2 + 1) * S],
                                          colm[:, layer, 2 * which, k:k + 1], colm[:, layer, 2 * which + 1, k:k + 1],
                                          ALU.mult, ALU.add).then_inc(hT_dve, 1)

            def project(units, side):
                if units[0] in (0, 6):
                    dve.wait_ge(xn_turned, 4 if units[0] == 0 else 12)
                for u in units:
                    layer, chunk, t, kind = UNITS[u]
                    if kind != "v":
                        rope(u, chunk, t, kind)
                    for job in side.get(u - units[0], ()):
                        job()

            def rope(u, chunk, t, kind):
                r = ropes_before(u)
                n = 256 if kind == "kv" else 512
                hn = n // HD
                b = ps[:, 6 + u % 2, 0:n]
                b3 = b.rearrange("p (h d) -> p h d", d=HD)
                r2 = rope2[:, 0:n].rearrange("p (h d) -> p h d", d=HD)
                dve.wait_ge(projected, u + 1)
                own(dve.tensor_tensor(rope1[:, 0:n].rearrange("p (h d) -> p h d", d=HD), b3,
                                      cos2[:, t].unsqueeze(1).to_broadcast([P, hn, HD]), ALU.mult))
                own(dve.tensor_tensor(r2[:, :, 0:HALF], b3[:, :, HALF:HD],
                                      sin2[:, t, 0:HALF].unsqueeze(1).to_broadcast([P, hn, HALF]), ALU.mult))
                sign(dve.tensor_tensor(r2[:, :, HALF:HD], b3[:, :, 0:HALF],
                                       sin2[:, t, HALF:HD].unsqueeze(1).to_broadcast([P, hn, HALF]), ALU.mult),
                     rope_read, r + 1)
                if r >= 2:
                    dve.wait_ge(qk_turned, r - 1)
                if kind == "kv":
                    dup = roped_sb[r % 2].rearrange("p (j two d) -> p j two d", two=2, d=HD)
                    a, bb = (z[:, 0:n].rearrange("p (j d) -> p j d", d=HD) for z in (rope1, rope2))
                    own(dve.tensor_tensor(dup[:, :, 0], a, bb, ALU.add))
                    sign(dve.tensor_tensor(dup[:, :, 1], a, bb, ALU.add), roped, r + 1)
                else:
                    sign(dve.tensor_tensor(roped_sb[r % 2], rope1, rope2, ALU.add), roped, r + 1)

            def take_o(s):
                layer, group, h, narrow = HEADS[s]
                dve.wait_ge(exped, 2 * s + 2)
                dve.wait_ge(pv_done, s + 1)
                src = ps[:, 5 + s % 2, 0:NT * HD].rearrange("p (t d) -> p t d", d=HD)
                if layer == 0:
                    dve.wait_ge(sink_exped, h + 1)
                    own(dve.tensor_tensor(den[:, h], den[:, h], esk[:, h], ALU.add))
                    own(dve.reciprocal(esk[:, h], den[:, h]))
                    dve.tensor_tensor(oA[:, :, HD * h:HD * h + HD], src,
                                      esk[:, h].unsqueeze(2).to_broadcast([P, NT, HD]), ALU.mult).then_inc(o_copied, 1)
                else:
                    dve.tensor_copy(oB[:, group, :, HD * h:HD * h + HD], src).then_inc(o_copied, 1)

            def heads(steps, side):
                for s in steps:
                    layer, group, h, narrow = HEADS[s]
                    width = P if narrow else S
                    col = group * B_HEADS + h
                    m = (M_A if layer == 0 else (M_B0, M_B1, M_B2)[group])
                    dve.wait_ge(s_mask, 16 * (layer + 1))
                    dve.wait_ge(scored, s + 1)
                    if s >= 3:
                        dve.wait_ge(exped, 2 * (s - 2))
                    sign(dve.scalar_tensor_tensor(sm[s % 3][:, 0:2 * width], ps[:, s % 3, 0:2 * width], SCALE,
                                                  msk[:, m:m + 2 * width], ALU.mult, ALU.add), masked, s + 1)
                    own(dve.reduce_max(mx[:, :], sm[s % 3][:, 0:2 * width].rearrange("p (t n) -> p t n", t=NT), AX_X))
                    if layer == 0:
                        dve.tensor_scalar(nm[:, col], mx[:, :], sink[:, h:h + 1], -1.0, ALU.max, ALU.mult).then_inc(negmax, 1)
                    else:
                        dve.tensor_scalar(nm[:, col], mx[:, :], -1.0, None, ALU.mult).then_inc(negmax, 1)
                    if s - steps[0] >= 4:
                        take_o(s - 4)
                    for job in side.get(s - steps[0], ()):
                        job()
                for s in steps[-4:]:
                    take_o(s)

            def mix_out(layer, side=()):
                for b in (range(4) if layer == 0 else range(2)):
                    if b % 2 == 0:
                        dve.wait_ge(o_turned, (0, 4)[layer] + b + 1)
                        dve.tensor_copy(oT[:, 2 * b:2 * b + 2, :], ps[:, b, :].rearrange("p (c t) -> p c t", t=S))\
                           .then_inc(oT_dve, 1)
                for job in side:
                    job()
                for n in range(4):
                    t, h = n // 2, n % 2
                    cols = slice(512 * h, 512 * h + 512)
                    tmp = xnf[:, 512 * n:512 * n + 512]
                    dve.wait_ge(mixed, 4 * layer + n + 1)
                    own(dve.tensor_tensor(tmp, ps[:, 4 + n, :], gate_b[:, cols], ALU.mult))
                    ins = dve.tensor_tensor(xs[:, t, cols], xs[:, t, cols], tmp, ALU.add)
                    if n == 3:
                        sign(ins, x_updated, 2 * layer + 1)
                    else:
                        own(ins)

            def ranks(values, n):
                for j in range(4):
                    cmp = rr[:, j, 0:4 * n].rearrange("p (g i) -> p g i", i=4)
                    dve_first = values[:, :, j:j + 1]
                    own(dve.tensor_tensor(cmp[:, :, 0:j + 1], dve_first.to_broadcast([P, n, j + 1]),
                                          values[:, :, 0:j + 1], ALU.is_gt))
                    if j < 3:
                        own(dve.tensor_tensor(cmp[:, :, j + 1:4], dve_first.to_broadcast([P, n, 3 - j]),
                                              values[:, :, j + 1:4], ALU.is_ge))
                own(dve.tensor_tensor(rr[:, 0:2, 0:4 * n], rr[:, 0:2, 0:4 * n], rr[:, 2:4, 0:4 * n], ALU.add))
                own(dve.tensor_tensor(rr[:, 0, 0:4 * n], rr[:, 0, 0:4 * n], rr[:, 1, 0:4 * n], ALU.add))

            def route(layer):
                scores, biased, hi, lo, m1, m2, g_score, g_sel, wsel = (rt[:, j] for j in range(1, 10))
                dve.wait_ge(logits_exped, layer + 1)
                own(dve.tensor_scalar(biased, rt[:, 0], 1.0, None, ALU.add))
                own(dve.reciprocal(scores, biased))
                own(dve.tensor_tensor(biased.rearrange("p (t e) -> p t e", t=NT),
                                      scores.rearrange("p (t e) -> p t e", t=NT),
                                      rbias[:, :].unsqueeze(1).to_broadcast([P, NT, E]), ALU.add))
                b4 = biased.rearrange("p (g i) -> p g i", i=4)
                pair = biased.rearrange("p (m two) -> p m two", two=2)
                own(dve.tensor_tensor(hi[:, 0:16], pair[:, :, 0], pair[:, :, 1], ALU.max))
                own(dve.tensor_tensor(lo[:, 0:16], pair[:, :, 0], pair[:, :, 1], ALU.min))
                h2, l2 = (z[:, 0:16].rearrange("p (g two) -> p g two", two=2) for z in (hi, lo))
                own(dve.tensor_tensor(m1[:, 0:8], h2[:, :, 0], h2[:, :, 1], ALU.max))
                own(dve.tensor_tensor(m2[:, 0:8], h2[:, :, 0], h2[:, :, 1], ALU.min))
                own(dve.tensor_tensor(m2[:, 8:16], l2[:, :, 0], l2[:, :, 1], ALU.max))
                own(dve.tensor_tensor(m2[:, 16:24], m2[:, 0:8], m2[:, 8:16], ALU.max))
                own(dve.tensor_tensor(g_score[:, 0:8], m1[:, 0:8], m2[:, 16:24], ALU.add))
                ranks(g_score[:, 0:8].rearrange("p (t g) -> p t g", g=4), NT)
                own(dve.tensor_scalar(g_sel[:, 0:8], rr[:, 0, 0:8], 0.5, None, ALU.is_lt))
                ranks(b4, 8)
                s3 = sel[:, :, :].rearrange("p t (g i) -> p (t g) i", i=4)
                sign(dve.scalar_tensor_tensor(s3, rr[:, 0, :].rearrange("p (g i) -> p g i", i=4), 1.5,
                                             g_sel[:, 0:8].unsqueeze(2).to_broadcast([P, 8, 4]), ALU.is_lt, ALU.mult),
                     routed, layer + 1)
                w3 = wsel.rearrange("p (t e) -> p t e", t=NT)
                own(dve.tensor_tensor(w3, scores.rearrange("p (t e) -> p t e", t=NT), sel[:, :, :], ALU.mult))
                own(dve.reduce_sum(m1[:, 0:NT], w3, AX_X))
                own(dve.reciprocal(m2[:, 0:NT], m1[:, 0:NT]))
                own(dve.tensor_tensor(wgt[:, :, 0:E], w3, m2[:, 0:NT].unsqueeze(2).to_broadcast([P, NT, E]), ALU.mult))
                dve.wait_ge(ranked, layer + 1)
                own(dve.scalar_tensor_tensor(slot_raw[:, :, :], ps[:, 5, 0:NT * E].rearrange("p (t e) -> p t e", t=NT), 1.0,
                                             sel[:, :, :], ALU.add, ALU.mult))
                own(dve.tensor_scalar(slot[:, :, 0:E], slot_raw[:, :, :], -1.0, None, ALU.add))

            def list_extra_blocks(layer):
                x1, x2, more, s1, s2, s3 = (xb[:, j, 8:8 + E] for j in range(6))
                tokens = ps[:, 5, NT * E:NT * E + E]
                own(dve.memset(xb[:, :, :], 0.0))
                own(dve.tensor_scalar(x1, tokens, float(C), None, ALU.is_gt))
                own(dve.scalar_tensor_tensor(x2, tokens, 2.0 * C, x1, ALU.is_gt, ALU.add))
                own(dve.scalar_tensor_tensor(more, tokens, 3.0 * C, x2, ALU.is_gt, ALU.add))
                at = 2
                for shift, to in ((1, 3), (2, 4), (4, 3), (8, 4)):
                    own(dve.tensor_tensor(xb[:, to, 8:8 + E], xb[:, at, 8:8 + E], xb[:, at, 8 - shift:8 + E - shift], ALU.add))
                    at = to
                up_to = xb[:, at, 8:8 + E].unsqueeze(1).to_broadcast([P, X_BLOCKS, E])
                number = cst[:, IOTA:IOTA + X_BLOCKS]
                past, before = (xcmp[:, j].rearrange("p (b e) -> p b e", e=E) for j in range(2))
                own(dve.tensor_tensor(past, up_to, number.unsqueeze(2).to_broadcast([P, X_BLOCKS, E]), ALU.is_le))
                own(dve.reduce_sum(xsum[:, 0], past, AX_X))
                own(dve.tensor_tensor(before, past, more.unsqueeze(1).to_broadcast([P, X_BLOCKS, E]), ALU.mult))
                own(dve.reduce_sum(xsum[:, 1], before, AX_X))
                own(dve.tensor_tensor(xsum[:, 2], number, xsum[:, 1], ALU.subtract))
                own(dve.tensor_scalar(xsum[:, 3], xsum[:, 2], 1.0, float(C), ALU.add, ALU.mult))
                own(dve.tensor_copy(blk[:, layer, 0:X_BLOCKS], xsum[:, 0]))
                own(dve.tensor_copy(blk[:, layer, X_BLOCKS:2 * X_BLOCKS], xsum[:, 3]))
                sign(dve.tensor_copy(blk[:, layer, 2 * X_BLOCKS:2 * X_BLOCKS + 1], xb[:, at, 7 + E:8 + E]), counted, layer + 1)

            def mark(out, slots, e, weight=None):
                for t in range(NT):
                    column = slot[:, t, bass.ds(e, 1)]
                    if weight is None:
                        ins = dve.tensor_scalar(out[:, t], slots, column, None, ALU.is_equal)
                    else:
                        ins = dve.tensor_scalar(out[:, t], slots, column, weight[:, t, bass.ds(e, 1)], ALU.is_equal, ALU.mult)
                return ins

            def mark_pair(out, first, weight=None):
                for b in range(2):
                    ins = mark(out[:, :, C * b:C * b + C], cst[:, IOTA:IOTA + C], first + b, weight)
                return ins

            def modulate_gather(layer, n):
                dve.wait_ge(gathered, n)
                for b in range(2):
                    g3 = ps[:, b, :].rearrange("p (k s) -> p k s", s=P)
                    part = xg[:, 4 * b:4 * b + 4, :]
                    own(dve.tensor_tensor(part, g3, colm[:, layer, 2, 4 * b:4 * b + 4].unsqueeze(2).to_broadcast([P, 4, P]),
                                          ALU.mult))
                    ins = dve.tensor_tensor(part, part, colm[:, layer, 3, 4 * b:4 * b + 4].unsqueeze(2)
                                            .to_broadcast([P, 4, P]), ALU.add)
                ins.then_inc(xg_ready, 1)

            def add_scattered(q):
                for n in range(4):
                    t, h = n // 2, n % 2
                    y = yacc[:, t, 512 * h:512 * h + 512]
                    dve.wait_ge(scattered, q * 4 + (n + 1))
                    dve.tensor_tensor(y, y, ps[:, 6 + n % 2, :], ALU.add).then_inc(scatter_free, 1)

            def experts(layer):
                q0, g0 = PAIRS * layer, GATHERS * layer
                for t in range(NT):
                    dve.memset(yacc[:, t], 0.0).then_inc(scatter_free, 1)
                mark_pair(pick, 0).then_inc(picked, 1)
                list_extra_blocks(layer)
                modulate_gather(layer, g0 + 1)
                blocks_here = extra_block_count(dve, layer)

                def pair(i, first):
                    mark_pair(pick, i * 2 + 2).then_inc(picked, 1)
                    mark_pair(pw, i * 2, wgt).then_inc(pw_ready, 1)
                    dve.wait_ge(gate_exped, i + (q0 + 1))
                    own(dve.tensor_scalar(sg[:, :], eg[:, :], 1.0, None, ALU.add))
                    own(dve.reciprocal(eg[:, :], sg[:, :]))
                    own(dve.tensor_tensor(sg[:, :], ps[:, 2, :], eg[:, :], ALU.mult))
                    dve.wait_ge(up_done, i + (q0 + 1))
                    dve.tensor_tensor(sg[:, :], ps[:, 3, :], sg[:, :], ALU.mult).then_inc(a_ready, 1)
                    if not first:
                        add_scattered(i + (q0 - 1))
                    dve.wait_ge(pw_turned, i + (q0 + 1))
                    dve.tensor_copy(pwT[:, :], ps[:, 3, 0:S]).then_inc(pwT_ready, 1)
                    modulate_gather(layer, i + (g0 + 2))

                pair(0, True)
                static = own.n
                per = 2 + 3
                with dve.Fori(1, PAIRS) as i:
                    own.turn = (i - 1) * per
                    pair(i, False)
                    assert own.n - static == per
                    with dve.If(blocks_here > i - 1):
                        extra_block(layer, i - 1)
                own.turn = 0
                own.n = static + per * (PAIRS - 1)
                add_scattered(q0 + PAIRS - 1)

            blocks = dve.alloc_register("dve_blocks")
            steps = dve.alloc_register("dve_steps")
            dve.reg_mov(blocks, 1)
            dve.reg_mov(steps, 0)

            def extra_block(layer, b):
                def link(ins):
                    ins.then_inc(e_dve, 1)
                    dve.reg_add(steps, steps, 1)
                    dve.wait_ge(e_dve, steps)
                e = dve.value_load(blk[0:1, layer, bass.ds(b, 1)], min_val=0, max_val=E - 1)
                start = dve.value_load(blk[0:1, layer, bass.ds(b + X_BLOCKS, 1)], min_val=C, max_val=S - C)
                slots = cst[:, bass.ds(start + IOTA, C)]
                mark(pick[:, :, 0:C], slots, e)
                for half in range(2):
                    ins = mark(pw[:, :, C * half:C * half + C], slots, e, wgt)
                ins.then_inc(e_picked, 1)
                dve.wait_ge(e_gathered, blocks)
                g3 = ps[:, 0, :].rearrange("p (k s) -> p k s", s=C)
                link(dve.tensor_tensor(x_xg[:, :, :], g3, colm[:, layer, 2].unsqueeze(2).to_broadcast([P, KD, C]), ALU.mult))
                link(dve.tensor_tensor(x_xg[:, :, :], x_xg[:, :, :],
                                       colm[:, layer, 3].unsqueeze(2).to_broadcast([P, KD, C]), ALU.add))
                dve.tensor_copy(x_pwT[:, :], ps[:, 3, 0:S]).then_inc(e_xg, 1)
                dve.wait_ge(e_exped, blocks)
                link(dve.tensor_scalar(sg[0:C, :], eg[0:C, :], 1.0, None, ALU.add))
                link(dve.reciprocal(eg[0:C, :], sg[0:C, :]))
                link(dve.tensor_tensor(sg[0:C, :], ps[0:C, 2, :], eg[0:C, :], ALU.mult))
                dve.tensor_tensor(sg[0:C, :], ps[C:P, 3, :], sg[0:C, :], ALU.mult).then_inc(e_a, 1)
                dve.wait_ge(e_scattered, blocks)
                for n in range(4):
                    t, h = n // 2, n % 2
                    y = yacc[:, t, 512 * h:512 * h + 512]
                    ins = dve.tensor_tensor(y, y, ps[:, (6, 7, 0, 1)[n], :], ALU.add)
                ins.then_inc(e_added, 1)
                dve.reg_add(blocks, blocks, 1)

            def ffn_out(layer):
                dve.wait_ge(scatter_free, 2 * (layer + 1) + 4 * PAIRS * (layer + 1))
                dve.wait_ge(e_added, blocks)
                for t in range(NT):
                    own(dve.tensor_tensor(yacc[:, t], yacc[:, t], gate_b[:, :], ALU.mult))
                    ins = dve.tensor_tensor(xs[:, t], xs[:, t], yacc[:, t], ALU.add)
                    if t == NT - 1:
                        sign(ins, x_updated, 2 * layer + 2)
                    else:
                        own(ins)

            def ffn(layer):
                norm_and_modulate(2 * layer + 1)
                route(layer)
                experts(layer)
                ffn_out(layer)

            def ada_jobs(layer, part, *ks):
                return [lambda k=k: ada(layer, part, k) for k in ks]

            ada(0, 0, 0)
            ada(0, 0, 1)
            rotary_angles()
            for k in range(2, KD):
                ada(0, 0, k)
            norm_and_modulate(0)
            project(RUNS[0, 0][0], {2: ada_jobs(0, 1, 0, 1), 3: ada_jobs(0, 1, 2, 3), 4: ada_jobs(0, 1, 4, 5),
                                    5: ada_jobs(0, 1, 6, 7)})
            side = {1: [lambda: mod(0, 1)]}
            side.update({4 + k: ada_jobs(0, 2, k) for k in range(KD)})
            heads(RUNS[0, 0][1], side)
            mix_out(0, ada_jobs(1, 0, *range(KD)))
            ffn(0)
            norm_and_modulate(2)
            for g in range(B_GRPS):
                if g == 1:
                    mod(1, 1)
                more = g < 2
                project(RUNS[1, g][0], {3: ada_jobs(1, g + 1, 0, 1), 4: ada_jobs(1, g + 1, 2, 3),
                                        5: ada_jobs(1, g + 1, 4, 5)} if more else {})
                heads(RUNS[1, g][1], {1: ada_jobs(1, g + 1, 6), 3: ada_jobs(1, g + 1, 7)} if more else {})

            def grp(v, g):
                return v[:, g * B_HEADS:(g + 1) * B_HEADS, :]
            least, z = aw[:, 1, 0:B_HEADS], aw[:, 1, B_HEADS:2 * B_HEADS]
            own(dve.tensor_tensor(z, grp(nm, 0), grp(nm, 1), ALU.min))
            own(dve.tensor_tensor(least, z, grp(nm, 2), ALU.min))
            for g in range(B_GRPS):
                ins = dve.tensor_tensor(grp(aw[:, 0], g), grp(nm, g), least, ALU.subtract)
                if g < 2:
                    own(ins)
            sign(ins, merge_in, 1)
            dve.wait_ge(merge_exped, 1)
            own(dve.tensor_tensor(aw[:, 2], aw[:, 0], den[:, :, :], ALU.mult))
            own(dve.tensor_tensor(z, grp(aw[:, 2], 0), grp(aw[:, 2], 1), ALU.add))
            own(dve.tensor_tensor(least, z, grp(aw[:, 2], 2), ALU.add))
            own(dve.reciprocal(z, least))
            for g in range(B_GRPS):
                own(dve.tensor_tensor(grp(aw[:, 2], g), grp(aw[:, 0], g), z, ALU.mult))
            dve.wait_ge(o_copied, len(HEADS))
            for g in range(B_GRPS):
                for t in range(NT):
                    o = oB[:, g, t].rearrange("p (h d) -> p h d", d=HD)
                    own(dve.tensor_tensor(o, o, grp(aw[:, 2], g)[:, :, t:t + 1].to_broadcast([P, B_HEADS, HD]), ALU.mult))
            own(dve.tensor_tensor(oB[:, 0], oB[:, 0], oB[:, 1], ALU.add))
            dve.tensor_tensor(oB[:, 0], oB[:, 0], oB[:, 2], ALU.add).then_inc(o_ready, 1)

            mix_out(1)
            ffn(1)
            norm(4)
            dve.wait_ge(s_bias, 80)
            for t in range(NT):
                ins = dve.scalar_tensor_tensor(yacc[:, t], xs[:, t], rstd[:, t:t + 1], gate_b[:, :], ALU.mult, ALU.mult)
                if t == 0:
                    own(ins)
            ins.then_inc(x_updated, 1)

        @block.tensor
        def _(pe):
            def mod(layer, part):
                n = PIECES[layer, part]
                pe.wait_ge(ada_read, 12 * layer + 4 * part + 4)
                sums = acc_b if (layer, part) == (1, 0) else acc[:, :]
                for piece in range(1 if part == 0 else 3):
                    if n + piece >= 1:
                        pe.wait_ge(mod_read, n + piece)
                    b = ps[:, 7, :]
                    if piece == 0:
                        at = {0: 0, 1: D, 2: 0}[part]
                        for j in range(2 if part == 0 else 1):
                            v = sums[:, at + D * j:at + D * j + D].rearrange("p (n k) -> p n k", k=KD)
                            for k in range(KD):
                                ins = pe.matmul(b[:, KD * j + k:KD * j + k + 1], v[:, :, k], ones[:, 0:1],
                                                start=True, stop=True)
                    else:
                        at = {1: 0, 2: D}[part] + 512 * (piece - 1)
                        ins = pe.matmul(b, ones, sums[:, at:at + 512], start=True, stop=True)
                    ins.then_inc(mod_out, 1)

            def turn_xn(n):
                for b in range(4):
                    if b == 0:
                        pe.wait_ge(xn_ready, 2 * n + 2)
                    for k in (2 * b, 2 * b + 1):
                        for t in range(NT):
                            ins = pe.transpose(ps[:, b, (k % 2) * S + t * P:(k % 2) * S + (t + 1) * P], xn[:, t, k, :], ident)
                    ins.then_inc(xn_turned, 1)

            def project(units):
                def turn(u):
                    if UNITS[u][3] == "v":
                        return
                    r = ropes_before(u)
                    pe.wait_ge(roped, r + 1)
                    if r >= 2:
                        pe.wait_ge(qk_copied, r - 1)
                    for m in range(4):
                        ins = pe.transpose(ps[:, r % 2, m * P:(m + 1) * P], roped_sb[r % 2][:, m * P:(m + 1) * P], ident)
                    ins.then_inc(qk_turned, 1)

                if units[0] > 0:
                    pe.wait_ge(o_copied, RUNS_BEFORE[units[0]])
                for u in units:
                    layer, chunk, t, kind = UNITS[u]
                    name = ("qkv", layer, chunk)
                    if t == 0:
                        arrived(pe, name)
                    if u >= 2:
                        pe.wait_ge(rope_read, ropes_before(u - 1))
                        if v_copies_before(u - 1):
                            pe.wait_ge(v_copied, v_copies_before(u - 1))
                    w = as_chunks(slot_of(name), 512)
                    for k in range(KD):
                        ins = pe.matmul(ps[:, 6 + u % 2, :], hT[:, k, t * P:(t + 1) * P], w[:, k, :], start=k == 0,
                                        stop=k == KD - 1)
                    ins.then_inc(projected, 1)
                    if u > units[0]:
                        turn(u - 1)
                turn(units[-1])
                pe.wait_ge(qk_copied, ropes_before(units[-1] + 1))
                pe.wait_ge(v_copied, v_copies_before(units[-1] + 1))

            def score(s):
                layer, group, h, narrow = HEADS[s]
                rows = slice(HD * (h % 2), HD * (h % 2) + HD)
                kc = h // 4 if layer == 0 else h // 2
                if s >= 3:
                    pe.wait_ge(masked, s - 2)
                for t in range(NT):
                    q = qT[rows, h // 2, t * P:(t + 1) * P]
                    if narrow:
                        ins = pe.matmul(ps[:, s % 3, t * P:(t + 1) * P], q, kT[rows, kc, t * P:(t + 1) * P], start=True, stop=True)
                    else:
                        ins = pe.matmul(ps[:, s % 3, t * S:(t + 1) * S], q, kT[rows, kc, :], start=True, stop=True)
                ins.then_inc(scored, 1)

            def turn_p(s):
                narrow = HEADS[s][3]
                pe.wait_ge(exped, 2 * s + 2)
                if s >= 2:
                    pe.wait_ge(pT_copied, s - 1)
                for t in range(NT):
                    for kt in range(1 if narrow else NT):
                        src = pr[s % 3][:, t * P:(t + 1) * P] if narrow else pr[s % 3][:, t * S + kt * P:t * S + (kt + 1) * P]
                        ins = pe.transpose(ps[:, 3 + s % 2, kt * S + t * P:kt * S + (t + 1) * P], src, ident)
                ins.then_inc(p_turned, 1)

            def p_times_v(s):
                layer, group, h, narrow = HEADS[s]
                vc = HD * (h // 4 if layer == 0 else h)
                pe.wait_ge(pT_copied, s + 1)
                if s >= 2:
                    pe.wait_ge(o_copied, s - 1)
                for t in range(NT):
                    o = ps[:, 5 + s % 2, t * HD:(t + 1) * HD]
                    if narrow:
                        ins = pe.matmul(o, pT[s % 2][:, t * P:(t + 1) * P], vv[:, t, vc:vc + HD], start=True, stop=True)
                    else:
                        for kt in range(NT):
                            ins = pe.matmul(o, pT[s % 2][:, kt * S + t * P:kt * S + (t + 1) * P], vv[:, kt, vc:vc + HD],
                                            start=kt == 0, stop=kt == NT - 1)
                ins.then_inc(pv_done, 1)

            def heads(steps, side):
                for s in steps:
                    score(s)
                    if s >= steps[0] + 2:
                        turn_p(s - 2)
                    if s >= steps[0] + 3:
                        p_times_v(s - 3)
                    if s - steps[0] in side:
                        side[s - steps[0]]()
                turn_p(steps[-2])
                p_times_v(steps[-3])
                turn_p(steps[-1])
                p_times_v(steps[-2])
                p_times_v(steps[-1])

            def mix_out(layer):
                n_ch = (8, 4)[layer]
                o = oA if layer == 0 else oB[:, 0]
                if layer == 0:
                    pe.wait_ge(o_copied, A_HEADS)
                else:
                    pe.wait_ge(o_ready, 1)
                for b in range(n_ch // 2):
                    for ch in (2 * b, 2 * b + 1):
                        for t in range(NT):
                            ins = pe.transpose(ps[:, b, (ch % 2) * S + t * P:(ch % 2) * S + (t + 1) * P],
                                               o[:, t, P * ch:P * ch + P], ident)
                    ins.then_inc(o_turned, 1)
                pe.wait_ge(oT_dve, (2, 3)[layer])
                pe.wait_ge(oT_act, (2, 3)[layer])
                for n in range(4):
                    t, h = n // 2, n % 2
                    for ch in range(n_ch):
                        name = ("wo", layer, ch // 4)
                        if n == 0 and ch % 4 == 0:
                            arrived(pe, name)
                        ins = pe.matmul(ps[:, 4 + n, :], oT[:, ch, t * P:(t + 1) * P],
                                        as_chunks(slot_of(name), D)[:, ch % 4, 512 * h:512 * h + 512],
                                        start=ch == 0, stop=ch == n_ch - 1)
                    ins.then_inc(mixed, 1)

            def route(layer):
                pe.wait_ge(hT_dve, 8 * layer + 8)
                pe.wait_ge(hT_act, 8 * layer + 8)
                for t in range(NT):
                    for k in range(KD):
                        ins = pe.matmul(ps[:, 4, t * E:(t + 1) * E], hT[:, k, t * P:(t + 1) * P], rw[:, k, :], start=k == 0,
                                        stop=k == KD - 1)
                ins.then_inc(logits, 1)
                pe.wait_ge(routed, layer + 1)
                r = ps[:, 5, :]
                pe.matmul(r[:, 0:E], tri, sel[:, 0, :], start=True, stop=True)
                pe.matmul(r[:, E:2 * E], ones, sel[:, 0, :], start=True, stop=False)
                pe.matmul(r[:, E:2 * E], tri, sel[:, 1, :], start=False, stop=True)
                pe.matmul(r[:, 2 * E:3 * E], ones, sel[:, 0, :], start=True, stop=False)
                pe.matmul(r[:, 2 * E:3 * E], ones, sel[:, 1, :], start=False, stop=True).then_inc(ranked, 1)

            def gather(n):
                for k in range(KD):
                    at = k * n
                    for t in range(NT):
                        ins = pe.matmul(ps[:, at // 512, at % 512:at % 512 + n], xn[:, t, k, :], pick[:, t, 0:n],
                                        start=t == 0, stop=t == NT - 1)
                return ins

            def two(bank_a, bank_b, stationary, moving, chunks):
                for k in range(chunks):
                    for b, bank in enumerate((bank_a, bank_b)):
                        ins = pe.matmul(ps[C * b:C * b + C, bank, :], stationary(b, k), moving(b, k), start=k == 0,
                                        stop=k == chunks - 1)
                return ins

            def experts(layer):
                base = LOAD[("moe", layer, 0)]
                q0, g0 = PAIRS * layer, GATHERS * layer
                pe.wait_ge(picked, g0 + 1)
                gather(P).then_inc(gathered, 1)
                blocks_here = extra_block_count(pe, layer)

                def scatter(q):
                    pe.wait_ge(pwT_ready, q + 1)
                    pe.wait_ge(y_copied, q * 2 + 2)
                    for n in range(4):
                        t, h = n // 2, n % 2
                        pe.wait_ge(scatter_free, q * 4 + (n + 2 * layer + 1))
                        pe.matmul(ps[:, 6 + n % 2, :], pwT[:, t * P:(t + 1) * P], ye[:, 512 * h:512 * h + 512],
                                  start=True, stop=True).then_inc(scattered, 1)

                def pair(i, first):
                    def weights(part):
                        views = []
                        for n in (base + 2 * part, base + 2 * part + 1):
                            pe.wait_ge(landed[n % RING], i * 16 + 16 * (n // RING + 1))
                            views.append(as_chunks(ring[n % RING], D if part == 2 else F))
                        return views

                    gate_w = weights(0)
                    pe.wait_ge(xg_ready, i + (g0 + 1))
                    two(2, 2, lambda b, k: xg[:, k, C * b:C * b + C], lambda b, k: gate_w[b][:, k, :], KD)\
                        .then_inc(gate_done, 1)
                    up_w = weights(1)
                    two(3, 3, lambda b, k: xg[:, k, C * b:C * b + C], lambda b, k: up_w[b][:, k, :], KD)\
                        .then_inc(up_done, 1)
                    pe.wait_ge(picked, i + (g0 + 2))
                    gather(P).then_inc(gathered, 1)
                    if not first:
                        scatter(i + (q0 - 1))
                    pe.wait_ge(a_ready, i + (q0 + 1))
                    for f in range(KF):
                        ins = pe.transpose(ps[:, 2, f * P:(f + 1) * P], sg[:, f * P:(f + 1) * P], ident)
                    ins.then_inc(a_turned, 1)
                    pe.wait_ge(pw_ready, i + (q0 + 1))
                    for t in range(NT):
                        ins = pe.transpose(ps[:, 3, t * P:(t + 1) * P], pw[:, t, :], ident)
                    ins.then_inc(pw_turned, 1)
                    down_w = weights(2)
                    pe.wait_ge(aT_ready, i + (q0 + 1))
                    for h in range(2):
                        ins = two(4 + h, 4 + h, lambda b, f: aT[:, f, C * b:C * b + C],
                                  lambda b, f: down_w[b][:, f, 512 * h:512 * h + 512], KF)
                    ins.then_inc(down_done, 1)

                pair(0, True)
                with pe.Fori(1, PAIRS) as i:
                    pair(i, False)
                    with pe.If(blocks_here > i - 1):
                        extra_block()
                scatter(q0 + PAIRS - 1)

            blocks = pe.alloc_register("pe_blocks")
            landings = pe.alloc_register("pe_landings")
            pe.reg_mov(blocks, 1)
            pe.reg_mov(landings, 48)

            def extra_block():
                gate_w, up_w, down_w = as_chunks(x_gate, F), as_chunks(x_up, F), as_chunks(x_down, D)
                pe.wait_ge(e_picked, blocks)
                gather(C)
                for t in range(NT):
                    ins = pe.transpose(ps[:, 3, t * P:(t + 1) * P], pw[:, t, :], ident)
                ins.then_inc(e_gathered, 1)
                pe.wait_ge(e_landed, landings)
                pe.wait_ge(e_xg, blocks)
                two(2, 3, lambda b, k: x_xg[:, k, :], lambda b, k: (gate_w, up_w)[b][:, k, :], KD).then_inc(e_up, 1)
                pe.wait_ge(e_a, blocks)
                pe.reg_add(landings, landings, 48)
                for f in range(KF):
                    ins = pe.transpose(ps[:, 2, f * C:(f + 1) * C], sg[0:C, f * P:(f + 1) * P], ident[0:C, 0:C])
                ins.then_inc(e_turned, 1)
                pe.wait_ge(e_aT, blocks)
                two(4, 5, lambda b, f: aT[:, f, 0:C], lambda b, f: down_w[:, f, 512 * b:512 * b + 512], KF)\
                    .then_inc(e_down, 1)
                pe.wait_ge(e_y, blocks)
                for n in range(4):
                    t, h = n // 2, n % 2
                    rows = slice(C * h, C * h + C)
                    ins = pe.matmul(ps[:, (6, 7, 0, 1)[n], :], x_pwT[rows, t * P:(t + 1) * P], x_ye[rows, :],
                                    start=True, stop=True)
                ins.then_inc(e_scattered, 1)
                pe.reg_add(blocks, blocks, 1)
                pe.wait_ge(e_added, blocks)

            pe.wait_ge(s_const, 80)
            mod(0, 0)
            turn_xn(0)
            pe.wait_ge(hT_dve, 4)
            pe.wait_ge(hT_act, 4)
            pe.wait_ge(mod_read, PIECES[0, 0] + 1)
            project(RUNS[0, 0][0])
            heads(RUNS[0, 0][1], {1: lambda: mod(0, 1)})
            mix_out(0)
            pe.wait_ge(x_updated, 1)
            mod(0, 2)
            mod(1, 0)
            turn_xn(1)
            route(0)
            experts(0)
            turn_xn(2)
            pe.wait_ge(hT_dve, 12)
            pe.wait_ge(hT_act, 12)
            for g in range(B_GRPS):
                if g == 1:
                    mod(1, 1)
                    pe.wait_ge(mod_read, PIECES[1, 1] + 3)
                project(RUNS[1, g][0])
                heads(RUNS[1, g][1], {})
            mix_out(1)
            pe.wait_ge(x_updated, 3)
            mod(1, 2)
            turn_xn(3)
            route(1)
            experts(1)


INPUTS = ["x", "c", "positions", "ada_w", "ada_b", "norm_mix_g", "norm_ffn_g", "a_w_qkv", "a_w_o", "a_sink",
          "b_w_qkv", "b_w_o", "router_w", "router_bias", "exp_w_gate", "exp_w_up", "exp_w_down", "final_norm_g"]


def kernel(**inputs):
    import concourse.bacc as bacc
    from concourse.bass_utils import run_bass_kernel_spmd

    nc = bacc.Bacc("TRN2", target_bir_lowering=False, num_devices=1)
    arrays = {name: np.ascontiguousarray(inputs[name]) for name in INPUTS}
    arrays["const"] = constants()
    arrays["mask"] = masks()
    args = [nc.dram_tensor(name, a.shape, mybir.dt.from_np(a.dtype), kind="ExternalInput").ap()
            for name, a in arrays.items()]
    args.append(nc.dram_tensor("out", (1, S, D), F32, kind="ExternalOutput").ap())
    build(nc, *args)
    result = run_bass_kernel_spmd(nc, [arrays], core_ids=[0])
    return result.results[0]["out"]
```

```python
from contextlib import ExitStack

import numpy as np

import concourse.bass as bass
from concourse import mybir

ALU = mybir.AluOpType
ACT = mybir.ActivationFunctionType
F32 = mybir.dt.float32
I32 = mybir.dt.int32
AX_X = mybir.AxisListType.X

P = 128
S, D = 256, 1024
NT = S // P
KD = D // P
HD = 64
HALF = HD // 2
A_HEADS, A_KV = 16, 4
B_HEADS, B_GRPS = 8, 3
E, GRP = 16, 4
F = 512
KF = F // P
C = 64
PAIRS = E // 2
TOP_K = 2
X_BLOCKS = S * TOP_K // C - 1
RING = 6
SLOT = 4096
EPS = 1e-6
SCALE = float(HD) ** -0.5
TWO_PI_HI = 6.28125
TWO_PI_MID = float(np.float32(2 * np.pi - TWO_PI_HI).view(np.uint32) & 0xFFFFF000)
TWO_PI_MID = float(np.uint32(int(TWO_PI_MID)).view(np.float32))
TWO_PI_LO = float(2 * np.pi - TWO_PI_HI - TWO_PI_MID)
ROUND = 1.5 * 2.0 ** 23
PI_SAFE = 3.1415925

IDENT, ONES, TRI, IOTA, INVF = 0, P, 2 * P, 3 * P, 3 * P + S
N_CONST = INVF + HALF


def token_of_row():
    t = np.arange(S).reshape(S // 16, 4, 4)
    return t.transpose(2, 1, 0).reshape(S)


def constants():
    c = np.zeros((P, N_CONST), np.float32)
    c[:, IDENT:IDENT + P] = np.eye(P)
    c[:, ONES:ONES + P] = 1.0
    c[:, TRI:TRI + P] = np.triu(np.ones((P, P)), 1)
    c[:, IOTA:IOTA + S] = np.arange(S)
    c[:, INVF:] = (10000.0 ** (-np.arange(0, HD, 2) / HD)).astype(np.float32)
    return c


def masks():
    t = token_of_row()
    gap = np.abs(t[:, None] - t[None, :])
    own = np.stack([gap[:P, :P], gap[P:, P:]], 1)
    full = np.stack([gap[:P], gap[P:]], 1)
    parts = [full <= 128, full <= 64, (own % 4 == 0) & (own <= 64 * 4), (own % 16 == 0) & (own <= 64 * 16)]
    m = np.concatenate([p.reshape(P, -1) for p in parts], 1)
    return np.where(m, 0.0, -1e30).astype(np.float32)


M_A, M_B0, M_B1, M_B2, N_MASK = 0, 512, 1024, 1280, 1536


def plan_loads():
    order = [("ada", 0, 0, j) for j in range(4)]
    order += [("qkv", 0, 2), ("qkv", 0, 0)] + [("ada", 0, 1, j) for j in range(4)] + [("qkv", 0, 1)]
    order += [("ada", 0, 2, j) for j in range(4)]
    order += [("ada", 1, 0, j) for j in range(4)] + [("wo", 0, j) for j in range(2)]
    order += [("moe", 0, j) for j in range(3 * E)]
    order += [("qkv", 1, 0)]
    for j in range(4):
        order += [("qkv", 1, 1 + j), ("ada", 1, 1, j)]
    order += [("qkv", 1, 5), ("qkv", 1, 6), ("ada", 1, 2, 0), ("ada", 1, 2, 1)]
    order += [("qkv", 1, 7), ("ada", 1, 2, 2), ("ada", 1, 2, 3), ("qkv", 1, 8), ("wo", 1, 0)]
    order += [("moe", 1, j) for j in range(3 * E)]
    return order


ORDER = plan_loads()
LOAD = {name: n for n, name in enumerate(ORDER)}
AHEAD = [LOAD["moe", layer, j] for layer in range(2) for j in (6, 7)]


def plan_units():
    units = [(0, c, t, "kv" if c == 2 else "q") for c in (2, 0, 1) for t in range(NT)]
    units += [(1, c, t, "qkv"[c % 3]) for c in range(9) for t in range(NT)]
    return units


UNITS = plan_units()


def plan_heads():
    return [(0, 0, h, False) for h in range(A_HEADS)] + \
           [(1, g, h, g > 0) for g in range(B_GRPS) for h in range(B_HEADS)]


HEADS = plan_heads()
RUNS = {(0, 0): (range(0, 6), range(0, 16)),
        (1, 0): (range(6, 12), range(16, 24)),
        (1, 1): (range(12, 18), range(24, 32)),
        (1, 2): (range(18, 24), range(32, 40))}
POOL_PART = (0, 2)
BETWEEN_0 = {1: 4, 3: 5}
BETWEEN_1 = {1: 0, 3: 1, 4: 2, 5: 3, 6: 4, 7: 5}
PIECES = {(layer, part): 7 * layer + (0, 1, 4)[part] for layer in range(2) for part in range(3)}


def mod_bank(layer, part, piece):
    return {(0, 2, 1): 6, (1, 2, 1): 6, (1, 0, 0): 2, (1, 1, 0): 5, (1, 1, 1): 5, (1, 1, 2): 5}.get((layer, part, piece), 7)


GATHERS = PAIRS + 1


def ropes_before(u):
    return sum(k != "v" for _, _, _, k in UNITS[:u])


def v_copies_before(u):
    return sum("v" in k for _, _, _, k in UNITS[:u])


class Own:

    def __init__(self, eng, sem):
        self.eng, self.sem, self.n, self.turn = eng, sem, 0, 0

    def __call__(self, ins):
        self.n += 1
        ins.then_inc(self.sem, 1)
        self.eng.wait_ge(self.sem, self.turn + self.n)


def build(nc, x, c, positions, ada_w, ada_b, norm_mix_g, norm_ffn_g, a_w_qkv, a_w_o, a_sink, b_w_qkv,
          b_w_o, router_w, router_bias, exp_w_gate, exp_w_up, exp_w_down, final_norm_g, const, mask, out):
    ctx = ExitStack()
    with ctx:
        def sb(name, shape, dt=F32):
            return ctx.enter_context(nc.sbuf_tensor(name, shape, dt))

        def sem(name):
            return ctx.enter_context(nc.semaphore(name))

        ring = [sb(f"ring{s}", [P, SLOT]) for s in range(RING)]
        shared = sb("shared", [P, 3 * SLOT])
        xs = sb("xs", [P, NT, D])
        xn = sb("xn", [P, NT, KD, P])
        hT = sb("hT", [P, KD, S])
        acc = sb("acc", [P, 2048])
        gate_b = sb("gate_b", [P, D])
        cst = sb("cst", [P, N_CONST])
        cos2 = sb("cos2", [P, NT, HD])
        sin2 = sb("sin2", [P, NT, HD])
        yxg = sb("yxg", [P, 2 * D])
        ye = yxg[:, 0:D]
        xg = yxg[:, D:2 * D].rearrange("p (k s) -> p k s", s=P)
        acc_pool = yxg[:, 0:D]
        bias_b = sb("bias_b", [P, D])
        eg = bias_b[:, 0:F]
        sg = bias_b[:, F:D]
        aT = sb("aT", [P, KF, P])
        pick = sb("pick", [P, NT, P])
        pw = sb("pw", [P, NT, P])
        pwT = sb("pwT", [P, S])
        x_part = sb("x_part", [P, KD * C])
        x_xg = x_part[:, :].rearrange("p (k s) -> p k s", s=C)
        x_pwT = sb("x_pwT", [P, S])
        x_ye = sb("x_ye", [P, 512])
        x_sg = x_ye[0:C, :]
        colm = sb("colm", [P, 2, 4, KD])
        colb = sb("colb", [P, 2, 6, KD])
        colg = sb("colg", [P, 2, 2, KD])
        colt = sb("colt", [P, KD])
        cc = sb("cc", [P, KD])
        sc = sb("sc", [P, KD])
        rw = sb("rw", [P, KD, E])
        rbias = sb("rbias", [P, E])
        sink = sb("sink", [P, A_HEADS])
        posi = sb("posi", [P, NT], I32)
        posf = sb("posf", [P, NT])
        ss = sb("ss", [P, NT])
        std = sb("std", [P, NT])
        rstd = sb("rstd", [P, NT])
        sel = sb("sel", [P, NT, E])
        wgt = sb("wgt", [P, NT, E + 2])
        slot = sb("slot", [P, NT, E + 2])
        blk = sb("blk", [P, 2, 2 * X_BLOCKS + 1], I32)
        ps = ctx.enter_context(nc.psum_tensor("ps", [P, 8, 512], F32))

        ident = cst[:, IDENT:IDENT + P]
        ones = cst[:, ONES:ONES + P]
        tri = cst[:, TRI:TRI + P]

        def area(at, n):
            return shared[:, at:at + n]
        qT_all = area(0, 2048).rearrange("p (c t) -> p c t", t=S)
        kT_0 = area(2048, 1024).rearrange("p (c t) -> p c t", t=S)
        vv_0 = area(3072, 1024).rearrange("p (t n) -> p t n", t=NT)
        kT_1 = yxg[:, 0:1024].rearrange("p (c t) -> p c t", t=S)
        vv_1 = yxg[:, 1024:2048].rearrange("p (t n) -> p t n", t=NT)

        def qkv_of(layer, group):
            if layer == 0:
                return qT_all, kT_0, vv_0
            return qT_all[:, 4 * (group % 2):4 * (group % 2) + 4, :], (kT_0, kT_1)[group % 2], (vv_0, vv_1)[group % 2]
        pT = [area(6144 + 512 * b, 512) for b in range(2)]
        o_all = area(7168, 3072)
        products = area(9216, 1024)
        msk = area(10240, N_MASK)
        STEPS = B_GRPS * B_HEADS
        nm = area(11776, STEPS * NT).rearrange("p (s t) -> p s t", t=NT)
        den = area(11824, STEPS * NT).rearrange("p (s t) -> p s t", t=NT)
        esk = area(11872, A_HEADS * NT).rearrange("p (s t) -> p s t", t=NT)
        mx = area(11904, NT)
        aw = area(11906, 3 * STEPS * NT).rearrange("p (j s t) -> p j s t", j=3, t=NT)
        rt = area(0, 320).rearrange("p (j n) -> p j n", j=10)
        rr = area(320, 128).rearrange("p (j n) -> p j n", j=4)
        xb = area(448, 144).rearrange("p (j n) -> p j n", j=6)
        xcmp = area(592, 2 * X_BLOCKS * E).rearrange("p (j n) -> p j n", j=2)
        xsum = area(816, 4 * X_BLOCKS).rearrange("p (j n) -> p j n", j=4)
        slot_raw = area(848, NT * E).rearrange("p (t e) -> p t e", e=E)
        x_eg = x_part[0:C, :]
        x_aT = x_part[:, 0:KF * C].rearrange("p (f s) -> p f s", s=C)
        rw_gain = x_part[:, 0:KD * E].rearrange("p (k e) -> p k e", e=E)
        rw_shift = x_part[:, KD * E:2 * KD * E].rearrange("p (k e) -> p k e", e=E)
        shift_sum = x_part[:, 2 * KD * E:2 * KD * E + E]
        shift_row = x_part[:, 2 * KD * E + E:2 * KD * E + 2 * E]
        oA = o_all[:, 0:2048].rearrange("p (t n) -> p t n", t=NT)
        oB = o_all.rearrange("p (g t n) -> p g t n", g=B_GRPS, t=NT)
        xnf = xn[:, :, :, :].rearrange("p t k n -> p (t k n)")
        rope1, rope2 = xnf[:, 0:512], xnf[:, 512:1024]
        sm = [area(4096, 512), area(4608, 512)]
        pr = [area(5120, 512), area(5632, 512)]
        score_bank = [ps[:, 0, :], ps[:, 1, :]]
        p_bank = [ps[:, 2, :], ps[:, 3, :]]
        o_bank = ps[:, 4, 0:NT * HD]
        qk_bank = ps[:, 5, :]
        roped_sb = [xnf[:, 1024 + 512 * b:1536 + 512 * b] for b in range(2)]
        oT = hT
        yacc = hT[:, :, :].rearrange("p k s -> p (k s)").rearrange("p (t n) -> p t n", t=NT)
        junk = area(2048, 2048).rearrange("p (t n) -> p t n", t=NT)
        xT = hT
        def oT_bank(layer, b):
            return (5, 6, 5, 3)[b] if layer == 0 else b
        gates_1 = [area(SLOT * j, SLOT) for j in (1, 2)]
        x_gate, x_up, x_down = (area(SLOT * j, SLOT) for j in range(3))
        ang, turns, raw, k1, k2 = (area(7168 + 64 * j, 64) for j in range(5))
        ct = area(7488, 2 * KD).rearrange("p (j k) -> p j k", j=2)

        landed = [sem(f"landed{s}") for s in range(RING)]
        s_const, s_x, s_c, s_misc, s_bias, s_out = (sem(n) for n in (
            "const_landed", "x_landed", "c_landed", "misc_landed", "gate_bias_landed", "out_stored"))
        gates_ahead = sem("gates_ahead")
        s_mask, s_mask_again = sem("mask_landed"), sem("mask_landed_again")
        dve_step = sem("dve_step")
        c_exp, c_silu, angles, tables = sem("c_exp"), sem("c_silu"), sem("angles"), sem("rope_tables")
        ada_read, ada_read_pool, pool_step = sem("ada_read"), sem("ada_read_pool"), sem("pool_step")
        mod_out, mod_read = sem("mod_out"), sem("mod_read")
        squared, var_ready, std_ready = sem("squared"), sem("var_ready"), sem("std_ready")
        xn_ready, xn_turned = sem("xn_ready"), sem("xn_turned")
        hT_dve, hT_act = sem("hT_dve"), sem("hT_act")
        x_turned, xT_act, xT_dve, shift_summed = sem("x_turned"), sem("xT_act"), sem("xT_dve"), sem("shift_summed")
        projected, rope_read, roped = sem("projected"), sem("rope_read"), sem("roped")
        v_copied, qk_turned, qk_copied = sem("v_copied"), sem("qk_turned"), sem("qk_copied")
        scored, masked, negmax, exped = sem("scored"), sem("masked"), sem("negmax"), sem("exped")
        sink_exped, p_turned, pT_copied = sem("sink_exped"), sem("p_turned"), sem("pT_copied")
        pv_done, o_copied = sem("pv_done"), sem("o_copied")
        merge_in, merge_exped, o_ready = sem("merge_in"), sem("merge_exped"), sem("o_ready")
        o_turned, oT_dve, oT_act = sem("o_turned"), sem("oT_dve"), sem("oT_act")
        mixed, x_updated = sem("mixed"), sem("x_updated")
        rstd_ready, scaled, out_dve, out_act = sem("rstd_ready"), sem("scaled"), sem("out_dve"), sem("out_act")
        logits_scaled = sem("logits_scaled")
        logits, logits_exped, routed = sem("logits"), sem("logits_exped"), sem("routed")
        ranked, counted = sem("ranked"), sem("counted")
        picked, pw_ready, pw_turned, pwT_ready = sem("picked"), sem("pw_ready"), sem("pw_turned"), sem("pwT_ready")
        gathered, xg_ready = sem("gathered"), sem("xg_ready")
        gate_done, up_done, gate_exped, a_ready = sem("gate_done"), sem("up_done"), sem("gate_exped"), sem("a_ready")
        down_done, y_copied = sem("down_done"), sem("y_copied")
        a_turned, aT_ready, e_turned, e_aT = sem("a_turned"), sem("aT_ready"), sem("e_turned"), sem("e_aT")
        scattered, scatter_free = sem("scattered"), sem("scatter_free")
        e_landed, e_landed_down, e_picked = sem("e_landed"), sem("e_landed_down"), sem("e_picked")
        e_gathered, e_xg = sem("e_gathered"), sem("e_xg")
        e_up, e_exped, e_a, e_down, e_y = sem("e_up"), sem("e_exped"), sem("e_a"), sem("e_down"), sem("e_y")
        e_scattered, e_added, e_dve = sem("e_scattered"), sem("e_added"), sem("e_dve")

        def slot_of(name):
            return ring[LOAD[name] % RING]

        def landed_value(n):
            return 16 * (n // RING + 1 - sum(a < n and a % RING == n % RING for a in AHEAD))

        def arrived(eng, name):
            n = LOAD[name]
            eng.wait_ge(landed[n % RING], landed_value(n))

        def last_use(name):
            kind, layer = name[0], name[1]
            if kind == "ada":
                reads = [(ada_read, 12 * layer + 4 * name[2] + name[3] + 1)]
                return reads + ([(ada_read_pool, name[3] + 1)] if name[1:3] == POOL_PART else [])
            if kind == "qkv":
                return [(projected, 2 + UNITS.index((layer, name[2], 0, {2: "kv"}.get(name[2], "q") if layer == 0 else
                                                    "qkv"[name[2] % 3])))]
            if kind == "wo":
                return [(mixed, 4 * layer + 4)]
            part, pairs = name[2] % 6 // 2, PAIRS * layer + name[2] // 6 + 1
            return [((gate_done, up_done, down_done)[part], pairs * (1, 1, 2)[part])]

        def source(name):
            kind, layer = name[0], name[1]
            if kind == "ada":
                part, j = name[2], name[3]
                return ada_w[layer].rearrange("(p k) n -> p k n", k=KD)[:, 2 * j:2 * j + 2,
                                                                     2048 * part:2048 * part + 2048]
            if kind == "qkv":
                w = (a_w_qkv, b_w_qkv)[layer][0].rearrange("(p k) n -> p k n", k=KD)
                at = 512 * name[2]
                if layer == 1:
                    at = 1536 * (name[2] // 3) + 512 * (name[2] % 3)
                return w[:, :, at:at + 512]
            w = (a_w_o, b_w_o)[layer][0].rearrange("(c p) n -> p c n", p=P)
            return w[:, 4 * name[2]:4 * name[2] + 4, :]

        def expert_source(layer, e, part):
            w = (exp_w_gate, exp_w_up, exp_w_down)[part][layer][bass.ds(e, 1)]
            if part == 2:
                return w.rearrange("e (c p) n -> p (e c) n", p=P)
            return w.rearrange("e (p k) f -> p (e k) f", k=KD)

        def as_chunks(t, n):
            return t[:, :].rearrange("p (k n) -> p k n", n=n)

        def rows_of(dram, q):
            return dram.rearrange("(a b c) d -> c b a d", a=S // 16, b=4, c=4)[q]

        def extra_blocks(eng, blocks_here, i, begin, end):
            with eng.If(i > 1):
                with eng.If(blocks_here > i - 2):
                    end()
            with eng.If(blocks_here > i - 1):
                begin()

        def extra_block_count(eng, layer):
            eng.wait_ge(counted, layer + 1)
            return eng.value_load(blk[0:1, layer, 2 * X_BLOCKS:2 * X_BLOCKS + 1], min_val=0, max_val=X_BLOCKS)

        def units_between(group):
            return {k: RUNS[1, group + 1][0][n] for k, n in BETWEEN_1.items()} if group < B_GRPS - 1 else {}

        block = ctx.enter_context(nc.Block())

        @block.sync
        def _(sp):
            def load(name):
                n = LOAD[name]
                if n >= RING:
                    for done in last_use(ORDER[n - RING]):
                        sp.wait_ge(*done)
                t = slot_of(name)
                width = {"ada": 2048, "qkv": 512, "wo": D}[name[0]]
                sp.dma_start(as_chunks(t, width), source(name)).then_inc(landed[n % RING], 16)

            def load_experts(layer):
                base = LOAD[("moe", layer, 0)]

                def load_piece(i, j):
                    n = base + j
                    sp.dma_start(as_chunks(ring[n % RING], D if j // 2 == 2 else F),
                                 expert_source(layer, i * 2 + j % 2, j // 2))\
                      .then_inc(landed[n % RING], 16)

                def wait_for(i, j):
                    done, value = last_use(ORDER[base + j])[0]
                    per = 1 + j // 4
                    sp.wait_ge(done, i * per + value)

                for j in range(6):
                    if j == (0, 5)[layer]:
                        sp.wait_ge(o_turned, (4, 6)[layer])
                        for b in range(2):
                            sp.dma_start(as_chunks(gates_1[b], F), expert_source(layer, 2 + b, 0)).then_inc(gates_ahead, 16)
                    for done in last_use(ORDER[base + j - RING]):
                        sp.wait_ge(*done)
                    load_piece(0, j)
                for j in (0, 1):
                    wait_for(0, j)
                    load_piece(2, j)
                for j in range(2, 6):
                    wait_for(0, j)
                    load_piece(1, j)
                with sp.Fori(2, PAIRS - 1) as i:
                    for j in range(2, 6):
                        wait_for(i - 1, j)
                        load_piece(i, j)
                    for j in (0, 1):
                        wait_for(i, j)
                        load_piece(i + 1, j)
                for j in range(2, 6):
                    wait_for(PAIRS - 2, j)
                    load_piece(PAIRS - 1, j)

            sp.dma_start(cc[:, :], c[0].rearrange("(p k) -> p k", k=KD)).then_inc(s_c, 16)
            for q in range(4):
                sp.dma_start(xs[64 * (q % 2):64 * (q % 2) + 64, q // 2, :], rows_of(x[0], q)).then_inc(s_x, 16)
            sp.dma_start(cst[:, :], const).then_inc(s_const, 16)
            for n in range(LOAD[("moe", 0, 0)]):
                load(ORDER[n])
                if ORDER[n] == ("qkv", 0, 1):
                    sp.dma_start(msk, mask).then_inc(s_mask, 16)
            load_experts(0)
            for n in range(LOAD[("qkv", 1, 0)], LOAD[("moe", 1, 0)]):
                load(ORDER[n])
            load_experts(1)
            for q in range(4):
                sp.wait_ge((out_dve, out_act)[q // 2], 1)
                sp.dma_start(rows_of(out[0], q), yacc[64 * (q % 2):64 * (q % 2) + 64, q // 2, :])\
                  .then_inc(s_out, 16)
            sp.wait_ge(s_out, 64)

        @block.scalar
        def _(act):
            act.wait_ge(s_c, 16)
            act.activation(ct[:, 0], cc[:, :], ACT.Exp, scale=-1.0).then_inc(c_exp, 1)
            pos_rows = positions.rearrange("o (a b c) -> c b a o", a=S // 16, b=4, c=4)
            for q in range(4):
                act.dma_start(posi[64 * (q % 2):64 * (q % 2) + 64, q // 2:q // 2 + 1], pos_rows[q],
                              allow_slow_non_contiguous=True).then_inc(s_const, 16)
            for layer in range(2):
                act.dma_start(colb[:, layer], ada_b[layer].rearrange("(v p k) -> p v k", v=6, k=KD))\
                   .then_inc(s_misc, 16)
                act.dma_start(colg[:, layer, 0], norm_mix_g[layer].rearrange("(p k) -> p k", k=KD)).then_inc(s_misc, 16)
                act.dma_start(colg[:, layer, 1], norm_ffn_g[layer].rearrange("(p k) -> p k", k=KD)).then_inc(s_misc, 16)
            act.dma_start(rw[:, :, :], router_w.rearrange("(p k) e -> p k e", k=KD)).then_inc(s_misc, 16)
            act.dma_start(rbias[:, :], router_bias.partition_broadcast(P)).then_inc(s_misc, 16)
            act.dma_start(sink[:, :], a_sink[0].partition_broadcast(P)).then_inc(s_misc, 16)

            def gate_bias(layer, vector):
                act.dma_start(bias_b[:, :], ada_b[layer, D * vector:D * vector + D].partition_broadcast(P))\
                   .then_inc(s_bias, 16)
            gate_bias(0, 2)

            def rotary_tables():
                act.wait_ge(angles, 2)
                for t in range(NT):
                    cols = slice(t * HALF, (t + 1) * HALF)
                    act.activation(cos2[:, t, 0:HALF], ang[:, cols], ACT.Sin).then_inc(tables, 1)
                    act.activation(cos2[:, t, HALF:HD], ang[:, cols], ACT.Sin).then_inc(tables, 1)
                    act.activation(sin2[:, t, HALF:HD], turns[:, cols], ACT.Sin).then_inc(tables, 1)
                    act.activation(sin2[:, t, 0:HALF], turns[:, cols], ACT.Sin, scale=-1.0).then_inc(tables, 1)

            def fetch_sqrt():
                act.activation(std[:, :], ones[:, 0:NT], ACT.Sqrt)

            def norm(n):
                if n > 0:
                    fetch_sqrt()
                for t in range(NT):
                    if n == 0:
                        act.wait_ge(s_x, 64)
                    else:
                        act.wait_ge(x_updated, 2 * n + t - 1)
                    act.activation(junk[:, t], xs[:, t], ACT.Square, accum_out=ss[:, t:t + 1]).then_inc(squared, 1)
                act.wait_ge(var_ready, n + 1)
                act.activation(std[:, :], ss[:, :], ACT.Sqrt).then_inc(std_ready, 1)

            def modulate(layer):
                act.wait_ge(mod_read, PIECES[layer, 0] + 1)
                for b in (1, 3):
                    act.wait_ge(xn_turned, 4 * layer + b + 1)
                    for k in (2 * b, 2 * b + 1):
                        act.activation(hT[:, k, :], ps[:, b, (k % 2) * S:(k % 2 + 1) * S], ACT.Identity,
                                       bias=colm[:, layer, 1, k:k + 1], scale=colm[:, layer, 0, k:k + 1])\
                           .then_inc(hT_act, 1)

            def norm_before_ffn(layer):
                n = 2 * layer + 1
                fetch_sqrt()
                for t in range(NT):
                    act.wait_ge(x_updated, 2 * n + t - 1)
                    act.activation(junk[:, t], xs[:, t], ACT.Square, accum_out=ss[:, t:t + 1]).then_inc(squared, 1)
                    if t == 0:
                        for b in range(2):
                            act.wait_ge(x_turned, 4 * layer + b + 1)
                            act.activation(xT[:, 4 * b:4 * b + 4, 0:P], ps[:, b, :].rearrange("p (k t) -> p k t", t=P),
                                           ACT.Copy).then_inc(xT_act, 1)
                act.wait_ge(var_ready, n + 1)
                act.activation(std[:, :], ss[:, :], ACT.Sqrt).then_inc(std_ready, 1)

            def copy_v(u):
                layer, chunk, t, kind = UNITS[u]
                vv = qkv_of(layer, chunk // 3)[2]
                act.wait_ge(projected, u + 1)
                if kind == "kv":
                    act.wait_ge(rope_read, ropes_before(u) + 1)
                    src, dst = ps[:, 6 + u % 2, 256:512], vv[:, t, 0:256]
                else:
                    src, dst = ps[:, 6 + u % 2, :], vv[:, t, :]
                act.activation(dst, src, ACT.Copy).then_inc(v_copied, 1)

            def copy_qk(u):
                layer, chunk, t, kind = UNITS[u]
                qT, kT, _ = qkv_of(layer, chunk // 3)
                r = ropes_before(u)
                act.wait_ge(qk_turned, r + 1)
                if kind == "q":
                    first = 4 * chunk if layer == 0 else 0
                    dst = qT[:, first:first + 4, t * P:(t + 1) * P]
                else:
                    dst = kT[:, :, t * P:(t + 1) * P]
                act.activation(dst, qk_bank.rearrange("p (c t) -> p c t", t=P), ACT.Copy).then_inc(qk_copied, 1)

            def unit(u):
                if "v" in UNITS[u][3]:
                    copy_v(u)
                if u % 6 and u not in BETWEEN_0.values() and UNITS[u - 1][3] != "v":
                    copy_qk(u - 1)
                if u == 3:
                    copy_qk(u)

            def copy_pT(s):
                narrow = HEADS[s][3]
                act.wait_ge(p_turned, s + 1)
                if s >= 2:
                    act.wait_ge(pv_done, s - 1)
                n = S if narrow else 2 * S
                act.activation(pT[s % 2][:, 0:n], p_bank[s % 2][:, 0:n], ACT.Copy).then_inc(pT_copied, 1)

            def next_gate_bias(layer):
                act.wait_ge(mod_read, PIECES[layer, 1] + 3)
                gate_bias(layer, 5)

            def heads(steps, between, side):
                for s in steps:
                    layer, group, h, narrow = HEADS[s]
                    width = P if narrow else S
                    col = group * B_HEADS + h
                    if s - steps[0] in side:
                        side[s - steps[0]]()
                    if s >= steps[0] + 2:
                        copy_pT(s - 2)
                    act.wait_ge(negmax, s + 1)
                    m = s % 2
                    if s >= 2:
                        act.wait_ge(p_turned, s - 1)
                    for t in range(NT):
                        act.activation(pr[m][:, t * width:(t + 1) * width], sm[m][:, t * width:(t + 1) * width],
                                       ACT.Exp, bias=nm[:, col, t:t + 1], accum_out=den[:, col, t:t + 1])\
                           .then_inc(exped, 1)
                    if layer == 0:
                        act.activation(esk[:, h, :], nm[:, col, :], ACT.Exp, bias=sink[:, h:h + 1])\
                           .then_inc(sink_exped, 1)
                    if s - steps[0] in between:
                        unit(between[s - steps[0]])
                copy_pT(steps[-2])
                copy_pT(steps[-1])

            def copy_oT(layer, b):
                act.wait_ge(o_turned, (0, 4)[layer] + b + 1)
                act.activation(oT[:, 2 * b:2 * b + 2, :], ps[:, oT_bank(layer, b), :].rearrange("p (c t) -> p c t", t=S),
                               ACT.Copy).then_inc(oT_act, 1)

            def experts(layer):
                act.wait_ge(logits_scaled, layer + 1)
                act.activation(rt[:, 0], rt[:, 9], ACT.Exp, scale=-1.0).then_inc(logits_exped, 1)
                q0 = PAIRS * layer
                blocks_here = extra_block_count(act, layer)

                def pair(i, first):
                    act.wait_ge(gate_done, i + (q0 + 1))
                    act.activation(eg[:, :], ps[:, 2, :], ACT.Exp, scale=-1.0).then_inc(gate_exped, 1)
                    act.wait_ge(a_turned, i + (q0 + 1))
                    act.activation(aT[:, :, :].rearrange("p f s -> p (f s)"), ps[:, 2, :], ACT.Copy).then_inc(aT_ready, 1)
                    if not first:
                        act.wait_ge(scattered, i * 4 + 4 * q0)
                    for h in range(2):
                        act.wait_ge(down_done, i * 2 + (2 * q0 + h + 1))
                        act.activation(ye[:, 512 * h:512 * h + 512], ps[:, 4 + h, :], ACT.Copy).then_inc(y_copied, 1)
                pair(0, True)
                with act.Fori(1, PAIRS) as i:
                    pair(i, False)
                    extra_blocks(act, blocks_here, i, begin_extra, end_extra)
                with act.If(blocks_here > PAIRS - 2):
                    end_extra()

            blocks = act.alloc_register("act_blocks")
            act.reg_mov(blocks, 1)

            def begin_extra():
                act.wait_ge(e_up, blocks)
                act.activation(x_eg, ps[0:C, 0, :], ACT.Exp, scale=-1.0).then_inc(e_exped, 1)

            def end_extra():
                act.wait_ge(e_turned, blocks)
                act.activation(x_aT, ps[:, 2, 0:KF * C].rearrange("p (f s) -> p f s", s=C), ACT.Copy).then_inc(e_aT, 1)
                act.wait_ge(e_down, blocks)
                act.activation(x_ye[0:C, :], ps[0:C, 4, :], ACT.Copy)
                act.activation(x_ye[C:P, :], ps[C:P, 5, :], ACT.Copy).then_inc(e_y, 1)
                act.reg_add(blocks, blocks, 1)

            norm(0)
            rotary_tables()
            modulate(0)
            for u in RUNS[0, 0][0][:4]:
                unit(u)
            heads(RUNS[0, 0][1], BETWEEN_0, {3: lambda: copy_qk(4), 5: lambda: copy_qk(5), 9: lambda: next_gate_bias(0),
                                             10: lambda: copy_oT(0, 0), 14: lambda: copy_oT(0, 1)})
            copy_oT(0, 2)
            norm_before_ffn(0)
            experts(0)
            norm(2)
            gate_bias(1, 2)
            modulate(1)
            for u in RUNS[1, 0][0]:
                unit(u)
            for g in range(B_GRPS):
                heads(RUNS[1, g][1], units_between(g), {4: lambda: next_gate_bias(1)} if g == 1 else {})
            act.wait_ge(merge_in, 1)
            act.activation(aw[:, 0], aw[:, 0], ACT.Exp, scale=-1.0).then_inc(merge_exped, 1)
            copy_oT(1, 1)
            norm_before_ffn(1)
            experts(1)
            act.wait_ge(a_turned, 2 * PAIRS)
            act.wait_ge(e_added, blocks)
            act.dma_start(bias_b[:, :], final_norm_g.partition_broadcast(P)).then_inc(s_bias, 16)
            norm(4)
            act.wait_ge(rstd_ready, 1)
            act.wait_ge(scaled, 2)
            act.activation(yacc[:, 1], yacc[:, 1], ACT.Copy, scale=rstd[:, 1:2]).then_inc(out_act, 1)

        @block.gpsimd
        def _(pool):
            own = Own(pool, pool_step)
            pool.wait_ge(c_silu, 1)
            for k in range(KD):
                layer, part = POOL_PART
                name = ("ada", layer, part, k // 2)
                w = as_chunks(slot_of(name), 2048)[:, k % 2, D:2 * D]
                if k % 2 == 0:
                    arrived(pool, name)
                if k == 0:
                    ins = pool.tensor_scalar(acc_pool, w, sc[:, 0:1], None, ALU.mult)
                else:
                    own(pool.tensor_scalar(products, w, sc[:, k:k + 1], None, ALU.mult))
                    ins = pool.tensor_tensor(acc_pool, acc_pool, products, ALU.add)
                if k % 2:
                    ins.then_inc(ada_read_pool, 1)
                    pool.wait_ge(ada_read_pool, k // 2 + 1)
                else:
                    own(ins)

            blocks = pool.alloc_register("pool_blocks")
            pool.reg_mov(blocks, 0)
            for layer in range(2):
                if layer == 1:
                    pool.wait_ge(x_updated, 4)
                    pool.dma_start(msk, mask).then_inc(s_mask_again, 16)
                pool.wait_ge(logits, layer + 1)
                for t in range(NT):
                    pool.memset(yacc[:, t], 0.0).then_inc(scatter_free, 1)
                blocks_here = extra_block_count(pool, layer)

                def load_extra(b, first):
                    e = pool.value_load(blk[0:1, layer, bass.ds(b, 1)], min_val=0, max_val=E - 1)
                    if not first:
                        pool.wait_ge(e_a, blocks)
                        pool.reg_add(blocks, blocks, 0)
                    for part, dst in enumerate((x_gate, x_up)):
                        if part == 1 and first:
                            pool.wait_ge(gate_done, PAIRS * layer + 2)
                        pool.dma_start(as_chunks(dst, F), expert_source(layer, e, part)).then_inc(e_landed, 16)
                    if not first:
                        pool.wait_ge(e_y, blocks)
                    pool.reg_add(blocks, blocks, 1)
                    pool.dma_start(as_chunks(x_down, D), expert_source(layer, e, 2)).then_inc(e_landed_down, 16)

                with pool.If(blocks_here > 0):
                    load_extra(0, True)
                with pool.Fori(1, X_BLOCKS) as b:
                    with pool.If(blocks_here > b):
                        load_extra(b, False)

        @block.vector
        def _(dve):
            own = Own(dve, dve_step)
            own(dve.memset(wgt[:, :, :], 0.0))
            dve.memset(slot[:, :, :], -1.0).then_inc(e_added, 1)

            def sign(ins, s, value):
                ins.then_inc(s, 1)
                dve.wait_ge(s, value)

            dve.wait_ge(c_exp, 1)
            own(dve.tensor_scalar(ct[:, 1], ct[:, 0], 1.0, None, ALU.add))
            own(dve.reciprocal(ct[:, 0], ct[:, 1]))
            sign(dve.tensor_tensor(sc[:, :], cc[:, :], ct[:, 0], ALU.mult), c_silu, 1)

            def rotary_angles():
                dve.wait_ge(s_const, 80)
                own(dve.tensor_copy(posf[:, :], posi[:, :]))
                for t in range(NT):
                    own(dve.tensor_scalar(raw[:, t * HALF:(t + 1) * HALF], cst[:, INVF:INVF + HALF], posf[:, t:t + 1], None,
                                          ALU.mult))
                for dst, lead in ((ang, 0.25), (turns, 0.0)):
                    own(dve.tensor_scalar(k1, raw, 1.0 / (2 * np.pi), lead, ALU.mult, ALU.add))
                    own(dve.tensor_scalar(k2, k1, ROUND, None, ALU.add))
                    own(dve.tensor_scalar(k1, k2, ROUND, None, ALU.subtract))
                    own(dve.scalar_tensor_tensor(dst, k1, -TWO_PI_HI, raw, ALU.mult, ALU.add))
                    own(dve.scalar_tensor_tensor(k2, k1, -TWO_PI_MID, dst, ALU.mult, ALU.add))
                    own(dve.scalar_tensor_tensor(dst, k1, -TWO_PI_LO, k2, ALU.mult, ALU.add))
                    own(dve.tensor_scalar(k2, dst, lead * 2 * np.pi, PI_SAFE, ALU.add, ALU.min))
                    dve.tensor_scalar(dst, k2, -PI_SAFE, None, ALU.max).then_inc(angles, 1)

            def ada(layer, part, k):
                name = ("ada", layer, part, k // 2)
                n = 2048 if (layer, part) != POOL_PART else D
                w = as_chunks(slot_of(name), 2048)[:, k % 2, 0:n]
                if k % 2 == 0:
                    arrived(dve, name)
                acc_k = acc[:, 0:n]
                if k == 0:
                    if (layer, part) != (0, 0):
                        dve.wait_ge(mod_out, PIECES[POOL_PART] + 1 if (layer, part) == (1, 0) else PIECES[layer, part])
                    ins = dve.tensor_scalar(acc_k, w, sc[:, 0:1], None, ALU.mult)
                else:
                    ins = dve.scalar_tensor_tensor(acc_k, w, sc[:, k:k + 1], acc_k, ALU.mult, ALU.add)
                if k % 2:
                    sign(ins, ada_read, 12 * layer + 4 * part + k // 2 + 1)
                else:
                    own(ins)

            def mod(layer, part):
                n = PIECES[layer, part]
                dve.wait_ge(mod_out, n + 1)
                if n == 0:
                    dve.wait_ge(s_misc, 144)
                b = ps[:, mod_bank(layer, part, 0), :]
                if part == 0:
                    own(dve.tensor_tensor(colt[:, :], b[:, KD:2 * KD], colb[:, layer, 1], ALU.add))
                    dve.tensor_tensor(colm[:, layer, 1], b[:, 0:KD], colb[:, layer, 0], ALU.add)
                    sign(dve.scalar_tensor_tensor(colm[:, layer, 0], colt[:, :], 1.0, colg[:, layer, 0], ALU.add,
                                                  ALU.mult), mod_read, n + 1)
                elif part == 1:
                    sign(dve.tensor_tensor(colm[:, layer, 3], b[:, 0:KD], colb[:, layer, 3], ALU.add), mod_read, n + 1)
                else:
                    own(dve.tensor_tensor(colt[:, :], b[:, 0:KD], colb[:, layer, 4], ALU.add))
                    sign(dve.scalar_tensor_tensor(colm[:, layer, 2], colt[:, :], 1.0, colg[:, layer, 1], ALU.add,
                                                  ALU.mult), mod_read, n + 1)

            def gate(layer, part, halves=(0, 1)):
                n = PIECES[layer, part]
                dve.wait_ge(s_bias, 16 * (2 * layer + part))
                for h in halves:
                    dve.wait_ge(mod_out, n + 2 + h)
                    sign(dve.tensor_tensor(gate_b[:, 512 * h:512 * h + 512], ps[:, mod_bank(layer, part, 1 + h), :],
                                           bias_b[:, 512 * h:512 * h + 512], ALU.add), mod_read, n + 2 + h)

            def norm(n):
                dve.wait_ge(squared, 2 * n + 2)
                sign(dve.tensor_scalar(ss[:, :], ss[:, :], 1.0 / D, EPS, ALU.mult, ALU.add), var_ready, n + 1)
                dve.wait_ge(std_ready, n + 1)
                own(dve.reciprocal(rstd[:, :], std[:, :]))

            def normalize():
                for t in range(NT):
                    ins = dve.tensor_scalar(xn[:, t].rearrange("p k n -> p n k"),
                                            xs[:, t].rearrange("p (n k) -> p n k", k=KD), rstd[:, t:t + 1], None, ALU.mult)
                return ins

            def modulate(layer):
                for b in (0, 2):
                    dve.wait_ge(xn_turned, 4 * layer + b + 1)
                    for k in (2 * b, 2 * b + 1):
                        dve.tensor_scalar(hT[:, k, :], ps[:, b, (k % 2) * S:(k % 2 + 1) * S],
                                          colm[:, layer, 0, k:k + 1], colm[:, layer, 1, k:k + 1],
                                          ALU.mult, ALU.add).then_inc(hT_dve, 1)

            def project(units, side):
                for u in units:
                    rope(u)
                    for job in side.get(u - units[0], ()):
                        job()

            def rope(u):
                layer, chunk, t, kind = UNITS[u]
                if kind == "v":
                    return
                if u in (0, 6):
                    dve.wait_ge(xn_turned, 4 if u == 0 else 8)
                r = ropes_before(u)
                n = 256 if kind == "kv" else 512
                hn = n // HD
                b = ps[:, 6 + u % 2, 0:n]
                b3 = b.rearrange("p (h d) -> p h d", d=HD)
                r2 = rope2[:, 0:n].rearrange("p (h d) -> p h d", d=HD)
                dve.wait_ge(projected, u + 1)
                own(dve.tensor_tensor(rope1[:, 0:n].rearrange("p (h d) -> p h d", d=HD), b3,
                                      cos2[:, t].unsqueeze(1).to_broadcast([P, hn, HD]), ALU.mult))
                own(dve.tensor_tensor(r2[:, :, 0:HALF], b3[:, :, HALF:HD],
                                      sin2[:, t, 0:HALF].unsqueeze(1).to_broadcast([P, hn, HALF]), ALU.mult))
                sign(dve.tensor_tensor(r2[:, :, HALF:HD], b3[:, :, 0:HALF],
                                       sin2[:, t, HALF:HD].unsqueeze(1).to_broadcast([P, hn, HALF]), ALU.mult),
                     rope_read, r + 1)
                if r >= 2:
                    dve.wait_ge(qk_turned, r - 1)
                if kind == "kv":
                    dup = roped_sb[r % 2].rearrange("p (j two d) -> p j two d", two=2, d=HD)
                    a, bb = (z[:, 0:n].rearrange("p (j d) -> p j d", d=HD) for z in (rope1, rope2))
                    own(dve.tensor_tensor(dup[:, :, 0], a, bb, ALU.add))
                    sign(dve.tensor_tensor(dup[:, :, 1], a, bb, ALU.add), roped, r + 1)
                else:
                    sign(dve.tensor_tensor(roped_sb[r % 2], rope1, rope2, ALU.add), roped, r + 1)

            def take_o(s):
                layer, group, h, narrow = HEADS[s]
                dve.wait_ge(exped, 2 * s + 2)
                dve.wait_ge(pv_done, s + 1)
                src = o_bank.rearrange("p (t d) -> p t d", d=HD)
                if layer == 0:
                    dve.wait_ge(sink_exped, h + 1)
                    own(dve.tensor_tensor(den[:, h], den[:, h], esk[:, h], ALU.add))
                    own(dve.reciprocal(esk[:, h], den[:, h]))
                    dve.tensor_tensor(oA[:, :, HD * h:HD * h + HD], src,
                                      esk[:, h].unsqueeze(2).to_broadcast([P, NT, HD]), ALU.mult).then_inc(o_copied, 1)
                else:
                    dve.tensor_copy(oB[:, group, :, HD * h:HD * h + HD], src).then_inc(o_copied, 1)

            def heads(steps, between, side):
                for s in steps:
                    layer, group, h, narrow = HEADS[s]
                    width = P if narrow else S
                    col = group * B_HEADS + h
                    m = (M_A if layer == 0 else (M_B0, M_B1, M_B2)[group])
                    dve.wait_ge((s_mask, s_mask_again)[layer], 16)
                    dve.wait_ge(scored, s + 1)
                    sm_s = sm[s % 2]
                    if s >= 2:
                        dve.wait_ge(exped, 2 * (s - 1))
                    sign(dve.scalar_tensor_tensor(sm_s[:, 0:2 * width], score_bank[s % 2][:, 0:2 * width], SCALE,
                                                  msk[:, m:m + 2 * width], ALU.mult, ALU.add), masked, s + 1)
                    own(dve.reduce_max(mx[:, :], sm_s[:, 0:2 * width].rearrange("p (t n) -> p t n", t=NT), AX_X))
                    if layer == 0:
                        dve.tensor_scalar(nm[:, col], mx[:, :], sink[:, h:h + 1], -1.0, ALU.max, ALU.mult).then_inc(negmax, 1)
                    else:
                        dve.tensor_scalar(nm[:, col], mx[:, :], -1.0, None, ALU.mult).then_inc(negmax, 1)
                    if s - steps[0] >= 3:
                        take_o(s - 3)
                    if s - steps[0] in between:
                        rope(between[s - steps[0]])
                    for job in side.get(s - steps[0], ()):
                        job()
                for s in steps[-3:]:
                    take_o(s)

            def mix_out(layer, side=()):
                mod(layer, 2)
                dve.tensor_tensor(rw_gain, rw[:, :, :], colm[:, layer, 2].unsqueeze(2).to_broadcast([P, KD, E]), ALU.mult)
                own(dve.tensor_tensor(rw_shift, rw[:, :, :], colm[:, layer, 3].unsqueeze(2).to_broadcast([P, KD, E]),
                                      ALU.mult))
                dve.reduce_sum(shift_sum, rw_shift.rearrange("p k e -> p e k"), AX_X).then_inc(shift_summed, 1)
                b = (3, 0)[layer]
                dve.wait_ge(o_turned, (0, 4)[layer] + b + 1)
                dve.tensor_copy(oT[:, 2 * b:2 * b + 2, :], ps[:, oT_bank(layer, b), :].rearrange("p (c t) -> p c t", t=S))\
                   .then_inc(oT_dve, 1)
                for job in side:
                    job()
                for n in range(4):
                    t, h = n // 2, n % 2
                    cols = slice(512 * h, 512 * h + 512)
                    tmp = xnf[:, 512 * n:512 * n + 512]
                    dve.wait_ge(mixed, 4 * layer + n + 1)
                    own(dve.tensor_tensor(tmp, ps[:, 4 + n, :], gate_b[:, cols], ALU.mult))
                    ins = dve.tensor_tensor(xs[:, t, cols], xs[:, t, cols], tmp, ALU.add)
                    if h == 1:
                        sign(ins, x_updated, 4 * layer + t + 1)

            def ranks(values, n):
                for j in range(4):
                    cmp = rr[:, j, 0:4 * n].rearrange("p (g i) -> p g i", i=4)
                    one = values[:, :, j:j + 1]
                    if j < 3:
                        dve.tensor_tensor(cmp[:, :, j + 1:4], one.to_broadcast([P, n, 3 - j]), values[:, :, j + 1:4],
                                          ALU.is_ge)
                    ins = dve.tensor_tensor(cmp[:, :, 0:j + 1], one.to_broadcast([P, n, j + 1]), values[:, :, 0:j + 1],
                                            ALU.is_gt)
                own(ins)
                own(dve.tensor_tensor(rr[:, 0:2, 0:4 * n], rr[:, 0:2, 0:4 * n], rr[:, 2:4, 0:4 * n], ALU.add))
                own(dve.tensor_tensor(rr[:, 0, 0:4 * n], rr[:, 0, 0:4 * n], rr[:, 1, 0:4 * n], ALU.add))

            def route(layer):
                scores, biased, hi, lo, m1, m2, g_score, g_sel, wsel = (rt[:, j] for j in range(1, 10))
                dve.wait_ge(logits, layer + 1)
                own(dve.tensor_copy(shift_row, ps[:, 4, NT * E:NT * E + E]))
                for t in range(NT):
                    ins = dve.scalar_tensor_tensor(wsel[:, t * E:(t + 1) * E], ps[:, 4, t * E:(t + 1) * E], rstd[:, t:t + 1],
                                                   shift_row, ALU.mult, ALU.add)
                ins.then_inc(logits_scaled, 1)
                dve.wait_ge(logits_exped, layer + 1)
                own(dve.tensor_scalar(biased, rt[:, 0], 1.0, None, ALU.add))
                own(dve.reciprocal(scores, biased))
                own(dve.tensor_tensor(biased.rearrange("p (t e) -> p t e", t=NT),
                                      scores.rearrange("p (t e) -> p t e", t=NT),
                                      rbias[:, :].unsqueeze(1).to_broadcast([P, NT, E]), ALU.add))
                b4 = biased.rearrange("p (g i) -> p g i", i=4)
                pair = biased.rearrange("p (m two) -> p m two", two=2)
                dve.tensor_tensor(hi[:, 0:16], pair[:, :, 0], pair[:, :, 1], ALU.max)
                own(dve.tensor_tensor(lo[:, 0:16], pair[:, :, 0], pair[:, :, 1], ALU.min))
                h2, l2 = (z[:, 0:16].rearrange("p (g two) -> p g two", two=2) for z in (hi, lo))
                dve.tensor_tensor(m1[:, 0:8], h2[:, :, 0], h2[:, :, 1], ALU.max)
                dve.tensor_tensor(m2[:, 0:8], h2[:, :, 0], h2[:, :, 1], ALU.min)
                own(dve.tensor_tensor(m2[:, 8:16], l2[:, :, 0], l2[:, :, 1], ALU.max))
                own(dve.tensor_tensor(m2[:, 16:24], m2[:, 0:8], m2[:, 8:16], ALU.max))
                own(dve.tensor_tensor(g_score[:, 0:8], m1[:, 0:8], m2[:, 16:24], ALU.add))
                ranks(g_score[:, 0:8].rearrange("p (t g) -> p t g", g=4), NT)
                own(dve.tensor_scalar(g_sel[:, 0:8], rr[:, 0, 0:8], 0.5, None, ALU.is_lt))
                ranks(b4, 8)
                s3 = sel[:, :, :].rearrange("p t (g i) -> p (t g) i", i=4)
                sign(dve.scalar_tensor_tensor(s3, rr[:, 0, :].rearrange("p (g i) -> p g i", i=4), 1.5,
                                             g_sel[:, 0:8].unsqueeze(2).to_broadcast([P, 8, 4]), ALU.is_lt, ALU.mult),
                     routed, layer + 1)
                w3 = wsel.rearrange("p (t e) -> p t e", t=NT)
                own(dve.tensor_tensor(w3, scores.rearrange("p (t e) -> p t e", t=NT), sel[:, :, :], ALU.mult))
                own(dve.reduce_sum(m1[:, 0:NT], w3, AX_X))
                own(dve.reciprocal(m2[:, 0:NT], m1[:, 0:NT]))
                own(dve.tensor_tensor(wgt[:, :, 0:E], w3, m2[:, 0:NT].unsqueeze(2).to_broadcast([P, NT, E]), ALU.mult))
                gate(layer, 2)
                if layer == 0:
                    mod(1, 0)
                dve.wait_ge(ranked, layer + 1)
                own(dve.scalar_tensor_tensor(slot_raw[:, :, :], ps[:, 5, 0:NT * E].rearrange("p (t e) -> p t e", t=NT), 1.0,
                                             sel[:, :, :], ALU.add, ALU.mult))
                own(dve.tensor_scalar(slot[:, :, 0:E], slot_raw[:, :, :], -1.0, None, ALU.add))

            def list_extra_blocks(layer):
                x1, x2, more, s1, s2, s3 = (xb[:, j, 8:8 + E] for j in range(6))
                tokens = ps[:, 5, NT * E:NT * E + E]
                own(dve.memset(xb[:, :, :], 0.0))
                own(dve.tensor_scalar(x1, tokens, float(C), None, ALU.is_gt))
                own(dve.scalar_tensor_tensor(x2, tokens, 2.0 * C, x1, ALU.is_gt, ALU.add))
                own(dve.scalar_tensor_tensor(more, tokens, 3.0 * C, x2, ALU.is_gt, ALU.add))
                at = 2
                for shift, to in ((1, 3), (2, 4), (4, 3), (8, 4)):
                    own(dve.tensor_tensor(xb[:, to, 8:8 + E], xb[:, at, 8:8 + E], xb[:, at, 8 - shift:8 + E - shift], ALU.add))
                    at = to
                up_to = xb[:, at, 8:8 + E].unsqueeze(1).to_broadcast([P, X_BLOCKS, E])
                number = cst[:, IOTA:IOTA + X_BLOCKS]
                past, before = (xcmp[:, j].rearrange("p (b e) -> p b e", e=E) for j in range(2))
                own(dve.tensor_tensor(past, up_to, number.unsqueeze(2).to_broadcast([P, X_BLOCKS, E]), ALU.is_le))
                own(dve.reduce_sum(xsum[:, 0], past, AX_X))
                own(dve.tensor_tensor(before, past, more.unsqueeze(1).to_broadcast([P, X_BLOCKS, E]), ALU.mult))
                own(dve.reduce_sum(xsum[:, 1], before, AX_X))
                own(dve.tensor_tensor(xsum[:, 2], number, xsum[:, 1], ALU.subtract))
                own(dve.tensor_scalar(xsum[:, 3], xsum[:, 2], 1.0, float(C), ALU.add, ALU.mult))
                own(dve.tensor_copy(blk[:, layer, 0:X_BLOCKS], xsum[:, 0]))
                own(dve.tensor_copy(blk[:, layer, X_BLOCKS:2 * X_BLOCKS], xsum[:, 3]))
                sign(dve.tensor_copy(blk[:, layer, 2 * X_BLOCKS:2 * X_BLOCKS + 1], xb[:, at, 7 + E:8 + E]), counted, layer + 1)

            def mark(out, slots, e, weight=None):
                for t in range(NT):
                    column = slot[:, t, bass.ds(e, 1)]
                    if weight is None:
                        ins = dve.tensor_scalar(out[:, t], slots, column, None, ALU.is_equal)
                    else:
                        ins = dve.tensor_scalar(out[:, t], slots, column, weight[:, t, bass.ds(e, 1)], ALU.is_equal, ALU.mult)
                return ins

            def mark_pair(out, first, weight=None):
                for b in range(2):
                    ins = mark(out[:, :, C * b:C * b + C], cst[:, IOTA:IOTA + C], first + b, weight)
                return ins

            def modulate_gather(layer, n):
                for b in range(2):
                    dve.wait_ge(gathered, n * 2 + (b - 1))
                    g3 = ps[:, b, :].rearrange("p (k s) -> p k s", s=P)
                    part = xg[:, 4 * b:4 * b + 4, :]
                    own(dve.tensor_tensor(part, g3, colm[:, layer, 2, 4 * b:4 * b + 4].unsqueeze(2).to_broadcast([P, 4, P]),
                                          ALU.mult))
                    ins = dve.tensor_tensor(part, part, colm[:, layer, 3, 4 * b:4 * b + 4].unsqueeze(2)
                                            .to_broadcast([P, 4, P]), ALU.add)
                ins.then_inc(xg_ready, 1)

            def add_scattered(q):
                for n in range(4):
                    t, h = n % 2, n // 2
                    y = yacc[:, t, 512 * h:512 * h + 512]
                    dve.wait_ge(scattered, q * 4 + (n + 1))
                    dve.tensor_tensor(y, y, ps[:, 6 + n % 2, :], ALU.add).then_inc(scatter_free, 1)

            def experts(layer):
                q0, g0 = PAIRS * layer, GATHERS * layer
                mark_pair(pick, 0).then_inc(picked, 1)
                list_extra_blocks(layer)
                modulate_gather(layer, g0 + 1)
                dve.wait_ge(scatter_free, 4 * q0 + 2)
                blocks_here = extra_block_count(dve, layer)

                def pair(i, first):
                    mark_pair(pick, i * 2 + 2).then_inc(picked, 1)
                    mark_pair(pw, i * 2, wgt).then_inc(pw_ready, 1)
                    dve.wait_ge(gate_exped, i + (q0 + 1))
                    own(dve.tensor_scalar(sg[:, :], eg[:, :], 1.0, None, ALU.add))
                    own(dve.reciprocal(eg[:, :], sg[:, :]))
                    own(dve.tensor_tensor(sg[:, :], ps[:, 2, :], eg[:, :], ALU.mult))
                    dve.wait_ge(up_done, i + (q0 + 1))
                    dve.tensor_tensor(sg[:, :], ps[:, 3, :], sg[:, :], ALU.mult).then_inc(a_ready, 1)
                    if not first:
                        add_scattered(i + (q0 - 1))
                    dve.wait_ge(pw_turned, i + (q0 + 1))
                    dve.tensor_copy(pwT[:, :], ps[:, 3, 0:S]).then_inc(pwT_ready, 1)
                    modulate_gather(layer, i + (g0 + 2))

                pair(0, True)
                static = own.n
                per = 2 + 3
                with dve.Fori(1, PAIRS) as i:
                    own.turn = (i - 1) * per
                    pair(i, False)
                    assert own.n - static == per
                    extra_blocks(dve, blocks_here, i, lambda: begin_extra(layer, i - 1), end_extra)
                with dve.If(blocks_here > PAIRS - 2):
                    end_extra()
                own.turn = 0
                own.n = static + per * (PAIRS - 1)

            blocks = dve.alloc_register("dve_blocks")
            steps = dve.alloc_register("dve_steps")
            dve.reg_mov(blocks, 1)
            dve.reg_mov(steps, 0)

            def begin_extra(layer, b):
                def link(ins):
                    ins.then_inc(e_dve, 1)
                    dve.reg_add(steps, steps, 1)
                    dve.wait_ge(e_dve, steps)
                e = dve.value_load(blk[0:1, layer, bass.ds(b, 1)], min_val=0, max_val=E - 1)
                start = dve.value_load(blk[0:1, layer, bass.ds(b + X_BLOCKS, 1)], min_val=C, max_val=S - C)
                slots = cst[:, bass.ds(start + IOTA, C)]
                mark(pick[:, :, 0:C], slots, e)
                for half in range(2):
                    ins = mark(pw[:, :, C * half:C * half + C], slots, e, wgt)
                ins.then_inc(e_picked, 1)
                dve.wait_ge(e_gathered, blocks)
                g3 = ps[:, 0, :].rearrange("p (k s) -> p k s", s=C)
                link(dve.tensor_tensor(x_xg[:, :, :], g3, colm[:, layer, 2].unsqueeze(2).to_broadcast([P, KD, C]), ALU.mult))
                link(dve.tensor_tensor(x_xg[:, :, :], x_xg[:, :, :],
                                       colm[:, layer, 3].unsqueeze(2).to_broadcast([P, KD, C]), ALU.add))
                dve.tensor_copy(x_pwT[:, :], ps[:, 3, 0:S]).then_inc(e_xg, 1)
                dve.wait_ge(e_exped, blocks)
                link(dve.tensor_scalar(x_sg, x_eg, 1.0, None, ALU.add))
                link(dve.reciprocal(x_eg, x_sg))
                link(dve.tensor_tensor(x_sg, ps[0:C, 0, :], x_eg, ALU.mult))
                dve.tensor_tensor(x_sg, ps[C:P, 1, :], x_sg, ALU.mult).then_inc(e_a, 1)

            def end_extra():
                dve.wait_ge(e_scattered, blocks)
                for n in range(4):
                    t, h = n // 2, n % 2
                    y = yacc[:, t, 512 * h:512 * h + 512]
                    ins = dve.tensor_tensor(y, y, ps[:, (6, 7, 0, 1)[n], :], ALU.add)
                ins.then_inc(e_added, 1)
                dve.reg_add(blocks, blocks, 1)

            def ffn_out(layer):
                dve.wait_ge(e_added, blocks)
                own(dve.tensor_tensor(yacc[:, 0], yacc[:, 0], gate_b[:, :], ALU.mult))
                dve.tensor_tensor(xs[:, 0], xs[:, 0], yacc[:, 0], ALU.add)
                own(dve.tensor_tensor(yacc[:, 1], yacc[:, 1], gate_b[:, :], ALU.mult))
                own(dve.tensor_tensor(xs[:, 1], xs[:, 1], yacc[:, 1], ALU.add))
                q = PAIRS * (layer + 1) - 1
                for n in range(4):
                    t, h = n % 2, n // 2
                    cols = slice(512 * h, 512 * h + 512)
                    dve.wait_ge(scattered, q * 4 + n + 1)
                    y = yacc[:, t, cols]
                    own(dve.tensor_tensor(y, ps[:, 6 + n % 2, :], gate_b[:, cols], ALU.mult))
                    ins = dve.tensor_tensor(xs[:, t, cols], xs[:, t, cols], y, ALU.add)
                    if h == 0:
                        ins.then_inc(scatter_free, 1)
                    else:
                        sign(ins, x_updated, 4 * layer + t + 3)

            def ffn(layer):
                n = 2 * layer + 1
                for b in range(2):
                    dve.wait_ge(x_turned, 4 * layer + b + 3)
                    dve.tensor_copy(xT[:, 4 * b:4 * b + 4, P:S], ps[:, 2 + b, :].rearrange("p (k t) -> p k t", t=P))\
                       .then_inc(xT_dve, 1)
                norm(n)
                normalize()
                route(layer)
                experts(layer)
                ffn_out(layer)

            def ada_jobs(layer, part, *ks):
                return [lambda k=k: ada(layer, part, k) for k in ks]

            ada(0, 0, 0)
            ada(0, 0, 1)
            norm(0)
            normalize().then_inc(xn_ready, 1)
            rotary_angles()
            for k in range(2, KD):
                ada(0, 0, k)
            mod(0, 0)
            modulate(0)
            dve.wait_ge(tables, 8)
            project(RUNS[0, 0][0][:4], {1: ada_jobs(0, 1, 0, 1), 2: ada_jobs(0, 1, 2, 3),
                                        3: ada_jobs(0, 1, 4, 5, 6)})
            side = {0: ada_jobs(0, 1, 7)}
            side.update({5: [lambda: mod(0, 1)], 6: [lambda: gate(0, 1, (0,))], 7: [lambda: gate(0, 1, (1,))]})
            side.update({8 + k: ada_jobs(0, 2, k) for k in range(KD)})
            heads(RUNS[0, 0][1], BETWEEN_0, side)
            mix_out(0, ada_jobs(1, 0, *range(KD)))
            ffn(0)
            norm(2)
            normalize().then_inc(xn_ready, 1)
            modulate(1)
            project(RUNS[1, 0][0], {n + 2: ada_jobs(1, 1, n) for n in range(4)})
            jobs = {step: ada_jobs(1, 1, 4 + n) for n, step in enumerate((1, 3, 4, 5))}
            jobs[7] = [lambda: mod(1, 1), lambda: gate(1, 1, (0,))]
            heads(RUNS[1, 0][1], units_between(0), jobs)
            gate(1, 1, (1,))
            heads(RUNS[1, 1][1], units_between(1), {n: ada_jobs(1, 2, n) for n in range(KD)})
            heads(RUNS[1, 2][1], {}, {})

            def grp(v, g):
                return v[:, g * B_HEADS:(g + 1) * B_HEADS, :]
            least, z = aw[:, 1, 0:B_HEADS], aw[:, 1, B_HEADS:2 * B_HEADS]
            own(dve.tensor_tensor(z, grp(nm, 0), grp(nm, 1), ALU.min))
            own(dve.tensor_tensor(least, z, grp(nm, 2), ALU.min))
            for g in range(B_GRPS):
                ins = dve.tensor_tensor(grp(aw[:, 0], g), grp(nm, g), least, ALU.subtract)
                if g < 2:
                    own(ins)
            sign(ins, merge_in, 1)
            dve.wait_ge(merge_exped, 1)
            own(dve.tensor_tensor(aw[:, 2], aw[:, 0], den[:, :, :], ALU.mult))
            own(dve.tensor_tensor(z, grp(aw[:, 2], 0), grp(aw[:, 2], 1), ALU.add))
            own(dve.tensor_tensor(least, z, grp(aw[:, 2], 2), ALU.add))
            own(dve.reciprocal(z, least))
            for g in range(B_GRPS):
                ins = dve.tensor_tensor(grp(aw[:, 2], g), grp(aw[:, 0], g), z, ALU.mult)
            own(ins)
            dve.wait_ge(o_copied, len(HEADS))
            for t in range(NT):
                for g in range(B_GRPS):
                    o = oB[:, g, t].rearrange("p (h d) -> p h d", d=HD)
                    ins = dve.tensor_tensor(o, o, grp(aw[:, 2], g)[:, :, t:t + 1].to_broadcast([P, B_HEADS, HD]), ALU.mult)
                own(ins)
                own(dve.tensor_tensor(oB[:, 0, t], oB[:, 0, t], oB[:, 1, t], ALU.add))
                dve.tensor_tensor(oB[:, 0, t], oB[:, 0, t], oB[:, 2, t], ALU.add).then_inc(o_ready, 1)

            mix_out(1)
            ffn(1)
            dve.wait_ge(s_bias, 80)
            for t in range(NT):
                ins = dve.tensor_tensor(yacc[:, t], xs[:, t], bias_b[:, :], ALU.mult)
                ins.then_inc(scaled, 1)
            dve.wait_ge(squared, 10)
            sign(dve.tensor_scalar(ss[:, :], ss[:, :], 1.0 / D, EPS, ALU.mult, ALU.add), var_ready, 5)
            dve.wait_ge(std_ready, 5)
            sign(dve.reciprocal(rstd[:, :], std[:, :]), rstd_ready, 1)
            dve.wait_ge(scaled, 1)
            dve.tensor_scalar(yacc[:, 0], yacc[:, 0], rstd[:, 0:1], None, ALU.mult).then_inc(out_dve, 1)

        @block.tensor
        def _(pe):
            def mod(layer, part, piece):
                n = PIECES[layer, part]
                sums = acc[:, :]
                b = ps[:, mod_bank(layer, part, piece), :]
                if piece == 0:
                    pe.wait_ge(ada_read, 12 * layer + 4 * part + 4)
                if n + piece >= 1 and (layer, part) != (1, 0) and (part, piece) != (2, 2):
                    pe.wait_ge(mod_read, n + piece)
                if piece == 0:
                    at = {0: 0, 1: D, 2: 0}[part]
                    for j in range(2 if part == 0 else 1):
                        v = sums[:, at + D * j:at + D * j + D].rearrange("p (n k) -> p n k", k=KD)
                        for k in range(KD):
                            ins = pe.matmul(b[:, KD * j + k:KD * j + k + 1], v[:, :, k], ones[:, 0:1], start=True, stop=True)
                else:
                    at = {1: 0, 2: D}[part] + 512 * (piece - 1)
                    if (layer, part) == POOL_PART:
                        pe.wait_ge(ada_read_pool, 4)
                        sums, at = acc_pool, at - D
                    ins = pe.matmul(b, ones, sums[:, at:at + 512], start=True, stop=True)
                ins.then_inc(mod_out, 1)

            def turn_xn(n):
                for b in range(4):
                    if b == 0:
                        pe.wait_ge(xn_ready, n + 1)
                    for k in (2 * b, 2 * b + 1):
                        for t in range(NT):
                            ins = pe.transpose(ps[:, b, (k % 2) * S + t * P:(k % 2) * S + (t + 1) * P], xn[:, t, k, :], ident)
                    ins.then_inc(xn_turned, 1)

            def turn_x(layer, t):
                pe.wait_ge(x_updated, 4 * layer + t + 1)
                x3 = xs[:, t].rearrange("p (n k) -> p n k", k=KD)
                for k in range(KD):
                    ins = pe.transpose(ps[:, 2 * t + k // 4, (k % 4) * P:(k % 4 + 1) * P], x3[:, :, k], ident)
                    if k % 4 == 3:
                        ins.then_inc(x_turned, 1)

            def router_products(t):
                for k in range(KD):
                    ins = pe.matmul(ps[:, 4, t * E:(t + 1) * E], xT[:, k, t * P:(t + 1) * P], rw_gain[:, k, :], start=k == 0,
                                    stop=k == KD - 1)
                return ins

            def turn(u):
                if UNITS[u][3] == "v":
                    return
                r = ropes_before(u)
                pe.wait_ge(roped, r + 1)
                if u == RUNS[1, 2][0][0]:
                    pe.wait_ge(mod_read, PIECES[1, 1] + 3)
                if r:
                    pe.wait_ge(qk_copied, r)
                for m in range(4):
                    ins = pe.transpose(qk_bank[:, m * P:(m + 1) * P], roped_sb[r % 2][:, m * P:(m + 1) * P], ident)
                ins.then_inc(qk_turned, 1)

            def unit(u):
                layer, chunk, t, kind = UNITS[u]
                name = ("qkv", layer, chunk)
                if t == 0:
                    arrived(pe, name)
                if u >= 2:
                    pe.wait_ge(rope_read, ropes_before(u - 1))
                    if v_copies_before(u - 1):
                        pe.wait_ge(v_copied, v_copies_before(u - 1))
                w = as_chunks(slot_of(name), 512)
                for k in range(KD):
                    ins = pe.matmul(ps[:, 6 + u % 2, :], hT[:, k, t * P:(t + 1) * P], w[:, k, :], start=k == 0,
                                    stop=k == KD - 1)
                ins.then_inc(projected, 1)
                if u % 6 and u not in BETWEEN_0.values():
                    turn(u - 1)
                if u == 3:
                    turn(u)

            def score(s):
                layer, group, h, narrow = HEADS[s]
                qT, kT, _ = qkv_of(layer, group)
                rows = slice(HD * (h % 2), HD * (h % 2) + HD)
                kc = h // 4 if layer == 0 else h // 2
                if h == 0:
                    last = RUNS[layer, group][0][3 if layer == 0 else 5]
                    pe.wait_ge(qk_copied, ropes_before(last + 1))
                    pe.wait_ge(v_copied, v_copies_before(last + 1))
                if (layer, h) == (0, A_HEADS // 2):
                    pe.wait_ge(qk_copied, 6)
                if s >= 2:
                    pe.wait_ge(masked, s - 1)
                for t in range(NT):
                    q = qT[rows, h // 2, t * P:(t + 1) * P]
                    keys = kT[rows, kc, t * P:(t + 1) * P] if narrow else kT[rows, kc, :]
                    n = P if narrow else S
                    ins = pe.matmul(score_bank[s % 2][:, t * n:(t + 1) * n], q, keys, start=True, stop=True)
                ins.then_inc(scored, 1)

            def turn_p(s):
                narrow = HEADS[s][3]
                pe.wait_ge(exped, 2 * s + 2)
                if s >= 2:
                    pe.wait_ge(pT_copied, s - 1)
                probs = pr[s % 2]
                for t in range(NT):
                    for kt in range(1 if narrow else NT):
                        src = probs[:, t * P:(t + 1) * P] if narrow else probs[:, t * S + kt * P:t * S + (kt + 1) * P]
                        ins = pe.transpose(p_bank[s % 2][:, kt * S + t * P:kt * S + (t + 1) * P], src, ident)
                ins.then_inc(p_turned, 1)

            def p_times_v(s):
                layer, group, h, narrow = HEADS[s]
                vv = qkv_of(layer, group)[2]
                vc = HD * (h // 4 if layer == 0 else h)
                pe.wait_ge(pT_copied, s + 1)
                if s:
                    pe.wait_ge(o_copied, s)
                for t in range(NT):
                    o = o_bank[:, t * HD:(t + 1) * HD]
                    if narrow:
                        ins = pe.matmul(o, pT[s % 2][:, t * P:(t + 1) * P], vv[:, t, vc:vc + HD], start=True, stop=True)
                    else:
                        for kt in range(NT):
                            ins = pe.matmul(o, pT[s % 2][:, kt * S + t * P:kt * S + (t + 1) * P], vv[:, kt, vc:vc + HD],
                                            start=kt == 0, stop=kt == NT - 1)
                ins.then_inc(pv_done, 1)

            def heads(steps, between, side):
                for s in steps:
                    score(s)
                    if s >= steps[0] + 2:
                        turn_p(s - 2)
                    if s >= steps[0] + 3:
                        p_times_v(s - 3)
                    if s - steps[0] in between:
                        unit(between[s - steps[0]])
                    if s - steps[0] in side:
                        side[s - steps[0]]()
                turn_p(steps[-2])
                p_times_v(steps[-3])
                turn_p(steps[-1])
                p_times_v(steps[-2])
                p_times_v(steps[-1])

            def turn_o_chunk(layer, ch, t):
                o = oA if layer == 0 else oB[:, 0]
                at = (ch % 2) * S + t * P
                return pe.transpose(ps[:, oT_bank(layer, ch // 2), at:at + P], o[:, t, P * ch:P * ch + P], ident)

            def turn_o(b):
                pe.wait_ge(o_copied, 4 * b + 4)
                for ch in (2 * b, 2 * b + 1):
                    for t in range(NT):
                        ins = turn_o_chunk(0, ch, t)
                ins.then_inc(o_turned, 1)

            def mix_out(layer):
                n_ch = (8, 4)[layer]
                mod(layer, 2, 0)
                if layer == 0:
                    turn_o(3)
                else:
                    for t in range(NT):
                        pe.wait_ge(o_ready, t + 1)
                        for ch in range(n_ch):
                            ins = turn_o_chunk(1, ch, t)
                            if t == NT - 1 and ch % 2:
                                ins.then_inc(o_turned, 1)
                pe.wait_ge(oT_dve, (1, 2)[layer])
                pe.wait_ge(oT_act, (3, 4)[layer])
                for n in range(4):
                    t, h = n // 2, n % 2
                    if n == 3:
                        turn_x(layer, 0)
                        pe.wait_ge(mod_read, PIECES[layer, 2] + 1)
                    for ch in range(n_ch):
                        name = ("wo", layer, ch // 4)
                        if n == 0 and ch % 4 == 0:
                            arrived(pe, name)
                        ins = pe.matmul(ps[:, 4 + n, :], oT[:, ch, t * P:(t + 1) * P],
                                        as_chunks(slot_of(name), D)[:, ch % 4, 512 * h:512 * h + 512],
                                        start=ch == 0, stop=ch == n_ch - 1)
                    ins.then_inc(mixed, 1)

            def route(layer):
                pe.wait_ge(shift_summed, layer + 1)
                pe.matmul(ps[:, 4, NT * E:NT * E + E], ones, shift_sum, start=True, stop=True)
                pe.wait_ge(xT_act, 2 * layer + 2)
                router_products(0)
                turn_x(layer, 1)
                pe.wait_ge(xT_dve, 2 * layer + 2)
                router_products(1).then_inc(logits, 1)
                mod(layer, 2, 1)
                mod(layer, 2, 2)
                if layer == 0:
                    mod(1, 0, 0)
                pe.wait_ge(routed, layer + 1)
                r = ps[:, 5, :]
                pe.matmul(r[:, 0:E], tri, sel[:, 0, :], start=True, stop=True)
                pe.matmul(r[:, E:2 * E], ones, sel[:, 0, :], start=True, stop=False)
                pe.matmul(r[:, E:2 * E], tri, sel[:, 1, :], start=False, stop=True)
                pe.matmul(r[:, 2 * E:3 * E], ones, sel[:, 0, :], start=True, stop=False)
                pe.matmul(r[:, 2 * E:3 * E], ones, sel[:, 1, :], start=False, stop=True).then_inc(ranked, 1)

            def gather(n):
                for k in range(KD):
                    at = k * n
                    for t in range(NT):
                        ins = pe.matmul(ps[:, at // 512, at % 512:at % 512 + n], xn[:, t, k, :], pick[:, t, 0:n],
                                        start=t == 0, stop=t == NT - 1)
                    if n == P and k % 4 == 3:
                        ins.then_inc(gathered, 1)

            def two(bank_a, bank_b, stationary, moving, chunks):
                for k in range(chunks):
                    for b, bank in enumerate((bank_a, bank_b)):
                        ins = pe.matmul(ps[C * b:C * b + C, bank, :], stationary(b, k), moving(b, k), start=k == 0,
                                        stop=k == chunks - 1)
                return ins

            def experts(layer):
                base = LOAD[("moe", layer, 0)]
                q0, g0 = PAIRS * layer, GATHERS * layer
                pe.wait_ge(picked, g0 + 1)
                gather(P)
                blocks_here = extra_block_count(pe, layer)

                def scatter(q):
                    pe.wait_ge(pwT_ready, q + 1)
                    for n in range(4):
                        t, h = n % 2, n // 2
                        pe.wait_ge(y_copied, q * 2 + (h + 1))
                        pe.wait_ge(scatter_free, q * 4 + (n + 1))
                        pe.matmul(ps[:, 6 + n % 2, :], pwT[:, t * P:(t + 1) * P], ye[:, 512 * h:512 * h + 512],
                                  start=True, stop=True).then_inc(scattered, 1)

                def pair(i, first=False, second=False):
                    def weights(part):
                        views = []
                        for n in (base + 2 * part, base + 2 * part + 1):
                            late = 16 if part == 0 and not first else 0
                            pe.wait_ge(landed[n % RING], i * 16 + (landed_value(n) - late))
                            views.append(as_chunks(ring[n % RING], D if part == 2 else F))
                        return views

                    if second:
                        pe.wait_ge(gates_ahead, 32 * (layer + 1))
                        gate_w = [as_chunks(g, F) for g in gates_1]
                    else:
                        gate_w = weights(0)
                    pe.wait_ge(xg_ready, i + (g0 + 1))
                    two(2, 2, lambda b, k: xg[:, k, C * b:C * b + C], lambda b, k: gate_w[b][:, k, :], KD)\
                        .then_inc(gate_done, 1)
                    up_w = weights(1)
                    two(3, 3, lambda b, k: xg[:, k, C * b:C * b + C], lambda b, k: up_w[b][:, k, :], KD)\
                        .then_inc(up_done, 1)
                    pe.wait_ge(picked, i + (g0 + 2))
                    gather(P)
                    if not first:
                        scatter(i + (q0 - 1))
                    pe.wait_ge(a_ready, i + (q0 + 1))
                    for f in range(KF):
                        ins = pe.transpose(ps[:, 2, f * P:(f + 1) * P], sg[:, f * P:(f + 1) * P], ident)
                    ins.then_inc(a_turned, 1)
                    pe.wait_ge(pw_ready, i + (q0 + 1))
                    for t in range(NT):
                        ins = pe.transpose(ps[:, 3, t * P:(t + 1) * P], pw[:, t, :], ident)
                    ins.then_inc(pw_turned, 1)
                    down_w = weights(2)
                    pe.wait_ge(aT_ready, i + (q0 + 1))
                    for h in range(2):
                        two(4 + h, 4 + h, lambda b, f: aT[:, f, C * b:C * b + C],
                            lambda b, f: down_w[b][:, f, 512 * h:512 * h + 512], KF).then_inc(down_done, 1)

                pair(0, True)
                pair(1, second=True)
                with pe.If(blocks_here > 0):
                    begin_extra()
                with pe.Fori(2, PAIRS) as i:
                    pair(i)
                    extra_blocks(pe, blocks_here, i, begin_extra, lambda: end_extra(layer, i))
                with pe.If(blocks_here > PAIRS - 2):
                    end_extra(layer, PAIRS - 1)
                scatter(q0 + PAIRS - 1)

            blocks = pe.alloc_register("pe_blocks")
            landings = pe.alloc_register("pe_landings")
            down_landings = pe.alloc_register("pe_down_landings")
            pe.reg_mov(blocks, 1)
            pe.reg_mov(landings, 32)
            pe.reg_mov(down_landings, 0)

            def begin_extra():
                gate_w, up_w = as_chunks(x_gate, F), as_chunks(x_up, F)
                pe.wait_ge(e_picked, blocks)
                gather(C)
                for t in range(NT):
                    ins = pe.transpose(ps[:, 3, t * P:(t + 1) * P], pw[:, t, :], ident)
                ins.then_inc(e_gathered, 1)
                pe.wait_ge(e_landed, landings)
                pe.wait_ge(e_xg, blocks)
                two(0, 1, lambda b, k: x_xg[:, k, :], lambda b, k: (gate_w, up_w)[b][:, k, :], KD).then_inc(e_up, 1)
                pe.reg_add(landings, landings, 32)

            def end_extra(layer, i):
                down_w = as_chunks(x_down, D)
                pe.wait_ge(y_copied, i * 2 + (2 * PAIRS * layer + 2))
                pe.wait_ge(scatter_free, i * 4 + (4 * PAIRS * layer + 2))
                pe.wait_ge(xg_ready, i + (GATHERS * layer + 2))
                pe.wait_ge(e_a, blocks)
                pe.reg_add(down_landings, down_landings, 16)
                for f in range(KF):
                    ins = pe.transpose(ps[:, 2, f * C:(f + 1) * C], x_sg[:, f * P:(f + 1) * P], ident[0:C, 0:C])
                ins.then_inc(e_turned, 1)
                pe.wait_ge(e_aT, blocks)
                pe.wait_ge(e_landed_down, down_landings)
                two(4, 5, lambda b, f: x_aT[:, f, :], lambda b, f: down_w[:, f, 512 * b:512 * b + 512], KF)\
                    .then_inc(e_down, 1)
                pe.wait_ge(e_y, blocks)
                for n in range(4):
                    t, h = n // 2, n % 2
                    rows = slice(C * h, C * h + C)
                    ins = pe.matmul(ps[:, (6, 7, 0, 1)[n], :], x_pwT[rows, t * P:(t + 1) * P], x_ye[rows, :],
                                    start=True, stop=True)
                ins.then_inc(e_scattered, 1)
                pe.reg_add(blocks, blocks, 1)
                pe.wait_ge(e_added, blocks)

            pe.wait_ge(s_const, 80)
            turn_xn(0)
            mod(0, 0, 0)
            pe.wait_ge(hT_dve, 4)
            pe.wait_ge(hT_act, 4)
            for u in RUNS[0, 0][0][:4]:
                unit(u)
            heads(RUNS[0, 0][1], BETWEEN_0, {2: lambda: turn(4), 4: lambda: turn(5), 5: lambda: mod(0, 1, 0),
                                             6: lambda: mod(0, 1, 1), 7: lambda: mod(0, 1, 2), 9: lambda: turn_o(0),
                                             13: lambda: turn_o(1)})
            pe.wait_ge(oT_act, 1)
            turn_o(2)
            mix_out(0)
            route(0)
            experts(0)
            turn_xn(1)
            pe.wait_ge(hT_dve, 8)
            pe.wait_ge(hT_act, 8)
            for u in RUNS[1, 0][0]:
                unit(u)
            def first_sums():
                pe.wait_ge(qk_copied, ropes_before(RUNS[1, 1][0][-1] + 1))
                mod(1, 1, 0)
            heads(RUNS[1, 0][1], units_between(0), {6: first_sums, 7: lambda: mod(1, 1, 1)})
            mod(1, 1, 2)
            heads(RUNS[1, 1][1], units_between(1), {})
            heads(RUNS[1, 2][1], {}, {})
            mix_out(1)
            route(1)
            experts(1)


INPUTS = ["x", "c", "positions", "ada_w", "ada_b", "norm_mix_g", "norm_ffn_g", "a_w_qkv", "a_w_o", "a_sink",
          "b_w_qkv", "b_w_o", "router_w", "router_bias", "exp_w_gate", "exp_w_up", "exp_w_down", "final_norm_g"]


def kernel(**inputs):
    import concourse.bacc as bacc
    from concourse.bass_utils import run_bass_kernel_spmd

    nc = bacc.Bacc("TRN2", target_bir_lowering=False, num_devices=1)
    arrays = {name: np.ascontiguousarray(inputs[name]) for name in INPUTS}
    arrays["const"] = constants()
    arrays["mask"] = masks()
    args = [nc.dram_tensor(name, a.shape, mybir.dt.from_np(a.dtype), kind="ExternalInput").ap()
            for name, a in arrays.items()]
    args.append(nc.dram_tensor("out", (1, S, D), F32, kind="ExternalOutput").ap())
    build(nc, *args)
    result = run_bass_kernel_spmd(nc, [arrays], core_ids=[0])
    return result.results[0]["out"]
```
